# Optimizing a Trainium2 kernel written in Bass

```python
import math
import jax, jax.numpy as jnp
from jax import lax
import numpy as np

D_MODEL = 2048
BATCH = 1
SEQ = 512
DEPTH = 1
DEC_BATCH = 1
DEC_SEQ = 32
PAST_LEN = 1024

CHUNK = 64
Q_BLOCK = 128
D_MIX = D_MODEL
ATT_WIDTH = D_MIX // 2
ML_WIDTH = D_MIX - ATT_WIDTH
ATT_HEADS = 8
ATT_DV = ATT_WIDTH // ATT_HEADS
ATT_DQK = ATT_DV // 2
ML_HEADS = 8
ML_DK = ML_WIDTH // ML_HEADS
ML_DV = ML_WIDTH // ML_HEADS
CONV_W = 4
D_FF = 4 * D_MODEL
EPS = 1e-6
N_IN = 3 * ATT_WIDTH + 4 * ML_WIDTH + 2 * ML_HEADS

kernel_name = 'hymba_diffattn_mlstm_stream_step'

def rms_norm(x, w):
    xf = x.astype(jnp.float32)
    y = xf * lax.rsqrt(jnp.mean(xf * xf, axis=-1, keepdims=True) + EPS)
    return (y * w.astype(jnp.float32)).astype(x.dtype)

def split_in(h):
    sizes = (ATT_WIDTH,) * 3 + (ML_WIDTH,) * 4 + (ML_HEADS,) * 2
    cuts = [int(c) for c in np.cumsum(sizes)[:-1]]
    return jnp.split(h, cuts, axis=-1)

def causal_conv(u, buf, w, b):
    L = u.shape[1]
    full = jnp.concatenate([buf.astype(u.dtype), u], axis=1)
    acc = b
    for j in range(CONV_W):
        acc = acc + full[:, j:j + L] * w[j]
    return jax.nn.silu(acc), full[:, L:]

def diff_attn_block(q, k, v, lam, mask):
    s = jnp.einsum('bqhcd,bkhcd->bhcqk', q.astype(jnp.float32), k.astype(jnp.float32)) * (ATT_DQK ** -0.5)
    if mask is not None:
        s = jnp.where(mask, s, -jnp.inf)
    p = jax.nn.softmax(s, axis=-1)
    a = p[:, :, 0] - lam * p[:, :, 1]
    return jnp.einsum('bhqk,bkhd->bqhd', a, v.astype(jnp.float32)).astype(v.dtype)

def diff_attn_prompt(q, k, v, lam):
    B, L = q.shape[0], q.shape[1]
    nb = L // Q_BLOCK
    qb = jnp.moveaxis(q.reshape(B, nb, Q_BLOCK, ATT_HEADS, 2, ATT_DQK), 1, 0)
    key_chunk = jnp.arange(L) // CHUNK

    def body(args):
        i, qi = args
        q_chunk = (i * Q_BLOCK + jnp.arange(Q_BLOCK)) // CHUNK
        mask = key_chunk[None, :] <= q_chunk[:, None]
        return diff_attn_block(qi, k, v, lam, mask)

    out = lax.map(body, (jnp.arange(nb), qb))
    return jnp.moveaxis(out, 0, 1).reshape(B, L, ATT_HEADS, ATT_DV)

def mlstm_chunk(carry, inp):
    C, n, m = carry
    q, k, v, ig, lf = inp
    L = q.shape[2]
    b = jnp.cumsum(lf, axis=-1)
    causal = jnp.tril(jnp.ones((L, L), dtype=bool))
    log_d = jnp.where(causal, b[..., :, None] - b[..., None, :] + ig[..., None, :], -jnp.inf)
    log_inter = b + m[..., None]
    m_t = jnp.maximum(log_inter, jnp.max(log_d, axis=-1))
    d = jnp.exp(log_d - m_t[..., None])
    w_inter = jnp.exp(log_inter - m_t)
    qk = jnp.einsum('bhtd,bhsd->bhts', q, k) * d
    num = w_inter[..., None] * jnp.einsum('bhtd,bhde->bhte', q, C) + jnp.einsum('bhts,bhse->bhte', qk, v)
    den = w_inter * jnp.einsum('bhtd,bhd->bht', q, n) + jnp.sum(qk, axis=-1)
    h = num / jnp.maximum(jnp.abs(den), jnp.exp(-m_t))[..., None]
    m_new = m_t[..., -1]
    w_c = jnp.exp(b[..., -1] + m - m_new)
    w_s = jnp.exp(b[..., -1:] - b + ig - m_new[..., None])
    C_new = w_c[..., None, None] * C + jnp.einsum('bhs,bhsd,bhse->bhde', w_s, k, v)
    n_new = w_c[..., None] * n + jnp.einsum('bhs,bhsd->bhd', w_s, k)
    return (C_new, n_new, m_new), h

def mlstm_prompt(carry, q, k, v, ig, lf):
    B, H, L, _ = q.shape
    nc = L // CHUNK
    blk = lambda t: jnp.moveaxis(t.reshape(B, H, nc, CHUNK, *t.shape[3:]), 2, 0)
    carry, h = lax.scan(mlstm_chunk, carry, (blk(q), blk(k), blk(v), blk(ig), blk(lf)))
    return carry, jnp.moveaxis(h, 0, 2).reshape(B, H, L, ML_DV)

def heads(u):
    B, L, _ = u.shape
    return u.reshape(B, L, ML_HEADS, -1).transpose(0, 2, 1, 3).astype(jnp.float32)

def layer(x, l, p, past):
    B, L, _ = x.shape
    xn = rms_norm(x, p['norm1_w'])
    aq, ak, av, mq, mk, mv, mo, mi, mf = split_in(xn @ p['w_in'])

    q = rms_norm(aq.reshape(B, L, ATT_HEADS, 2, ATT_DQK), p['q_norm_w'])
    k = rms_norm(ak.reshape(B, L, ATT_HEADS, 2, ATT_DQK), p['k_norm_w'])
    v = av.reshape(B, L, ATT_HEADS, ATT_DV)
    lam_init = 0.8 - 0.6 * math.exp(-0.3 * l)
    lqk = p['lambda_qk'].astype(jnp.float32)
    lam = jnp.exp(jnp.sum(lqk[0] * lqk[1])) - jnp.exp(jnp.sum(lqk[2] * lqk[3])) + lam_init

    if past is None:
        att = diff_attn_prompt(q, k, v, lam)
        conv_buf = jnp.zeros((B, CONV_W - 1, 2 * ML_WIDTH), x.dtype)
        C0 = jnp.zeros((B, ML_HEADS, ML_DK, ML_DV), jnp.float32)
        n0 = jnp.zeros((B, ML_HEADS, ML_DK), jnp.float32)
        m0 = jnp.zeros((B, ML_HEADS), jnp.float32)
    else:
        k_cache, v_cache, C0, n0, m0, conv_buf = past
        k_all = jnp.concatenate([k_cache.reshape(B, -1, ATT_HEADS, 2, ATT_DQK).astype(k.dtype), k], axis=1)
        v_all = jnp.concatenate([v_cache.astype(v.dtype), v], axis=1)
        att = diff_attn_block(q, k_all, v_all, lam, None)
        C0 = C0.astype(jnp.float32)
        n0 = n0.astype(jnp.float32)
        m0 = m0.astype(jnp.float32)
    att = (rms_norm(att, p['att_norm_w']) * (1.0 - lam_init)).reshape(B, L, ATT_WIDTH).astype(x.dtype)

    qk_c, conv_new = causal_conv(jnp.concatenate([mq, mk], axis=-1), conv_buf, p['conv_w'], p['conv_b'])
    qh = heads(qk_c[..., :ML_WIDTH])
    kh = heads(qk_c[..., ML_WIDTH:]) * (ML_DK ** -0.5)
    vh = heads(mv)
    gates = (jnp.concatenate([mi, mf], axis=-1) + p['b_gates']).astype(jnp.float32)
    ig = gates[..., :ML_HEADS].transpose(0, 2, 1)
    lf = jax.nn.log_sigmoid(gates[..., ML_HEADS:]).transpose(0, 2, 1)
    if past is None:
        (C1, n1, m1), h = mlstm_prompt((C0, n0, m0), qh, kh, vh, ig, lf)
    else:
        (C1, n1, m1), h = mlstm_chunk((C0, n0, m0), (qh, kh, vh, ig, lf))
    h = h.transpose(0, 2, 1, 3)
    o = jax.nn.sigmoid(mo.astype(jnp.float32)).reshape(B, L, ML_HEADS, ML_DV)
    ml = (rms_norm(h, p['ml_norm_w']) * o).reshape(B, L, ML_WIDTH).astype(x.dtype)

    x = x + jnp.concatenate([att, ml], axis=-1) @ p['w_out']
    hn = rms_norm(x, p['norm2_w'])
    x = x + jnp.square(jax.nn.relu(hn @ p['w_up'])) @ p['w_down']
    return x, (k.reshape(B, L, ATT_HEADS, 2 * ATT_DQK), v, C1, n1, m1, conv_new)

def setup_inputs(seed: int = 0) -> dict:
    key = jax.random.key(seed)
    ks = jax.random.split(key, 24)
    nrm = lambda kk, shape, s: s * jax.random.normal(kk, shape, jnp.float32)
    b_gates = jnp.concatenate([nrm(ks[12], (DEPTH, ML_HEADS), 0.1),
                               3.0 + nrm(ks[13], (DEPTH, ML_HEADS), 0.1)], axis=-1)
    return {
        'x_prompt': nrm(ks[0], (BATCH, SEQ, D_MODEL), 1.0),
        'x_sample': nrm(ks[1], (DEC_BATCH, DEC_SEQ, D_MODEL), 1.0),
        'cache_k': nrm(ks[2], (DEPTH, DEC_BATCH, PAST_LEN, ATT_HEADS, 2 * ATT_DQK), 1.0),
        'cache_v': nrm(ks[3], (DEPTH, DEC_BATCH, PAST_LEN, ATT_HEADS, ATT_DV), 1.0),
        'state_C': nrm(ks[4], (DEPTH, DEC_BATCH, ML_HEADS, ML_DK, ML_DV), 0.1),
        'state_n': nrm(ks[5], (DEPTH, DEC_BATCH, ML_HEADS, ML_DK), 0.1),
        'state_m': nrm(ks[6], (DEPTH, DEC_BATCH, ML_HEADS), 0.5),
        'state_conv': nrm(ks[7], (DEPTH, DEC_BATCH, CONV_W - 1, 2 * ML_WIDTH), 1.0),
        'norm1_w': 1.0 + nrm(ks[8], (DEPTH, D_MODEL), 0.02),
        'w_in': nrm(ks[9], (DEPTH, D_MODEL, N_IN), D_MODEL ** -0.5),
        'conv_w': nrm(ks[10], (DEPTH, CONV_W, 2 * ML_WIDTH), CONV_W ** -0.5),
        'conv_b': nrm(ks[11], (DEPTH, 2 * ML_WIDTH), 0.02),
        'b_gates': b_gates,
        'q_norm_w': 1.0 + nrm(ks[14], (DEPTH, ATT_DQK), 0.02),
        'k_norm_w': 1.0 + nrm(ks[15], (DEPTH, ATT_DQK), 0.02),
        'lambda_qk': nrm(ks[16], (DEPTH, 4, ATT_DQK), 0.1),
        'att_norm_w': 1.0 + nrm(ks[17], (DEPTH, ATT_DV), 0.02),
        'ml_norm_w': 1.0 + nrm(ks[18], (DEPTH, ML_DV), 0.02),
        'w_out': nrm(ks[19], (DEPTH, D_MIX, D_MODEL), D_MIX ** -0.5),
        'norm2_w': 1.0 + nrm(ks[20], (DEPTH, D_MODEL), 0.02),
        'w_up': nrm(ks[21], (DEPTH, D_MODEL, D_FF), D_MODEL ** -0.5),
        'w_down': nrm(ks[22], (DEPTH, D_FF, D_MODEL), D_FF ** -0.5),
    }

def reference(x_prompt, x_sample, cache_k, cache_v, state_C, state_n, state_m, state_conv,
              norm1_w, w_in, conv_w, conv_b, b_gates, q_norm_w, k_norm_w, lambda_qk,
              att_norm_w, ml_norm_w, w_out, norm2_w, w_up, w_down):
    yp, ys = x_prompt, x_sample
    sp, ss = [], []
    for l in range(DEPTH):
        p = {'norm1_w': norm1_w[l], 'w_in': w_in[l], 'conv_w': conv_w[l], 'conv_b': conv_b[l],
             'b_gates': b_gates[l], 'q_norm_w': q_norm_w[l], 'k_norm_w': k_norm_w[l],
             'lambda_qk': lambda_qk[l], 'att_norm_w': att_norm_w[l], 'ml_norm_w': ml_norm_w[l],
             'w_out': w_out[l], 'norm2_w': norm2_w[l], 'w_up': w_up[l], 'w_down': w_down[l]}
        yp, st_p = layer(yp, l, p, None)
        ys, st_s = layer(ys, l, p, (cache_k[l], cache_v[l], state_C[l], state_n[l],
                                    state_m[l], state_conv[l]))
        sp.append(st_p)
        ss.append(st_s)
    k_prompt, v_prompt, C_prompt, n_prompt, m_prompt, conv_prompt = [jnp.stack([s[i] for s in sp]) for i in range(6)]
    k_sample, v_sample, C_sample, n_sample, m_sample, conv_sample = [jnp.stack([s[i] for s in ss]) for i in range(6)]
    return (yp, ys, k_prompt, v_prompt, C_prompt, n_prompt, m_prompt, conv_prompt,
            k_sample, v_sample, C_sample, n_sample, m_sample, conv_sample)


_drawn_inputs = setup_inputs


def setup_inputs(seed=0):
    import zlib

    import numpy as np

    out = dict(_drawn_inputs(seed))
    spreads = {}
    factors = {'q_norm_w': 5.559,
     'k_norm_w': 3.015,
     'att_norm_w': 5.625,
     'ml_norm_w': 8.0,
     'norm2_w': 3.427}
    for name, (base, spread) in spreads.items():
        noise = np.random.default_rng([zlib.crc32(name.encode()), seed]).standard_normal(out[name].shape)
        drawn = base * np.exp(spread * noise) if base else spread * noise
        out[name] = __import__('jax').numpy.asarray(drawn.astype(out[name].dtype))
    for name, factor in factors.items():
        out[name] = (out[name] * factor).astype(out[name].dtype)
    return out
```

```python
from contextlib import ExitStack

import concourse.bass as bass
from concourse import mybir

D_MODEL, SEQ, DEC, PAST = 2048, 512, 32, 1024
HEADS, DK, DQK = 8, 128, 64
D_FF = 4 * D_MODEL
CONV_W = 4
EPS = 1e-6
LAM_INIT = 0.2
P = 128
T = SEQ + DEC
HB = T // 2
KT = D_MODEL // P
NCH = SEQ // P
PER_HEAD = 7
K_, Q_, V_, MK, MQ, MV, MO = range(7)
ROUNDS = HEADS * PER_HEAD
BLOCK = 4
NBLK = D_FF // P // BLOCK
U_GATES = 0
U_HEAD = 1
U_OUT = U_HEAD + ROUNDS
U_UP0 = U_OUT + KT
U_FFN = U_UP0 + BLOCK
U_LAST = U_FFN + 2 * BLOCK * (NBLK - 1)
UNITS = U_LAST + BLOCK
QW = 4 * P
QUARTERS = 4 * UNITS
PAD = CONV_W - 1
UW = T + 2 * PAD
CW = UW - PAD
CS = SEQ + PAD
SPLIT = [t for h in range(HEADS) for t in (h, HEADS + h)]
OFF = [0, 128, 384, 768]
AW = 1280
ATO = {0: 0, 1: 512, 3: 896, 2: 1024}
BIG = 1e30
GR = 40

S_N1 = 0
S_N2 = S_N1 + KT
S_CW = S_N2 + KT
S_CB = S_CW + 2 * HEADS * CONV_W
S_QN = S_CB + 2 * HEADS
S_KN = S_QN + 1
S_AN = S_KN + 1
S_MN = S_AN + 1
S_BG = S_MN + 1
S_M0 = S_BG + 1
S_SC = S_M0 + 1
S_LQ = S_SC + 2 * HEADS * PAD
S_ALL = S_LQ + 4 * DQK

ACT_LINKS = 4
N_CONSTS = 24
UP_SLOT = U_UP0 % 2
DVE_LINKS = 24


class Step:

    def __init__(self, first, per=0, reg=None):
        self.first, self.per, self.reg = first, per, reg

    def __add__(self, n):
        return Step(self.first + n, self.per, self.reg)

    def __mul__(self, n):
        return Step(self.first * n, self.per * n, self.reg)

    def mod(self, n):
        assert self.per % n == 0
        return self.first % n

    @property
    def v(self):
        return self.first if self.reg is None else self.reg * self.per + self.first


def build(nc, xT, wstream, smalls, kcT, vc, c0, yT, k_out, v_out, st_out, m_out, conv_out):
    f32, f32r, bf16 = mybir.dt.float32, mybir.dt.float32r, mybir.dt.bfloat16
    ALU, ACT, AX = mybir.AluOpType, mybir.ActivationFunctionType, mybir.AxisListType
    ctx = ExitStack()
    with ctx:
        def sb(name, shape, dt=f32):
            return ctx.enter_context(nc.sbuf_tensor(name, shape, dt))

        def sem(name):
            return ctx.enter_context(nc.semaphore(name))

        res = sb("res", [P, KT, T])
        act_hi = sb("act_hi", [P, KT, T], f32r)
        act_lo = sb("act_lo", [P, KT, T], f32r)
        w_raw = sb("w_raw", [P, 4, QW])
        w_hi = sb("w_hi", [P, 4, QW], f32r)
        w_lo = sb("w_lo", [P, 4, QW], f32r)
        sm = sb("sm", [P, S_ALL])
        ident = sb("ident", [P, P])
        ones = sb("ones", [P, P])
        rstd = sb("rstd", [P, T])
        tmp = [sb(f"tmp{i}", [P, T]) for i in range(4)]
        acc = tmp[3]

        eps_col = sb("eps_col", [P, 1])
        psum = ctx.enter_context(nc.psum_tensor("psum", [P, 8, 512], f32))

        def group(slot):
            return psum[:, 2 * slot:2 * slot + 2, 0:HB]

        pp = psum[:, 4:8, :]

        rows_dram = nc.dram_tensor("gate_rows", [3, HEADS, T], f32, kind="Internal").ap()

        raw_loaded = [sem(f"raw_loaded{i}") for i in range(4)]
        hi_ready, lo_ready = sem("hi_ready"), sem("lo_ready")
        quarter_done = sem("quarter_done")
        out_taken = sem("out_taken")
        smalls_loaded, consts_ready = sem("smalls_loaded"), sem("consts_ready")
        x_loaded = [sem(f"x_loaded{i}") for i in range(8)]
        x_hi, x_sq, x_lo, x_acc = sem("x_hi"), sem("x_sq"), sem("x_lo"), sem("x_acc")
        norm_done, rstd_ready, acc_clear = sem("norm_done"), sem("rstd_ready"), sem("acc_clear")
        stored = sem("stored")

        def flat(ap):
            return ap.rearrange("p a b -> p (a b)")

        def two(ap):
            return ap.rearrange("p (a b) -> p a b", a=2)

        phase_a = ExitStack()
        with phase_a:
            def sa(name, shape, dt=f32):
                return phase_a.enter_context(nc.sbuf_tensor(name, shape, dt))

            k_raw, q_raw, v_T = sa("k_raw", [P, T]), sa("q_raw", [P, T]), sa("v_T", [P, T])
            mk_u, mq_u = sa("mk_u", [P, UW]), sa("mq_u", [P, UW])
            mv_T, mo_T = sa("mv_T", [P, T]), sa("mo_T", [P, T])
            k_T = sa("k_T", [P, T])
            q_pad = sa("q_pad", [P, 2, SEQ])
            q_s = sa("q_s", [P, 2 * DEC])
            mk_T, mq_T = sa("mk_T", [P, CW]), sa("mq_T", [P, CW])
            v_tok, kw_tok = sa("v_tok", [P, NCH + 1, DK]), sa("kw_tok", [P, NCH + 1, DK])
            v_aug = sa("v_aug", [P, NCH + 1, DK + 1])
            big = sa("big", [P, 3, AW])
            prob = [big[:, 0, :], big[:, 1, :]]
            at = big[:, 2, :]
            s_prob = big[0:64, 1, 0:PAST + DEC]
            s_pt = big[:, 2, 0:9 * 64]
            decay = sa("decay", [P, T])
            wi_row, en_row = sa("wi_row", [P, T]), sa("en_row", [P, T])
            state = sa("state", [P, NCH + 1, DK + 1])
            c0_sb = sa("c0_sb", [P, DK + 1])
            n_b = big[:, 0, 0:SEQ].rearrange("p (c d) -> p c d", c=NCH)
            kc_sb, vc_sb = sa("kc_sb", [P, PAST]), sa("vc_sb", [P, PAST // P, DK])
            att_T = mk_T[:, 0:T]
            s_out = big[0:64, 1, PAST + DEC:PAST + DEC + DK]
            neg_max, sums, inv = sa("neg_max", [P, 2, NCH]), sa("sums", [P, 2, NCH]), sa("inv", [P, 2, NCH])
            s_max, s_sum, s_inv = sa("s_max", [64, 1]), sa("s_sum", [64, 1]), sa("s_inv", [64, 1])
            blk = sa("blk", [P, P])
            comb = sa("comb", [64, DEC])
            causal = sa("causal", [P, P])
            late_row, early_q = sa("late_row", [1, P], bf16), sa("early_q", [1, P], bf16)
            g_col, ws_col = sa("g_col", [P, NCH + 1, HEADS]), sa("ws_col", [P, NCH + 1, HEADS])
            conv_sb = sa("conv_sb", [P, 2 * HEADS, 2, PAD])
            qn8, an8, lam4, neg_lam, lam_sel = (sa("qn8", [P, 1]), sa("an8", [P, 1]), sa("lam4", [P, 4]),
                                                sa("neg_lam", [P, 1]), sa("lam_sel", [64, 1]))
            lam_p = kw_tok[:, 0, :].rearrange("p (a d) -> p a d", a=2)
            m_end, nm_end = sa("m_end", [HEADS, 2]), sa("nm_end", [HEADS, NCH + 1])
            gates = [flat(big[:, :, :])[0:GR, i * T:(i + 1) * T] for i in range(7)]
            zero_row = tmp[2][0:HEADS, :]

            gate_taken, gates_raw, gates_lf, gates_scan = sem("gate_taken"), sem("gates_raw"), sem("gates_lf"), sem("gates_scan")
            gates_exp, cols_done, cols_ready = sem("gates_exp"), sem("cols_done"), sem("cols_ready")
            rows_stored, rows_loaded, cache_loaded, c0_loaded = (sem("rows_stored"), sem("rows_loaded"),
                                                                 sem("cache_loaded"), sem("c0_loaded"))
            lam_sum, lam_exp = sem("lam_sum"), sem("lam_exp")
            kv_stored, st_stored = sem("kv_stored"), sem("st_stored")
            sq_ready, conv_ready, conv_exp = sem("sq_ready"), sem("conv_ready"), sem("conv_exp")
            qk_ms_done, qk_rstd, qk_ready, silu_ready = sem("qk_ms_done"), sem("qk_rstd"), sem("qk_ready"), sem("silu_ready")
            tok_done, tok_act, tok_dve, decay_sum, decay_ready = (sem("tok_done"), sem("tok_act"), sem("tok_dve"),
                                                                  sem("decay_sum"), sem("decay_ready"))
            scores_done, max_ready, probs_ready, weights_ready = (sem("scores_done"), sem("max_ready"),
                                                                  sem("probs_ready"), sem("weights_ready"))
            at_done, at_ready, pt_ready, pv_done = sem("at_done"), sem("at_ready"), sem("pt_ready"), sem("pv_done")
            att_ready, state_ready, s_scores_done, s_max_ready = (sem("att_ready"), sem("state_ready"),
                                                                  sem("s_scores_done"), sem("s_max_ready"))
            den_abs = sem("den_abs")
            s_exp_ready, s_probs_ready, h_done, h_ready, h_sq = (sem("s_exp_ready"), sem("s_probs_ready"), sem("h_done"),
                                                                 sem("h_ready"), sem("h_sq"))
            s_pt_done, s_pt_ready, s_pv_done, s_out_ready, ml_rstd, o_exp = (
                sem("s_pt_done"), sem("s_pt_ready"), sem("s_pv_done"), sem("s_out_ready"), sem("ml_rstd"), sem("o_exp"))
            comb_done, s_att_ready, att_sq, att_ms_done, att_rstd = (sem("comb_done"), sem("s_att_ready"), sem("att_sq"),
                                                                     sem("att_ms_done"), sem("att_rstd"))
            mix_ready, mix_hi, mix_lo, x_reloaded = sem("mix_ready"), sem("mix_hi"), sem("mix_lo"), sem("x_reloaded")
            dve_self, act_self, post_self, post_dve = sem("dve_self"), sem("act_self"), sem("post_self"), sem("post_dve")
            up_relu, up_hi, up_sq, up_lo, down_taken = sem("up_relu"), sem("up_hi"), sem("up_sq"), sem("up_lo"), sem("down_taken")


            def head_steps(eng, prologue, both, last, between=None):
                prologue(Step(0))
                both(Step(1), Step(0))
                with eng.Fori(0, HEADS // 2 - 1) as i:
                    both(Step(2, 2, i), Step(1, 2, i))
                    both(Step(3, 2, i), Step(2, 2, i))
                last(Step(HEADS - 1))

            def ffn_steps(eng, step):
                with eng.Fori(0, NBLK // 2 - 1) as i:
                    step(Step(0, 2, i))
                    step(Step(1, 2, i))
                step(Step(NBLK - 2))


            phase_a.close()
            hid_hi = sb("hid_hi", [P, 2, BLOCK, T], f32r)
            hid_lo = sb("hid_lo", [P, 2, BLOCK, T], f32r)
            block = ctx.enter_context(nc.Block())

            @block.sync
            def _(sp):
                for q in range(4):
                    sp.dma_start(w_raw[:, q, :], wstream[q]).then_inc(raw_loaded[q], 16)
                with sp.Fori(0, QUARTERS // 4 - 1) as i:
                    for q in range(4):
                        sp.wait_ge(lo_ready, i * 4 + (q + 1))
                        sp.dma_start(w_raw[:, q, :],
                                     wstream[bass.ds(i * 4 + (q + 4), 1)].rearrange("a p n -> p (a n)")
                                     ).then_inc(raw_loaded[q], 16)

            @block.gpsimd
            def _(pool):
                pool.dma_start(sm[:], smalls).then_inc(smalls_loaded, 16)
                n = [0]

                def const(ins):
                    n[0] += 1
                    ins.then_inc(consts_ready, 1)
                    pool.wait_ge(consts_ready, n[0])

                const(nc.gpsimd.memset(ones[:], 1.0))
                const(nc.gpsimd.memset(ident[:], 0.0))
                const(nc.gpsimd.memset(blk[:], 1.0))
                const(nc.gpsimd.memset(comb[:], 0.0))
                const(nc.gpsimd.memset(causal[:], 0.0))
                const(nc.gpsimd.memset(early_q[:], 0.0))
                const(nc.gpsimd.memset(late_row[:], 0.0))
                const(nc.gpsimd.memset(q_pad[:], 0.0))
                const(nc.gpsimd.memset(q_s[:], 0.0))
                const(nc.gpsimd.memset(mk_u[:, 0:PAD], 0.0))
                const(nc.gpsimd.memset(mq_u[:, 0:PAD], 0.0))
                const(nc.gpsimd.memset(v_aug[:, :, DK:DK + 1], 1.0))
                const(nc.gpsimd.memset(acc[:], 0.0))
                const(nc.gpsimd.memset(zero_row, 0.0))
                const(nc.gpsimd.memset(lam_sel[0:32, :], 1.0))
                const(nc.gpsimd.memset(eps_col[:], EPS))
                const(nc.gpsimd.affine_select(out=ident[:], in_=ident[:], compare_op=ALU.not_equal, fill=1.0,
                                              base=0, pattern=[[-1, P]], channel_multiplier=1))
                const(nc.gpsimd.memset(blk[0:64, 64:128], 0.0))
                const(nc.gpsimd.memset(blk[64:128, 0:64], 0.0))
                const(nc.gpsimd.affine_select(out=causal[:], in_=causal[:], compare_op=ALU.is_ge, fill=BIG,
                                              base=0, pattern=[[1, P]], channel_multiplier=-1))
                const(nc.gpsimd.affine_select(out=comb[:], in_=comb[:], compare_op=ALU.not_equal, fill=1.0,
                                              base=0, pattern=[[-1, DEC]], channel_multiplier=1))
                const(nc.gpsimd.memset(early_q[:, 0:64], 1.0))
                const(nc.gpsimd.memset(late_row[:, 64:128], -BIG))
                const(nc.gpsimd.affine_select(out=comb[:], in_=comb[:], compare_op=ALU.not_equal, fill=1.0,
                                              base=-DEC, pattern=[[-1, DEC]], channel_multiplier=1))
                assert n[0] == N_CONSTS, n

                def dma_after_waits(dst, src, done):
                    pool.wait_ge(smalls_loaded, 16)
                    pool.dma_start(dst, src).then_inc(done, 16)

                def load_head(p, first):
                    if not first:
                        pool.wait_ge(s_scores_done, p.v)
                    dma_after_waits(kc_sb[:], kcT[bass.ds(p.v, 1)].rearrange("a p n -> p (a n)"), cache_loaded)
                    if not first:
                        pool.wait_ge(smalls_loaded, 16)
                        pool.wait_ge(s_pv_done, p.v)
                        pool.wait_ge(h_done, p.v)
                        pool.wait_ge(h_ready, p.v)
                    pool.dma_start(vc_sb[:], vc[bass.ds(p.v, 1)].rearrange("a p t n -> p (a t) n")).then_inc(cache_loaded, 16)
                    pool.dma_start(c0_sb[:], c0[bass.ds(p.v, 1)].rearrange("a p n -> p (a n)")).then_inc(c0_loaded, 16)
                    for r, row in enumerate((decay, wi_row, en_row)):
                        pool.dma_start(row[:], rows_dram[r, bass.ds(p.v, 1), :].to_broadcast([P, T])).then_inc(rows_loaded, 16)

                def store_head(p):
                    pool.wait_ge(qk_ready, (p + 1).v)
                    dma_after_waits(k_out[bass.ds(p.v, 1)].rearrange("a p n -> p (a n)"), k_T[:], kv_stored)
                    pool.dma_start(v_out[bass.ds(p.v, 1)].rearrange("a p n -> p (a n)"), v_T[:]).then_inc(kv_stored, 16)
                    pool.wait_ge(state_ready, (p + 1).v)
                    dma_after_waits(st_out[bass.ds(p.v, 1)].rearrange("a s p n -> p (a s) n"),
                                    state[:, NCH - 1:NCH + 1, :], st_stored)

                def prologue(h):
                    pool.wait_ge(gates_exp, 1)
                    pool.dma_start(rows_dram[0], gates[4][0:HEADS, :]).then_inc(rows_stored, 16)
                    pool.dma_start(rows_dram[1], gates[6][0:HEADS, :]).then_inc(rows_stored, 16)
                    pool.dma_start(rows_dram[2], tmp[0][0:HEADS, :]).then_inc(rows_stored, 16)
                    pool.dma_start(m_out, m_end[:]).then_inc(stored, 16)
                    pool.wait_ge(rows_stored, 48)
                    load_head(Step(0), True)

                def both(h, p):
                    store_head(p)
                    load_head(h, False)

                head_steps(pool, prologue, both, store_head)
                for n_, t in enumerate(SPLIT):
                    pool.wait_ge(mix_lo, n_ + 1)
                    pool.dma_start(res[:, t, :], xT[:, t, :]).then_inc(x_reloaded, 16)
                pool.dma_start(conv_out, conv_sb[:]).then_inc(stored, 16)

                def square(t, slot):
                    pool.wait_ge(up_relu, (t + 1).v)
                    if not (t.reg is None and t.first < 2):
                        pool.wait_ge(up_lo, (t + (-1)).v)
                    nc.gpsimd.tensor_tensor(tmp[2 + slot][:], tmp[slot][:], tmp[slot][:], ALU.mult).then_inc(up_sq, 1)

                for t in range(BLOCK):
                    square(Step(t), t % 2)

                def step(b):
                    for t in range(BLOCK):
                        square((b + 1) * BLOCK + t, t % 2)

                ffn_steps(pool, step)
                pool.wait_ge(kv_stored, 16 * 2 * HEADS)
                pool.wait_ge(st_stored, 16 * HEADS)
                for m in range(KT):
                    pool.wait_ge(down_taken, (NBLK - 1) * KT + m + 1)
                    pool.dma_start(yT[:, m, :], res[:, m, :]).then_inc(stored, 16)
                pool.wait_ge(stored, 16 * (KT + 2))

            @block.tensor
            def _(pe):
                def passes(out, w_slot, col, m, x_hi_t, x_lo_t, start, stop):
                    for n_, (w, x) in enumerate(((w_hi, x_hi_t), (w_hi, x_lo_t), (w_lo, x_hi_t))):
                        for half in range(2):
                            last = nc.tensor.matmul(out[0:m, half, :], w[:, w_slot, col:col + m],
                                                    x[:, half * HB:(half + 1) * HB],
                                                    start=start and n_ == 0, stop=stop and n_ == 2)
                    return last

                def unit(u, m=P, x_ready=None, pieces=(None, None), taken=True, tiles=range(KT)):
                    out = group(u.mod(2))
                    if taken:
                        pe.wait_ge(out_taken, (u + (-1)).v)
                    for q in range(4):
                        pe.wait_ge(lo_ready, (u * 4 + (q + 1)).v)
                        for k in range(4):
                            kk = 4 * q + k
                            if x_ready is not None:
                                pe.wait_ge(x_ready[0], x_ready[1] + kk + 1)
                            t = tiles[kk]
                            last = passes(out, q, k * P, m, act_hi[:, t, :], act_lo[:, t, :], kk == 0, kk == KT - 1)
                        last.then_inc(quarter_done, 1)
                        if q == 1 and pieces[0]:
                            pieces[0]()
                        if q == 3 and pieces[1]:
                            pieces[1]()

                def sum_rows(w, src, bank):
                    for half in range(2):
                        last = nc.tensor.matmul(pp[:, bank + half, 0:HB], w[:], src[:, half * HB:(half + 1) * HB],
                                                start=True, stop=True)
                    return last

                def post(p):
                    def ms_qk():
                        pe.wait_ge(sq_ready, (p + 1).v)
                        sum_rows(blk, tmp[0], 0)
                        sum_rows(blk, tmp[1], 2).then_inc(qk_ms_done, 1)

                    def to_tokens():
                        pe.wait_ge(silu_ready, (p + 1).v)
                        pe.wait_ge(qk_rstd, (p + 1).v)
                        for n_, (src, at0) in enumerate(((v_T, SEQ), (mk_T, CS), (mv_T, SEQ))):
                            for c in range(NCH):
                                nc.tensor.transpose(pp[:, n_, c * P:(c + 1) * P], src[:, c * P:(c + 1) * P], ident[:])
                            last = nc.tensor.transpose(pp[0:DEC, 3, n_ * P:(n_ + 1) * P], src[:, at0:at0 + DEC], ident[:])
                        last.then_inc(tok_done, 1)

                    def scores(m):
                        def piece():
                            if m == 0:
                                pe.wait_ge(qk_ready, (p + 1).v)
                                pe.wait_ge(tok_act, (p + 1).v)
                                pe.wait_ge(tok_dve, (p + 1).v)
                            else:
                                pe.wait_ge(probs_ready, (p * 2 + 1).v)
                            for i in range(NCH):
                                w = (i + 1) * P
                                nc.tensor.matmul(pp[:, i, 0:w], q_pad[:, m, i * P:(i + 1) * P], k_T[:, 0:w],
                                                 start=True, stop=False, skip_group_check=True)
                                last = nc.tensor.matmul(pp[:, i, w - P:w], early_q[:], late_row[:],
                                                        start=False, stop=True, skip_group_check=True)
                            last.then_inc(scores_done, 1)
                        return piece

                    def transpose_weights():
                        pe.wait_ge(weights_ready, (p + 1).v)
                        pe.wait_ge(probs_ready, (p * 2 + 2).v)
                        for j in range(NCH):
                            for i in range(j, NCH):
                                o = ATO[j] + (i - j) * P
                                nc.tensor.transpose(pp[:, o // 512, o % 512:o % 512 + P],
                                                    prob[0][:, OFF[i] + j * P:OFF[i] + (j + 1) * P], ident[:])
                        for c in range(NCH):
                            nc.tensor.matmul(pp[:, 3, c * P:(c + 1) * P], mk_T[:, c * P:(c + 1) * P],
                                             mq_T[:, c * P:(c + 1) * P], start=True, stop=True)
                        nc.tensor.matmul(pp[0:DEC, 2, 256:256 + DEC], mk_T[:, CS:CS + DEC], mq_T[:, CS:CS + DEC],
                                         start=True, stop=True).then_inc(at_done, 1)

                    def values():
                        pe.wait_ge(at_ready, (p + 1).v)
                        pe.wait_ge(pt_ready, (p + 1).v)
                        for j in range(NCH):
                            nc.tensor.matmul(pp[:, 0, j * P:SEQ], v_tok[:, j, :], at[:, ATO[j]:ATO[j] + SEQ - j * P],
                                             start=(j == 0), stop=(j == NCH - 1))
                        for c in range(NCH):
                            o = c * (DK + 1) if c < 3 else 512
                            nc.tensor.matmul(pp[:, 1 + o // 512, o % 512:o % 512 + DK + 1], kw_tok[:, c, :], v_aug[:, c, :],
                                             start=True, stop=True)
                        nc.tensor.matmul(pp[:, 2, DK + 1:2 * (DK + 1)], kw_tok[0:DEC, NCH, :], v_aug[0:DEC, NCH, :],
                                         start=True, stop=True).then_inc(pv_done, 1)

                    def sample_scores():
                        pe.wait_ge(att_ready, (p + 1).v)
                        pe.wait_ge(state_ready, (p + 1).v)
                        pe.wait_ge(cache_loaded, ((p + 1) * 32).v)
                        for b in range(2):
                            nc.tensor.matmul(pp[0:64, b, :], q_s[:], kc_sb[:, b * 512:(b + 1) * 512],
                                             start=True, stop=True)
                        nc.tensor.matmul(pp[0:64, 2, 0:DEC], q_s[:], k_T[:, SEQ:T],
                                         start=True, stop=True).then_inc(s_scores_done, 1)

                    def mlstm():
                        pe.wait_ge(s_exp_ready, (p + 1).v)
                        for bank, inter, intra in ((0, lambda c: state[:, c, 0:DK], lambda c: v_aug[:, c, 0:DK]),
                                                   (2, lambda c: n_b[:, c, :], lambda c: ones[:])):
                            for c in range(NCH):
                                o = pp[:, bank, c * P:(c + 1) * P]
                                if c:
                                    nc.tensor.matmul(o, inter(c - 1), mq_T[:, c * P:(c + 1) * P], start=True, stop=False)
                                nc.tensor.matmul(o, intra(c), decay[:, c * P:(c + 1) * P], start=(c == 0), stop=True)
                            first = c0_sb[:, 0:DK] if bank == 0 else n_b[:, NCH - 1, :]
                            own = v_aug[0:DEC, NCH, 0:DK] if bank == 0 else ones[0:DEC, :]
                            o = pp[:, bank + 1, 0:DEC]
                            nc.tensor.matmul(o, first, mq_T[:, CS:CS + DEC], start=True, stop=False)
                            last = nc.tensor.matmul(o, own, decay[0:DEC, SEQ:T], start=False, stop=True)
                        last.then_inc(h_done, 1)

                    def sample_transpose():
                        pe.wait_ge(consts_ready, N_CONSTS)
                        pe.wait_ge(s_probs_ready, (p + 1).v)
                        pe.wait_ge(h_ready, (p + 1).v)
                        for j in range(PAST // P):
                            nc.tensor.transpose(pp[:, 0, j * 64:(j + 1) * 64], s_prob[:, j * P:(j + 1) * P], ident[0:64, 0:64])
                        nc.tensor.transpose(pp[0:DEC, 1, 0:64], s_prob[:, PAST:PAST + DEC], ident[0:64, 0:64]).then_inc(s_pt_done, 1)

                    def sample_values():
                        pe.wait_ge(s_pt_ready, (p + 1).v)
                        pe.wait_ge(h_sq, (p + 1).v)
                        for j in range(PAST // P):
                            nc.tensor.matmul(pp[0:64, 2, 0:DK], s_pt[:, j * 64:(j + 1) * 64], vc_sb[:, j, :],
                                             start=(j == 0), stop=False)
                        nc.tensor.matmul(pp[0:64, 2, 0:DK], s_pt[0:DEC, 512:576], v_tok[0:DEC, NCH, :], start=False, stop=True)
                        sum_rows(ones, tmp[0], 0).then_inc(s_pv_done, 1)

                    def sample_combine():
                        pe.wait_ge(s_out_ready, (p + 1).v)
                        nc.tensor.matmul(pp[:, 3, 0:DEC], s_out, comb[:], start=True, stop=True).then_inc(comb_done, 1)

                    def ms_att():
                        pe.wait_ge(att_sq, (p + 1).v)
                        pe.wait_ge(ml_rstd, (p + 1).v)
                        sum_rows(ones, tmp[1], 0).then_inc(att_ms_done, 1)

                    return [ms_qk, to_tokens, scores(0), scores(1), transpose_weights, values, sample_scores,
                            mlstm, sample_transpose, sample_values, sample_combine, ms_att, None, None]

                def norm_sum():
                    pe.wait_ge(x_acc, KT)
                    sum_rows(ones, acc, 0).then_inc(norm_done, 1)

                def gate_columns():
                    pe.wait_ge(gates_exp, 1)
                    pe.wait_ge(rstd_ready, 1)
                    for n_, row in enumerate((gates[0], tmp[1])):
                        for c in range(NCH + 1):
                            w = min(P, T - c * P)
                            last = nc.tensor.transpose(pp[0:w, n_, c * 8:c * 8 + 8], row[0:HEADS, c * P:c * P + w],
                                                       ident[0:HEADS, 0:HEADS])
                    last.then_inc(cols_done, 1)

                pe.wait_ge(consts_ready, N_CONSTS)
                unit(Step(U_GATES), GR, (x_lo, 0), (None, norm_sum), taken=False)

                def prologue(h):
                    for n_ in range(PER_HEAD):
                        unit(Step(U_HEAD + n_), taken=n_ > 0, pieces=(None, gate_columns if n_ == 3 else None))

                def both(h, p):
                    pieces = post(p)
                    for n_ in range(PER_HEAD):
                        unit(h * PER_HEAD + (U_HEAD + n_), pieces=pieces[2 * n_:2 * n_ + 2])

                def last_post(p):
                    for piece in post(p):
                        if piece:
                            piece()

                head_steps(pe, prologue, both, last_post)

                unit(Step(U_OUT), x_ready=(mix_lo, 0), tiles=SPLIT)
                unit(Step(U_OUT + 1), tiles=SPLIT)
                with pe.Fori(1, KT // 2) as i:
                    unit(Step(U_OUT, 2, i), tiles=SPLIT)
                    unit(Step(U_OUT + 1, 2, i), tiles=SPLIT)

                def norm2_sum():
                    pe.wait_ge(x_acc, 2 * KT)
                    sum_rows(ones, acc, 0).then_inc(norm_done, 1)


                def down(b, u, parity, first):
                    for m in range(KT):
                        out = group(2 + m % 2)
                        if not (first and m < 2):
                            pe.wait_ge(down_taken, (b * KT + (m - 1)).v)
                        pe.wait_ge(lo_ready, (u * 4 + (m + 1)).v)
                        if m == 0:
                            pe.wait_ge(up_lo, (b * BLOCK + BLOCK).v)
                        for k in range(BLOCK):
                            last = passes(out, m % 4, k * P, P, hid_hi[:, parity, k, :], hid_lo[:, parity, k, :],
                                          k == 0, k == BLOCK - 1)
                        last.then_inc(quarter_done, 1)

                def step(b, first=False):
                    u = b * (2 * BLOCK) + U_FFN
                    for t in range(BLOCK):
                        unit_up(u + t, (b + 1) * BLOCK + t)
                    down(b, u + BLOCK, b.mod(2), first)

                def unit_up(u, t, x_ready=None, piece=None):
                    out = group((t.mod(2) + UP_SLOT) % 2)
                    if t.reg is None and t.first < 2:
                        pe.wait_ge(out_taken, U_UP0)
                    else:
                        pe.wait_ge(up_relu, (t + (-1)).v)
                    for q in range(4):
                        pe.wait_ge(lo_ready, (u * 4 + (q + 1)).v)
                        for k in range(4):
                            kk = 4 * q + k
                            if x_ready is not None:
                                pe.wait_ge(x_ready[0], x_ready[1] + kk + 1)
                            last = passes(out, q, k * P, P, act_hi[:, kk, :], act_lo[:, kk, :], kk == 0, kk == KT - 1)
                        last.then_inc(quarter_done, 1)
                    if piece:
                        piece()

                unit_up(Step(U_UP0), Step(0), (x_lo, KT), norm2_sum)
                for t in range(1, BLOCK):
                    unit_up(Step(U_UP0 + t), Step(t))
                pe.wait_ge(rstd_ready, 2)

                step(Step(0), first=True)
                step(Step(1))
                with pe.Fori(1, NBLK // 2 - 1) as i:
                    step(Step(0, 2, i))
                    step(Step(1, 2, i))
                step(Step(NBLK - 2))
                down(Step(NBLK - 1), Step(U_LAST), (NBLK - 1) % 2, False)

            @block.scalar
            def _(act):
                def split(q):
                    if q.reg is None and q.first >= QUARTERS:
                        return
                    slot = q.mod(4)
                    act.wait_ge(raw_loaded[slot], (Step(q.first // 4, q.per // 4, q.reg) * 16 + 16).v)
                    if not (q.reg is None and q.first < 4):
                        act.wait_ge(quarter_done, (q + (-3)).v)
                    nc.scalar.activation(w_hi[:, slot, :], w_raw[:, slot, :], ACT.Copy).then_inc(hi_ready, 1)

                def rsqrt(out, src, n_, wait_sem, wait_value, done):
                    act.wait_ge(wait_sem, wait_value)
                    nc.scalar.activation(two(out[:]), src, ACT.Ln, scale=1.0 / n_, bias=eps_ap).then_inc(act_self, 1)
                    self_n[0] = self_n[0] + 1
                    act.wait_ge(act_self, self_n[0].v)
                    nc.scalar.activation(out[:], out[:], ACT.Exp, scale=-0.5).then_inc(done, 1)

                eps_ap = eps_col[:]
                self_n = [Step(0)]

                def x_tile(k):
                    act.wait_ge(x_loaded[k // 2], 16)
                    nc.scalar.activation(act_hi[:, k, :], res[:, k, :], ACT.Copy, scale=sm[:, S_N1 + k:S_N1 + k + 1]
                                         ).then_inc(x_hi, 1)
                    if k >= 2:
                        act.wait_ge(x_acc, k - 1)
                    nc.scalar.activation(tmp[k % 2][:], res[:, k, :], ACT.Square).then_inc(x_sq, 1)

                for i in range(8):
                    act.dma_start(res[:, 2 * i:2 * i + 2, :], xT[:, 2 * i:2 * i + 2, :]).then_inc(x_loaded[i], 16)
                nc.scalar.preload_act_table_set("natural_log_exp_and_others")
                act.wait_ge(smalls_loaded, 16)
                act.wait_ge(consts_ready, N_CONSTS)
                split(Step(0))
                for k in range(KT):
                    x_tile(k)
                    if k in (3, 7, 11):
                        split(Step(1 + k // 4))
                act.wait_ge(lam_sum, 1)
                nc.scalar.activation(lam4[:, 2:4], lam4[:, 0:2], ACT.Exp).then_inc(lam_exp, 1)
                split(Step(4))
                split(Step(5))
                split(Step(6))
                rsqrt(rstd, pp[:, 0:2, 0:HB], D_MODEL, norm_done, 1, rstd_ready)

                def gates_exp_stage():
                    act.wait_ge(gates_raw, 1)
                    nc.scalar.activation(gates[2][0:HEADS, :], gates[1][0:HEADS, :], ACT.Abs).then_inc(act_self, 1)
                    self_n[0] = self_n[0] + 1
                    act.wait_ge(act_self, self_n[0].v)
                    nc.scalar.activation(gates[2][0:HEADS, :], gates[2][0:HEADS, :], ACT.Exp, scale=-1.0).then_inc(act_self, 1)
                    self_n[0] = self_n[0] + 1
                    act.wait_ge(act_self, self_n[0].v)
                    nc.scalar.activation(gates[2][0:HEADS, :], gates[2][0:HEADS, :], ACT.Ln, bias=1.0).then_inc(gates_lf, 1)

                def gates_weights_stage():
                    act.wait_ge(gates_scan, 1)
                    g, M, m, wi = gates[0], gates[4], gates[5], gates[6]
                    for c in range(NCH + 1):
                        lo, hi = c * P, min(T, (c + 1) * P)
                        prev = 0.0 if c == 0 else (m[0:HEADS, lo - 1:lo] if c < NCH else sm[0:HEADS, S_M0:S_M0 + 1])
                        nc.scalar.activation(wi[0:HEADS, lo:hi], M[0:HEADS, lo:hi], ACT.Exp, scale=-1.0, bias=prev)
                        nc.scalar.activation(tmp[1][0:HEADS, lo:hi], g[0:HEADS, lo:hi], ACT.Exp, bias=nm_end[:, c:c + 1])
                    nc.scalar.activation(tmp[0][0:HEADS, :], m[0:HEADS, :], ACT.Exp, scale=-1.0).then_inc(gates_exp, 1)

                def post(p):
                    def s0():
                        if not (p.reg is None and p.first == 0):
                            act.wait_ge(mix_ready, (p * 2).v)
                        nc.scalar.activation(tmp[0][:], k_raw[:], ACT.Square)
                        nc.scalar.activation(tmp[1][:], q_raw[:], ACT.Square).then_inc(sq_ready, 1)
                        act.wait_ge(conv_ready, (p * 2 + 1).v)
                        nc.scalar.activation(tmp[2][:, 0:SEQ], mk_T[:, 0:SEQ], ACT.Exp, scale=-1.0)
                        nc.scalar.activation(tmp[2][:, SEQ:T], mk_T[:, CS:CW], ACT.Exp, scale=-1.0).then_inc(conv_exp, 1)
                        act.wait_ge(conv_ready, (p * 2 + 2).v)
                        nc.scalar.activation(tmp[3][:, 0:SEQ], mq_T[:, 0:SEQ], ACT.Exp, scale=-1.0)
                        nc.scalar.activation(tmp[3][:, SEQ:T], mq_T[:, CS:CW], ACT.Exp, scale=-1.0).then_inc(conv_exp, 1)

                    def s1():
                        act.wait_ge(qk_ms_done, (p + 1).v)
                        nc.scalar.activation(two(tmp[0][:]), pp[:, 0:2, 0:HB], ACT.Ln, scale=1.0 / DQK, bias=eps_ap)
                        nc.scalar.activation(two(tmp[1][:]), pp[:, 2:4, 0:HB], ACT.Ln, scale=1.0 / DQK, bias=eps_ap).then_inc(post_self, 1)
                        act.wait_ge(post_self, (p * ACT_LINKS + 1).v)
                        nc.scalar.activation(tmp[0][:], tmp[0][:], ACT.Exp, scale=-0.5)
                        nc.scalar.activation(tmp[1][:], tmp[1][:], ACT.Exp, scale=-0.5).then_inc(qk_rstd, 1)

                    def s2():
                        act.wait_ge(tok_done, (p + 1).v)
                        nc.scalar.activation(flat(v_tok[:, 0:NCH, :]), pp[:, 0, :], ACT.Copy)
                        nc.scalar.activation(v_tok[0:DEC, NCH, :], pp[0:DEC, 3, 0:P], ACT.Copy)
                        nc.scalar.activation(v_aug[0:DEC, NCH, 0:DK], pp[0:DEC, 3, 2 * P:3 * P], ACT.Copy)
                        for c in range(NCH):
                            nc.scalar.activation(kw_tok[:, c, :], pp[:, 1, c * P:(c + 1) * P], ACT.Copy,
                                                 scale=ws_col[:, c, bass.ds(p.v, 1)])
                        nc.scalar.activation(kw_tok[0:DEC, NCH, :], pp[0:DEC, 3, P:2 * P], ACT.Copy,
                                             scale=ws_col[0:DEC, NCH, bass.ds(p.v, 1)]).then_inc(tok_act, 1)
                        act.wait_ge(decay_sum, (p + 1).v)
                        for c in range(NCH):
                            nc.scalar.activation(decay[:, c * P:(c + 1) * P], decay[:, c * P:(c + 1) * P], ACT.Exp,
                                                 scale=-1.0, bias=g_col[:, c, bass.ds(p.v, 1)])
                        nc.scalar.activation(decay[0:DEC, SEQ:T], decay[0:DEC, SEQ:T], ACT.Exp, scale=-1.0,
                                             bias=g_col[0:DEC, NCH, bass.ds(p.v, 1)]).then_inc(decay_ready, 1)

                    def soft(m):
                        def stage():
                            act.wait_ge(max_ready, (p * 2 + (m + 1)).v)
                            for i in range(NCH):
                                w = (i + 1) * P
                                last = nc.scalar.activation(prob[m][:, OFF[i]:OFF[i] + w], pp[:, i, 0:w], ACT.Exp,
                                                            bias=neg_max[:, m, i:i + 1], accum_out=sums[:, m, i:i + 1])
                            last.then_inc(probs_ready, 1)
                        return stage

                    def s5():
                        act.wait_ge(at_done, (p + 1).v)
                        nc.scalar.activation(at[:, 0:1024], flat(pp[:, 0:2, :]), ACT.Copy).then_inc(at_ready, 1)

                    def s6():
                        act.wait_ge(pv_done, (p + 1).v)
                        nc.scalar.activation(att_T[:, 0:SEQ], pp[:, 0, :], ACT.Copy).then_inc(att_ready, 1)

                    def s7():
                        act.wait_ge(s_max_ready, (p + 1).v)
                        nc.scalar.activation(s_prob, flat(pp[0:64, 0:3, :])[:, 0:PAST + DEC], ACT.Exp, bias=s_max[:],
                                             accum_out=s_sum[:]).then_inc(s_exp_ready, 1)

                    def s8():
                        act.wait_ge(h_done, (p + 1).v)
                        nc.scalar.activation(tmp[2][:, 0:SEQ], pp[:, 2, :], ACT.Abs)
                        nc.scalar.activation(tmp[2][:, SEQ:T], pp[:, 3, 0:DEC], ACT.Abs).then_inc(den_abs, 1)
                        act.wait_ge(h_ready, (p + 1).v)
                        nc.scalar.activation(tmp[0][:], tmp[3][:], ACT.Square).then_inc(h_sq, 1)
                        nc.scalar.activation(mo_T[:], mo_T[:], ACT.Exp, scale=-1.0).then_inc(o_exp, 1)

                    def s9():
                        act.wait_ge(s_pt_done, (p + 1).v)
                        nc.scalar.activation(s_pt[:, 0:512], pp[:, 0, :], ACT.Copy)
                        nc.scalar.activation(s_pt[0:DEC, 512:576], pp[0:DEC, 1, 0:64], ACT.Copy).then_inc(s_pt_ready, 1)

                    def s10():
                        act.wait_ge(s_pv_done, (p + 1).v)
                        nc.scalar.activation(s_out, pp[0:64, 2, 0:DK], ACT.Copy).then_inc(s_out_ready, 1)
                        nc.scalar.activation(two(tmp[0][:]), pp[:, 0:2, 0:HB], ACT.Ln, scale=1.0 / DK, bias=eps_ap).then_inc(post_self, 1)
                        act.wait_ge(post_self, (p * ACT_LINKS + 2).v)
                        nc.scalar.activation(tmp[0][:], tmp[0][:], ACT.Exp, scale=-0.5).then_inc(ml_rstd, 1)

                    def s11():
                        act.wait_ge(comb_done, (p + 1).v)
                        nc.scalar.activation(att_T[:, SEQ:T], pp[:, 3, 0:DEC], ACT.Copy).then_inc(post_self, 1)
                        act.wait_ge(post_self, (p * ACT_LINKS + 3).v)
                        nc.scalar.activation(tmp[1][:], att_T, ACT.Square).then_inc(att_sq, 1)

                    def s12():
                        act.wait_ge(att_ms_done, (p + 1).v)
                        nc.scalar.activation(two(tmp[1][:]), pp[:, 0:2, 0:HB], ACT.Ln, scale=1.0 / DK, bias=eps_ap).then_inc(post_self, 1)
                        act.wait_ge(post_self, (p * ACT_LINKS + 4).v)
                        nc.scalar.activation(tmp[1][:], tmp[1][:], ACT.Exp, scale=-0.5).then_inc(att_rstd, 1)

                    return [s0, s1, s2, soft(0), soft(1), s5, s6, s7, s8, s9, s10, s11, s12, None]

                def unit(u, pieces=(None, None)):
                    q = u * 4
                    split(q + 3)
                    if pieces[0]:
                        pieces[0]()
                    split(q + 4)
                    split(q + 5)
                    if pieces[1]:
                        pieces[1]()
                    split(q + 6)

                def prologue(h):
                    for n_ in range(PER_HEAD):
                        unit(Step(U_HEAD + n_), pieces=((gates_exp_stage, gates_weights_stage) if n_ == 1 else (None, None)))
                        if n_ == 4:
                            act.wait_ge(cols_done, 1)
                            nc.scalar.activation(flat(g_col[:, 0:NCH, :]), pp[:, 0, 0:32], ACT.Copy)
                            nc.scalar.activation(g_col[0:DEC, NCH, :], pp[0:DEC, 0, 32:40], ACT.Copy)
                            nc.scalar.activation(flat(ws_col[:, 0:NCH, :]), pp[:, 1, 0:32], ACT.Copy)
                            nc.scalar.activation(ws_col[0:DEC, NCH, :], pp[0:DEC, 1, 32:40], ACT.Copy).then_inc(cols_ready, 1)
                    act.wait_ge(rows_stored, 48)

                def both(h, p):
                    stages = post(p)
                    for n_ in range(PER_HEAD):
                        if n_ == 0:
                            act.wait_ge(out_taken, (h * PER_HEAD + U_HEAD).v)
                        unit(h * PER_HEAD + (U_HEAD + n_), pieces=stages[2 * n_:2 * n_ + 2])

                def split_mix(n_):
                    t = SPLIT[n_]
                    if n_ == 0:
                        act.wait_ge(quarter_done, 4 * U_OUT)
                    act.wait_ge(mix_ready, 2 * (t % HEADS) + 1 + (t < HEADS))
                    nc.scalar.activation(act_hi[:, t, :], res[:, t, :], ACT.Copy).then_inc(mix_hi, 1)

                def last_post(p):
                    act.wait_ge(out_taken, U_OUT)
                    for n_, stage in enumerate(post(p)):
                        if stage:
                            stage()
                        split_mix(n_)
                    for n_ in (14, 15):
                        split_mix(n_)

                head_steps(act, prologue, both, last_post)

                def out_unit(u, m):
                    unit(u)
                    act.wait_ge(out_taken, (u + 1).v)
                    act.wait_ge(x_acc, (m + KT).v)
                    nc.scalar.activation(tmp[0][:], res[:, bass.ds(m.v, 1), :].rearrange("p a b -> p (a b)"),
                                         ACT.Square).then_inc(x_sq, 1)

                out_unit(Step(U_OUT), Step(0))
                out_unit(Step(U_OUT + 1), Step(1))
                with act.Fori(1, KT // 2) as i:
                    out_unit(Step(U_OUT, 2, i), Step(0, 2, i))
                    out_unit(Step(U_OUT + 1, 2, i), Step(1, 2, i))
                act.wait_ge(quarter_done, 4 * U_UP0)
                act.wait_ge(out_taken, U_UP0)
                for k in range(KT):
                    nc.scalar.activation(act_hi[:, k, :], res[:, k, :], ACT.Copy, scale=sm[:, S_N2 + k:S_N2 + k + 1]
                                         ).then_inc(x_hi, 1)

                def hidden(t, k, parity):
                    act.wait_ge(up_relu, (t + 1).v)
                    nc.scalar.activation(hid_hi[:, parity, k, :], tmp[k % 2][:], ACT.Square).then_inc(up_hi, 1)

                act.wait_ge(kv_stored, 32 * HEADS)
                act.wait_ge(st_stored, 16 * HEADS)
                act.wait_ge(stored, 32)

                def up_units(u, t, parity, first):
                    for k in range(BLOCK):
                        unit(u + k)
                        if first and k == 0:
                            rsqrt(rstd, pp[:, 0:2, 0:HB], D_MODEL, norm_done, 2, rstd_ready)
                        hidden(t + k, k, parity)

                def down_units(u):
                    for k in range(BLOCK):
                        unit(u + k)

                up_units(Step(U_UP0), Step(0), 0, True)

                def step(b):
                    u = b * (2 * BLOCK) + U_FFN
                    up_units(u, (b + 1) * BLOCK, 1 - b.mod(2), False)
                    down_units(u + BLOCK)

                ffn_steps(act, step)
                down_units(Step(U_LAST))

            @block.vector
            def _(dve):
                links = [0]

                def link(ins):
                    links[0] += 1
                    ins.then_inc(dve_self, 1)
                    dve.wait_ge(dve_self, links[0])

                def split(q):
                    if q.reg is None and q.first >= QUARTERS:
                        return
                    slot = q.mod(4)
                    dve.wait_ge(hi_ready, (q + 1).v)
                    nc.vector.tensor_tensor(w_lo[:, slot, :], w_raw[:, slot, :], w_hi[:, slot, :].bitcast(f32),
                                            ALU.subtract).then_inc(lo_ready, 1)

                def x_tile(k):
                    dve.wait_ge(x_hi, k + 1)
                    nc.vector.scalar_tensor_tensor(out=act_lo[:, k, :], in0=res[:, k, :], scalar=sm[:, S_N1 + k:S_N1 + k + 1],
                                                   in1=act_hi[:, k, :].bitcast(f32), op0=ALU.mult, op1=ALU.subtract
                                                   ).then_inc(x_lo, 1)
                    dve.wait_ge(x_sq, k + 1)
                    nc.vector.tensor_tensor(acc[:], acc[:], tmp[k % 2][:], ALU.add).then_inc(x_acc, 1)
                    dve.wait_ge(x_acc, k + 1)

                dve.wait_ge(smalls_loaded, 16)
                dve.wait_ge(consts_ready, N_CONSTS)
                split(Step(0))
                for k in range(KT):
                    x_tile(k)
                    if k in (3, 7, 11):
                        split(Step(1 + k // 4))
                link(nc.vector.tensor_scalar(qn8[:], sm[:, S_QN:S_QN + 1], DQK ** -0.5, None, ALU.mult))
                link(nc.vector.tensor_scalar(an8[:], sm[:, S_AN:S_AN + 1], 1.0 - LAM_INIT, None, ALU.mult))
                lq = sm[:, S_LQ:S_ALL].rearrange("p (a b d) -> p a b d", a=2, b=2)
                link(nc.vector.tensor_tensor(lam_p, lq[:, :, 0, :], lq[:, :, 1, :], ALU.mult))
                nc.vector.reduce_sum(lam4[:, 0:2], lam_p, axis=AX.X).then_inc(lam_sum, 1)
                dve.wait_ge(lam_exp, 1)
                link(nc.vector.scalar_tensor_tensor(out=neg_lam[:], in0=lam4[:, 3:4], scalar=-LAM_INIT, in1=lam4[:, 2:3],
                                                    op0=ALU.add, op1=ALU.subtract))
                link(nc.vector.tensor_copy(lam_sel[32:64, :], neg_lam[32:64, :]))
                split(Step(4))
                split(Step(5))
                split(Step(6))
                dve.wait_ge(rstd_ready, 1)
                dve.wait_ge(quarter_done, 4)
                nc.vector.tensor_tensor(two(gates[0][0:GR, :]), group(0)[0:GR], two(rstd[0:GR, :]), ALU.mult).then_inc(out_taken, 1)
                dve.wait_ge(out_taken, 1)
                nc.vector.tensor_scalar(gates[1][0:HEADS, :], gates[0][32:GR, :], sm[32:GR, S_BG:S_BG + 1], None,
                                        ALU.add).then_inc(gates_raw, 1)
                link(nc.vector.tensor_scalar(gates[0][0:HEADS, :], gates[0][0:HEADS, :], sm[0:HEADS, S_BG:S_BG + 1], None, ALU.add))

                def gates_scan_stage():
                    z, b, g, M, m = (gates[i][0:HEADS, :] for i in (1, 3, 0, 4, 5))
                    dve.wait_ge(gates_lf, 1)
                    link(nc.vector.scalar_tensor_tensor(out=z, in0=z, scalar=0.0, in1=gates[2][0:HEADS, :],
                                                        op0=ALU.min, op1=ALU.subtract))
                    for c in range(NCH + 1):
                        lo, hi = c * P, min(T, (c + 1) * P)
                        last = nc.vector.tensor_tensor_scan(out=b[:, lo:hi], data0=z[:, lo:hi], data1=zero_row[:, lo:hi],
                                                            initial=0.0, op0=ALU.add, op1=ALU.add)
                    link(last)
                    link(nc.vector.tensor_tensor(g, g, b, ALU.subtract))
                    for c in range(NCH + 1):
                        lo, hi = c * P, min(T, (c + 1) * P)
                        prev = 0.0 if c == 0 else (m[:, lo - 1:lo] if c < NCH else sm[0:HEADS, S_M0:S_M0 + 1])
                        link(nc.vector.tensor_tensor_scan(out=M[:, lo:hi], data0=g[:, lo:hi], data1=g[:, lo:hi],
                                                          initial=prev, op0=ALU.max, op1=ALU.max))
                        link(nc.vector.tensor_tensor(m[:, lo:hi], b[:, lo:hi], M[:, lo:hi], ALU.add))
                        nc.vector.tensor_scalar(nm_end[:, c:c + 1], M[:, hi - 1:hi], -1.0, None, ALU.mult)
                    nc.vector.tensor_copy(m_end[:, 0:1], m[:, SEQ - 1:SEQ])
                    nc.vector.tensor_copy(m_end[:, 1:2], m[:, T - 1:T]).then_inc(gates_scan, 1)

                OUTS = {K_: k_raw, Q_: q_raw, V_: v_T, MV: mv_T, MO: mo_T}

                def evac(h, n_):
                    u = h * PER_HEAD + (U_HEAD + n_)
                    src = group(u.mod(2))
                    if n_ == K_ and not (h.reg is None and h.first == 0):
                        dve.wait_ge(qk_ready, h.v)
                    dve.wait_ge(quarter_done, (u * 4 + 4).v)
                    if n_ == V_ and not (h.reg is None and h.first == 0):
                        dve.wait_ge(kv_stored, (h * 32).v)
                    if n_ in OUTS:
                        nc.vector.tensor_tensor(two(OUTS[n_][:]), src, two(rstd[:]), ALU.mult).then_inc(out_taken, 1)
                        return
                    dst, tile = (mk_u, HEADS) if n_ == MK else (mq_u, 0)
                    c = bass.ds((h + tile).v, 1)
                    nc.vector.tensor_copy(dst[:, CS:CS + PAD], sm[:, S_SC:S_LQ].rearrange("p (c j) -> p c j", j=PAD)[:, c, :]
                                          .rearrange("p a j -> p (a j)"))
                    nc.vector.tensor_tensor(dst[:, PAD:PAD + HB], src[:, 0, :], rstd[:, 0:HB], ALU.mult)
                    nc.vector.tensor_tensor(dst[:, PAD + HB:CS], src[:, 1, 0:SEQ - HB], rstd[:, HB:SEQ], ALU.mult)
                    nc.vector.tensor_tensor(dst[:, CS + PAD:UW], src[:, 1, SEQ - HB:HB], rstd[:, SEQ:T], ALU.mult).then_inc(out_taken, 1)

                def post(p):
                    k_links = [0]

                    def own(ins):
                        k_links[0] += 1
                        ins.then_inc(post_dve, 1)
                        dve.wait_ge(post_dve, (p * DVE_LINKS + k_links[0]).v)

                    def conv(u, out, tile):
                        wcol = sm[:, S_CW:S_CB].rearrange("p (c j) -> p c j", j=CONV_W)
                        for j in range(CONV_W):
                            w = wcol[:, bass.ds((p + tile).v, 1), j:j + 1].rearrange("p a j -> p (a j)")
                            if j == 0:
                                own(nc.vector.tensor_scalar(out[:], u[:, 0:CW], w, sm[:, bass.ds((p + (tile + S_CB)).v, 1)],
                                                            ALU.mult, ALU.add))
                            else:
                                i = nc.vector.scalar_tensor_tensor(out=out[:], in0=u[:, j:j + CW], scalar=w, in1=out[:],
                                                                   op0=ALU.mult, op1=ALU.add)
                                if j < CONV_W - 1:
                                    own(i)
                                else:
                                    i.then_inc(conv_ready, 1)
                        c = bass.ds((p + tile).v, 1)
                        nc.vector.tensor_copy(conv_sb[:, c, 0, :].rearrange("p a j -> p (a j)"), u[:, SEQ:CS])
                        nc.vector.tensor_copy(conv_sb[:, c, 1, :].rearrange("p a j -> p (a j)"), u[:, UW - PAD:UW])

                    def s0():
                        dve.wait_ge(out_taken, (p * PER_HEAD + (U_HEAD + PER_HEAD)).v)
                        conv(mk_u, mk_T, HEADS)
                        conv(mq_u, mq_T, 0)

                    def silu(e, out, scale, n_):
                        dve.wait_ge(conv_exp, (p * 2 + n_).v)
                        own(nc.vector.tensor_scalar(e[:], e[:], 1.0, None, ALU.add))
                        own(nc.vector.reciprocal(e[:], e[:]))
                        nc.vector.scalar_tensor_tensor(out=out[:, 0:SEQ], in0=out[:, 0:SEQ], scalar=scale, in1=e[:, 0:SEQ],
                                                       op0=ALU.mult, op1=ALU.mult)
                        return nc.vector.scalar_tensor_tensor(out=out[:, CS:CW], in0=out[:, CS:CW], scalar=scale,
                                                              in1=e[:, SEQ:T], op0=ALU.mult, op1=ALU.mult)

                    def s1():
                        silu(tmp[2], mk_T, DK ** -0.5, 1)
                        silu(tmp[3], mq_T, 1.0, 2).then_inc(silu_ready, 1)
                        dve.wait_ge(qk_rstd, (p + 1).v)
                        nc.vector.scalar_tensor_tensor(out=k_T[:], in0=k_raw[:], scalar=sm[:, S_KN:S_KN + 1], in1=tmp[0][:],
                                                       op0=ALU.mult, op1=ALU.mult)
                        for m in range(2):
                            h = slice(64 * m, 64 * m + 64)
                            nc.vector.scalar_tensor_tensor(out=q_pad[h, m, 0:SEQ], in0=q_raw[h, 0:SEQ], scalar=qn8[h, :],
                                                           in1=tmp[1][h, 0:SEQ], op0=ALU.mult, op1=ALU.mult)
                            last = nc.vector.scalar_tensor_tensor(out=q_s[h, m * DEC:(m + 1) * DEC], in0=q_raw[h, SEQ:T],
                                                                  scalar=qn8[h, :], in1=tmp[1][h, SEQ:T],
                                                                  op0=ALU.mult, op1=ALU.mult)
                        last.then_inc(qk_ready, 1)

                    def s2():
                        dve.wait_ge(tok_done, (p + 1).v)
                        nc.vector.tensor_copy(v_aug[:, 0:NCH, 0:DK], pp[:, 2, :].rearrange("p (c d) -> p c d", c=NCH)
                                              ).then_inc(tok_dve, 1)
                        dve.wait_ge(rows_loaded, ((p + 1) * 48).v)
                        for c in range(NCH):
                            nc.vector.tensor_tensor(decay[:, c * P:(c + 1) * P], decay[:, c * P:(c + 1) * P], causal[:], ALU.add)
                        nc.vector.tensor_tensor(decay[:, SEQ:T], decay[:, SEQ:T], causal[:, 0:DEC], ALU.add).then_inc(decay_sum, 1)

                    def maxima(m):
                        dve.wait_ge(scores_done, (p * 2 + (m + 1)).v)
                        for i in range(NCH):
                            last = nc.vector.tensor_reduce(neg_max[:, m, i:i + 1], pp[:, i, 0:(i + 1) * P], axis=AX.X,
                                                           op=ALU.max, negate=True)
                        last.then_inc(max_ready, 1)

                    def s3():
                        maxima(0)

                    def s4():
                        maxima(1)
                        dve.wait_ge(probs_ready, (p * 2 + 2).v)
                        own(nc.vector.reciprocal(flat(inv[:]), flat(sums[:])))
                        own(nc.vector.tensor_scalar(inv[:, 1, :], inv[:, 1, :], neg_lam[:], None, ALU.mult))
                        for i in range(NCH):
                            s = slice(OFF[i], OFF[i] + (i + 1) * P)
                            last = nc.vector.tensor_scalar(prob[1][:, s], prob[1][:, s], inv[:, 1, i:i + 1], None, ALU.mult)
                        own(last)
                        for i in range(NCH):
                            s = slice(OFF[i], OFF[i] + (i + 1) * P)
                            last = nc.vector.scalar_tensor_tensor(out=prob[0][:, s], in0=prob[0][:, s], scalar=inv[:, 0, i:i + 1],
                                                                  in1=prob[1][:, s], op0=ALU.mult, op1=ALU.add)
                        last.then_inc(weights_ready, 1)

                    def s5():
                        dve.wait_ge(at_done, (p + 1).v)
                        dve.wait_ge(decay_ready, (p + 1).v)
                        nc.vector.tensor_copy(at[:, 1024:AW], pp[:, 2, 0:256])
                        nc.vector.tensor_tensor(decay[:, 0:SEQ], pp[:, 3, :], decay[:, 0:SEQ], ALU.mult)
                        nc.vector.tensor_tensor(decay[0:DEC, SEQ:T], pp[0:DEC, 2, 256:256 + DEC], decay[0:DEC, SEQ:T],
                                                ALU.mult).then_inc(pt_ready, 1)

                    def s6():
                        dve.wait_ge(pv_done, (p + 1).v)
                        dve.wait_ge(c0_loaded, ((p + 1) * 16).v)
                        if not (p.reg is None and p.first == 0):
                            dve.wait_ge(st_stored, (p * 16).v)
                        own(nc.vector.tensor_copy(state[:, 0, :], pp[:, 1, 0:DK + 1]))
                        for c in range(1, NCH):
                            src = pp[:, 1, c * (DK + 1):(c + 1) * (DK + 1)] if c < 3 else pp[:, 2, 0:DK + 1]
                            own(nc.vector.scalar_tensor_tensor(out=state[:, c, :], in0=state[:, c - 1, :],
                                                               scalar=wi_row[:, (c + 1) * P - 1:(c + 1) * P], in1=src,
                                                               op0=ALU.mult, op1=ALU.add))
                        nc.vector.scalar_tensor_tensor(out=state[:, NCH, :], in0=c0_sb[:], scalar=wi_row[:, T - 1:T],
                                                       in1=pp[:, 2, DK + 1:2 * (DK + 1)], op0=ALU.mult, op1=ALU.add)
                        for c in range(NCH):
                            n_col = state[:, c, DK:DK + 1] if c < NCH - 1 else c0_sb[:, DK:DK + 1]
                            nc.vector.tensor_scalar(n_b[:, c, :], ones[:], n_col, None, ALU.mult)
                        nc.vector.tensor_tensor(mq_T[:, P:SEQ], mq_T[:, P:SEQ], wi_row[:, P:SEQ], ALU.mult)
                        nc.vector.tensor_tensor(mq_T[:, CS:CW], mq_T[:, CS:CW], wi_row[:, SEQ:T], ALU.mult).then_inc(state_ready, 1)

                    def s7():
                        dve.wait_ge(s_scores_done, (p + 1).v)
                        nc.vector.tensor_reduce(s_max[:], flat(pp[0:64, 0:3, :])[:, 0:PAST + DEC], axis=AX.X, op=ALU.max,
                                                negate=True).then_inc(s_max_ready, 1)
                        dve.wait_ge(s_exp_ready, (p + 1).v)
                        own(nc.vector.reciprocal(s_inv[:], s_sum[:]))
                        own(nc.vector.tensor_tensor(s_inv[:], s_inv[:], lam_sel[:], ALU.mult))
                        nc.vector.tensor_scalar(s_prob, s_prob, s_inv[:], None, ALU.mult).then_inc(s_probs_ready, 1)

                    def s8():
                        dve.wait_ge(den_abs, (p + 1).v)
                        own(nc.vector.tensor_tensor(tmp[2][:], tmp[2][:], en_row[:], ALU.max))
                        own(nc.vector.reciprocal(tmp[2][:], tmp[2][:]))
                        nc.vector.tensor_tensor(tmp[3][:, 0:SEQ], pp[:, 0, :], tmp[2][:, 0:SEQ], ALU.mult)
                        nc.vector.tensor_tensor(tmp[3][:, SEQ:T], pp[:, 1, 0:DEC], tmp[2][:, SEQ:T], ALU.mult).then_inc(h_ready, 1)

                    def s10():
                        dve.wait_ge(o_exp, (p + 1).v)
                        own(nc.vector.tensor_scalar(mo_T[:], mo_T[:], 1.0, None, ALU.add))
                        own(nc.vector.reciprocal(mo_T[:], mo_T[:]))
                        dve.wait_ge(ml_rstd, (p + 1).v)
                        own(nc.vector.scalar_tensor_tensor(out=tmp[3][:], in0=tmp[3][:], scalar=sm[:, S_MN:S_MN + 1],
                                                           in1=tmp[0][:], op0=ALU.mult, op1=ALU.mult))
                        nc.vector.tensor_tensor(res[:, bass.ds((p + HEADS).v, 1), :].rearrange("p a b -> p (a b)"),
                                                tmp[3][:], mo_T[:], ALU.mult).then_inc(mix_ready, 1)

                    def s12():
                        dve.wait_ge(att_rstd, (p + 1).v)
                        nc.vector.scalar_tensor_tensor(out=res[:, bass.ds(p.v, 1), :].rearrange("p a b -> p (a b)"),
                                                       in0=att_T, scalar=an8[:], in1=tmp[1][:],
                                                       op0=ALU.mult, op1=ALU.mult).then_inc(mix_ready, 1)
                        assert k_links[0] == DVE_LINKS, k_links

                    return [s0, s1, s2, s3, s4, s5, s6, s7, s8, None, s10, None, s12, None]

                def unit(u, pieces=(None, None)):
                    q = u * 4
                    split(q + 3)
                    if pieces[0]:
                        pieces[0]()
                    split(q + 4)
                    split(q + 5)
                    if pieces[1]:
                        pieces[1]()
                    split(q + 6)

                def prologue(h):
                    for n_ in range(PER_HEAD):
                        unit(Step(U_HEAD + n_), pieces=(None, gates_scan_stage if n_ == 1 else None))
                        evac(h, n_)

                def both(h, p):
                    stages = post(p)
                    for n_ in range(PER_HEAD):
                        unit(h * PER_HEAD + (U_HEAD + n_), pieces=stages[2 * n_:2 * n_ + 2])
                        evac(h, n_)

                def split_mix(n_):
                    t = SPLIT[n_]
                    dve.wait_ge(mix_hi, n_ + 1)
                    nc.vector.tensor_tensor(act_lo[:, t, :], res[:, t, :], act_hi[:, t, :].bitcast(f32),
                                            ALU.subtract).then_inc(mix_lo, 1)

                def last_post(p):
                    for n_, stage in enumerate(post(p)):
                        if stage:
                            stage()
                        split_mix(n_)
                    for n_ in (14, 15):
                        split_mix(n_)
                    nc.vector.memset(acc[:], 0.0).then_inc(acc_clear, 1)

                head_steps(dve, prologue, both, last_post)

                def out_unit(u, m):
                    unit(u)
                    dve.wait_ge(quarter_done, (u * 4 + 4).v)
                    r = res[:, bass.ds(m.v, 1), :].rearrange("p a b -> p (a b)")
                    nc.vector.tensor_tensor(two(r), group(u.mod(2)), two(r), ALU.add).then_inc(out_taken, 1)
                    dve.wait_ge(x_sq, (m + (KT + 1)).v)
                    nc.vector.tensor_tensor(acc[:], acc[:], tmp[0][:], ALU.add).then_inc(x_acc, 1)
                    dve.wait_ge(x_acc, (m + (KT + 1)).v)

                dve.wait_ge(acc_clear, 1)
                dve.wait_ge(x_reloaded, 16 * KT)
                out_unit(Step(U_OUT), Step(0))
                out_unit(Step(U_OUT + 1), Step(1))
                with dve.Fori(1, KT // 2) as i:
                    out_unit(Step(U_OUT, 2, i), Step(0, 2, i))
                    out_unit(Step(U_OUT + 1, 2, i), Step(1, 2, i))
                for k in range(KT):
                    dve.wait_ge(x_hi, KT + k + 1)
                    nc.vector.scalar_tensor_tensor(out=act_lo[:, k, :], in0=res[:, k, :], scalar=sm[:, S_N2 + k:S_N2 + k + 1],
                                                   in1=act_hi[:, k, :].bitcast(f32), op0=ALU.mult, op1=ALU.subtract
                                                   ).then_inc(x_lo, 1)

                def hidden_out(u, t, k):
                    dve.wait_ge(quarter_done, (u * 4 + 4).v)
                    if not (t.reg is None and t.first < 2):
                        dve.wait_ge(up_hi, (t + (-1)).v)
                        dve.wait_ge(up_sq, (t + (-1)).v)
                    nc.vector.scalar_tensor_tensor(out=two(tmp[k % 2][:]), in0=group((k + UP_SLOT) % 2), scalar=0.0,
                                                   in1=two(rstd[:]), op0=ALU.max, op1=ALU.mult).then_inc(up_relu, 1)

                def hidden_lo(t, k, parity):
                    dve.wait_ge(up_hi, (t + 1).v)
                    dve.wait_ge(up_sq, (t + 1).v)
                    nc.vector.tensor_tensor(hid_lo[:, parity, k, :], tmp[2 + k % 2][:], hid_hi[:, parity, k, :].bitcast(f32),
                                            ALU.subtract).then_inc(up_lo, 1)

                def up_units(u, t, parity, first):
                    for k in range(BLOCK):
                        if first:
                            unit(u + k)
                        else:
                            split((u + k) * 4 + 3)
                            if k:
                                hidden_lo(t + (k - 1), k - 1, parity)
                            for q in (4, 5, 6):
                                split((u + k) * 4 + q)
                        if first and k == 0:
                            dve.wait_ge(rstd_ready, 2)
                        hidden_out(u + k, t + k, k)
                        if first:
                            hidden_lo(t + k, k, parity)

                def down_units(b, u, before=None):
                    for k in range(BLOCK):
                        for q in range(4):
                            m = 4 * k + q
                            split((u + k) * 4 + (q + 3))
                            if m == 0 and before:
                                before()
                            dve.wait_ge(quarter_done, ((u + k) * 4 + (q + 1)).v)
                            r = two(res[:, m, :])
                            nc.vector.tensor_tensor(r, group(2 + m % 2), r, ALU.add).then_inc(down_taken, 1)

                up_units(Step(U_UP0), Step(0), 0, True)

                def step(b):
                    u = b * (2 * BLOCK) + U_FFN
                    t = (b + 1) * BLOCK
                    up_units(u, t, 1 - b.mod(2), False)
                    down_units(b, u + BLOCK, lambda: hidden_lo(t + (BLOCK - 1), BLOCK - 1, 1 - b.mod(2)))

                ffn_steps(dve, step)
                down_units(Step(NBLK - 1), Step(U_LAST))


def kernel(x_prompt, x_sample, cache_k, cache_v, state_C, state_n, state_m, state_conv,
           norm1_w, w_in, conv_w, conv_b, b_gates, q_norm_w, k_norm_w, lambda_qk,
           att_norm_w, ml_norm_w, w_out, norm2_w, w_up, w_down):
    import numpy as np
    import concourse.bacc as bacc
    from concourse.bass_utils import run_bass_kernel_spmd

    def host(a):
        return np.asarray(a)

    x = np.concatenate([host(x_prompt)[0], host(x_sample)[0]], axis=0)
    xT = x.T.reshape(KT, P, T).transpose(1, 0, 2)

    def quarters(w):
        k, n = w.shape
        return w.reshape(k // QW, 4, P, n // P, P).transpose(3, 0, 2, 1, 4).reshape(n // P, k // QW, P, QW)

    w = host(w_in)[0]
    gate_w = np.zeros((D_MODEL, P), w.dtype)
    gate_w[:, 0:HEADS] = w[:, ROUNDS * P:ROUNDS * P + HEADS]
    gate_w[:, 32:GR] = w[:, ROUNDS * P + HEADS:]
    w_heads = quarters(w[:, 0:ROUNDS * P])
    order = [base * HEADS + h for h in range(HEADS) for base in (1, 0, 2, 4, 3, 5, 6)]
    up = quarters(host(w_up)[0]).reshape(NBLK, 4 * BLOCK, P, QW)
    down = quarters(host(w_down)[0]).transpose(1, 0, 2, 3)
    w_o = host(w_out)[0].reshape(KT, P, D_MODEL)[SPLIT].reshape(D_MODEL, D_MODEL)
    parts = [quarters(gate_w).reshape(-1, P, QW), w_heads[order].reshape(-1, P, QW),
             quarters(w_o).reshape(-1, P, QW), up[0]]
    for b in range(NBLK - 1):
        parts += [up[b + 1], down[b]]
    parts.append(down[NBLK - 1])
    wstream = np.concatenate(parts, axis=0)

    smalls = np.zeros((P, S_ALL), x.dtype)
    smalls[:, S_N1:S_N2] = host(norm1_w)[0].reshape(KT, P).T
    smalls[:, S_N2:S_CW] = host(norm2_w)[0].reshape(KT, P).T
    smalls[:, S_CW:S_CB] = host(conv_w)[0].reshape(CONV_W, 2 * HEADS, P).transpose(2, 1, 0).reshape(P, -1)
    smalls[:, S_CB:S_QN] = host(conv_b)[0].reshape(2 * HEADS, P).T
    smalls[:, S_QN] = np.concatenate([host(q_norm_w)[0]] * 2)
    smalls[:, S_KN] = np.concatenate([host(k_norm_w)[0]] * 2)
    smalls[:, S_AN] = host(att_norm_w)[0]
    smalls[:, S_MN] = host(ml_norm_w)[0]
    smalls[0:HEADS, S_BG] = host(b_gates)[0, 0:HEADS]
    smalls[32:GR, S_BG] = host(b_gates)[0, HEADS:]
    smalls[0:HEADS, S_M0] = host(state_m)[0, 0]
    smalls[:, S_SC:S_LQ] = host(state_conv)[0, 0].reshape(PAD, 2 * HEADS, P).transpose(2, 1, 0).reshape(P, -1)
    smalls[:, S_LQ:S_ALL] = host(lambda_qk)[0].reshape(1, -1)

    kcT = host(cache_k)[0, 0].transpose(1, 2, 0)
    vcl = host(cache_v)[0, 0].reshape(PAST // P, P, HEADS, DK).transpose(2, 1, 0, 3)
    c0 = np.concatenate([host(state_C)[0, 0], host(state_n)[0, 0][:, :, None]], axis=2)

    nc = bacc.Bacc("TRN2", target_bir_lowering=False, num_devices=1)
    f32 = mybir.dt.float32
    arrays = {}

    def given(name, a):
        arrays[name] = np.ascontiguousarray(a)
        return nc.dram_tensor(name, a.shape, f32, kind="ExternalInput").ap()

    def wanted(name, shape):
        return nc.dram_tensor(name, shape, f32, kind="ExternalOutput").ap()

    build(nc, given("in_xT", xT), given("in_wstream", wstream), given("in_smalls", smalls), given("in_kcT", kcT),
          given("in_vc", vcl), given("in_c0", c0),
          wanted("out_yT", (P, KT, T)), wanted("out_k", (HEADS, P, T)), wanted("out_v", (HEADS, P, T)),
          wanted("out_st", (HEADS, 2, P, DK + 1)), wanted("out_m", (HEADS, 2)),
          wanted("out_conv", (P, 2 * HEADS, 2, PAD)))
    r = run_bass_kernel_spmd(nc, [arrays], core_ids=[0]).results[0]

    y = r["out_yT"].transpose(2, 1, 0).reshape(T, D_MODEL)
    k = r["out_k"].transpose(2, 0, 1)
    v = r["out_v"].transpose(2, 0, 1)
    st, m = r["out_st"], r["out_m"]
    conv = r["out_conv"].transpose(2, 3, 1, 0).reshape(2, PAD, 2 * HEADS * P)

    def side(s):
        t = slice(0, SEQ) if s == 0 else slice(SEQ, T)
        return (k[None, None, t], v[None, None, t], st[None, None, :, s, :, 0:DK], st[None, None, :, s, :, DK],
                m[None, None, :, s], conv[None, None, s])

    return tuple(np.ascontiguousarray(a) for a in (y[None, 0:SEQ], y[None, SEQ:], *side(0), *side(1)))
```

```python
from contextlib import ExitStack

import concourse.bass as bass
from concourse import mybir

D_MODEL, SEQ, DEC, PAST = 2048, 512, 32, 1024
HEADS, DK, DQK = 8, 128, 64
D_FF = 4 * D_MODEL
CONV_W = 4
EPS = 1e-6
LAM_INIT = 0.2
P = 128
T = SEQ + DEC
HB = T // 2
KT = D_MODEL // P
NCH = SEQ // P
PER_HEAD = 7
MK, MQ, K_, Q_, V_, MV, MO = range(7)
ROUNDS = HEADS * PER_HEAD
BLOCK = 4
NBLK = D_FF // P // BLOCK
OUT_ORDER = ([(g, kk, kk == 0, kk == KT - 3) for g in range(KT) for kk in range(KT - 2)]
             + [(KT + g, kk, kk == KT - 2, kk == KT - 1) for g in range(KT) for kk in (KT - 2, KT - 1)])
OUT_ENDS = [[g for i, (g, _, _, end) in enumerate(OUT_ORDER) if end and i // 4 == r] for r in range(4 * KT)]
U_GATES = 0
U_HEAD = 1
U_OUT = U_HEAD + ROUNDS
U_UP0 = U_OUT + KT
U_FFN = U_UP0 + BLOCK
U_LAST = U_FFN + 2 * BLOCK * (NBLK - 1)
UNITS = U_LAST + BLOCK
QW = 4 * P
QUARTERS = 4 * UNITS
PAD = CONV_W - 1
UW = T + 2 * PAD
CW = UW - PAD
CS = SEQ + PAD
EARLY = KT - 2
SPLIT = [t for h in range(HEADS) for t in (h, HEADS + h)]
OFF = [0, 128, 384, 768]
AW = 1280
ATO = {0: 0, 1: 512, 3: 896, 2: 1024}
SB = (PAST + DEC) // 3
BIG = 1e30
LN_MAX = 2.0 ** 63
GR = 40

S_N1 = 0
S_N2 = S_N1 + KT
S_CW = S_N2 + KT
S_CB = S_CW + 2 * HEADS * CONV_W
S_QN = S_CB + 2 * HEADS
S_KN = S_QN + 1
S_AN = S_KN + 1
S_MN = S_AN + 1
S_BG = S_MN + 1
S_M0 = S_BG + 1
S_SC = S_M0 + 1
S_LQ = S_SC + 2 * HEADS * PAD
S_ALL = S_LQ + 4 * DQK

ACT_LINKS = 7
N_CONSTS = 24
UP_SLOT = U_UP0 % 2
DVE_LINKS = 18


class Step:

    def __init__(self, first, per=0, reg=None):
        self.first, self.per, self.reg = first, per, reg

    def __add__(self, n):
        return Step(self.first + n, self.per, self.reg)

    def __mul__(self, n):
        return Step(self.first * n, self.per * n, self.reg)

    def mod(self, n):
        assert self.per % n == 0
        return self.first % n

    @property
    def v(self):
        return self.first if self.reg is None else self.reg * self.per + self.first


def build(nc, xT, wstream, smalls, kcT, vc, c0, yT, k_out, v_out, st_out, m_out, conv_out):
    f32, f32r, bf16 = mybir.dt.float32, mybir.dt.float32r, mybir.dt.bfloat16
    ALU, ACT, AX = mybir.AluOpType, mybir.ActivationFunctionType, mybir.AxisListType
    ctx = ExitStack()
    with ctx:
        def sb(name, shape, dt=f32):
            return ctx.enter_context(nc.sbuf_tensor(name, shape, dt))

        def sem(name):
            return ctx.enter_context(nc.semaphore(name))

        res = sb("res", [P, KT, T])
        act_hi = sb("act_hi", [P, KT, T], f32r)
        act_lo = sb("act_lo", [P, KT, T], f32r)
        w_raw = sb("w_raw", [P, 4, QW])
        w_hi = sb("w_hi", [P, 4, QW], f32r)
        w_lo = sb("w_lo", [P, 4, QW], f32r)
        sm = sb("sm", [P, S_ALL])
        ident = sb("ident", [P, P])
        ones = sb("ones", [P, P])
        rstd = sb("rstd", [P, T])
        tmp = [sb(f"tmp{i}", [P, T]) for i in range(4)]
        acc = tmp[3]

        eps_col = sb("eps_col", [P, 1])
        psum = ctx.enter_context(nc.psum_tensor("psum", [P, 8, 512], f32))

        def group(slot):
            return psum[:, 2 * slot:2 * slot + 2, 0:HB]

        pp = psum[:, 4:8, :]

        rows_dram = nc.dram_tensor("gate_rows", [3, HEADS, T], f32, kind="Internal").ap()

        raw_loaded = [sem(f"raw_loaded{i}") for i in range(4)]
        hi_ready, lo_ready = sem("hi_ready"), sem("lo_ready")
        quarter_done = sem("quarter_done")
        out_taken = sem("out_taken")
        smalls_loaded, consts_ready = sem("smalls_loaded"), sem("consts_ready")
        x_loaded = [sem(f"x_loaded{i}") for i in range(8)]
        x_hi, x_sq, x_lo, x_acc = sem("x_hi"), sem("x_sq"), sem("x_lo"), sem("x_acc")
        norm_done, rstd_ready, acc_clear = sem("norm_done"), sem("rstd_ready"), sem("acc_clear")
        stored = sem("stored")

        def flat(ap):
            return ap.rearrange("p a b -> p (a b)")

        def two(ap):
            return ap.rearrange("p (a b) -> p a b", a=2)

        phase_a = ExitStack()
        with phase_a:
            def sa(name, shape, dt=f32):
                return phase_a.enter_context(nc.sbuf_tensor(name, shape, dt))

            k_raw, q_raw, v_T = sa("k_raw", [P, T]), sa("q_raw", [P, T]), sa("v_T", [P, T])
            mk_u, mq_u = sa("mk_u", [P, UW]), sa("mq_u", [P, UW])
            mv_T, mo_T = sa("mv_T", [P, T]), sa("mo_T", [P, T])
            k_T = sa("k_T", [P, T])
            q_pad = sa("q_pad", [P, 2, SEQ])
            q_s = sa("q_s", [P, 2 * DEC])
            mk_T, mq_T = sa("mk_T", [P, CW]), sa("mq_T", [P, CW])
            v_tok, kw_tok = sa("v_tok", [P, NCH + 1, DK]), sa("kw_tok", [P, NCH + 1, DK])
            v_aug = sa("v_aug", [P, NCH + 1, DK + 1])
            big = sa("big", [P, 3, AW])
            prob = [big[:, 0, :], big[:, 1, :]]
            at = big[:, 2, :]
            s_prob = big[0:64, 1, 0:PAST + DEC]
            s_pt = big[:, 2, 0:9 * 64]
            decay = sa("decay", [P, T])
            wi_row, en_row = sa("wi_row", [P, T]), sa("en_row", [P, T])
            state = sa("state", [P, NCH + 1, DK + 1])
            c0_sb = sa("c0_sb", [P, DK + 1])
            n_b = big[:, 0, 0:SEQ].rearrange("p (c d) -> p c d", c=NCH)
            kc_sb, vc_sb = sa("kc_sb", [P, PAST + DEC]), sa("vc_sb", [P, PAST // P, DK])
            att_T = mk_T[:, 0:T]
            s_out = big[0:64, 1, PAST + DEC:PAST + DEC + DK]
            neg_max, sums, inv = sa("neg_max", [P, 2, NCH]), sa("sums", [P, 2, NCH]), sa("inv", [P, 2, NCH])
            s_max, s_sum, s_inv = sa("s_max", [64, 1]), sa("s_sum", [64, 1]), sa("s_inv", [64, 1])
            blk = sa("blk", [P, P])
            comb = sa("comb", [64, DEC])
            causal = sa("causal", [P, P])
            late_row, early_q = sa("late_row", [1, P], bf16), sa("early_q", [1, P], bf16)
            g_col, ws_col = sa("g_col", [P, NCH + 1, HEADS]), sa("ws_col", [P, NCH + 1, HEADS])
            conv_sb = sa("conv_sb", [P, 2 * HEADS, 2, PAD])
            qn8, an8, lam4, neg_lam, lam_sel = (sa("qn8", [P, 1]), sa("an8", [P, 1]), sa("lam4", [P, 4]),
                                                sa("neg_lam", [P, 1]), sa("lam_sel", [64, 1]))
            lam_p = kw_tok[:, 0, :].rearrange("p (a d) -> p a d", a=2)
            m_end, nm_end = sa("m_end", [HEADS, 2]), sa("nm_end", [HEADS, NCH + 1])
            gates = [flat(big[:, :, :])[0:GR, i * T:(i + 1) * T] for i in range(7)]
            zero_row = tmp[2][0:HEADS, :]

            gate_taken, gates_raw, gates_lf, gates_scan = sem("gate_taken"), sem("gates_raw"), sem("gates_lf"), sem("gates_scan")
            gates_exp, cols_done, cols_ready = sem("gates_exp"), sem("cols_done"), sem("cols_ready")
            rows_stored, rows_loaded, cache_loaded, c0_loaded = (sem("rows_stored"), sem("rows_loaded"),
                                                                 sem("cache_loaded"), sem("c0_loaded"))
            lam_sum, lam_exp = sem("lam_sum"), sem("lam_exp")
            kv_stored, st_stored = sem("kv_stored"), sem("st_stored")
            sq_ready, conv_ready, conv_exp = sem("sq_ready"), sem("conv_ready"), sem("conv_exp")
            qk_ms_done, qk_rstd, qk_ready, silu_ready = sem("qk_ms_done"), sem("qk_rstd"), sem("qk_ready"), sem("silu_ready")
            tok_done, tok_act, tok_dve, decay_sum, decay_ready = (sem("tok_done"), sem("tok_act"), sem("tok_dve"),
                                                                  sem("decay_sum"), sem("decay_ready"))
            scores_done, max_ready, probs_ready, weights_ready = (sem("scores_done"), sem("max_ready"),
                                                                  sem("probs_ready"), sem("weights_ready"))
            at_done, at_ready, pt_ready, pv_done = sem("at_done"), sem("at_ready"), sem("pt_ready"), sem("pv_done")
            att_ready, state_ready, s_scores_done, s_max_ready = (sem("att_ready"), sem("state_ready"),
                                                                  sem("s_scores_done"), sem("s_max_ready"))
            den_abs = sem("den_abs")
            s_exp_ready, s_probs_ready, h_done, h_ready, h_sq = (sem("s_exp_ready"), sem("s_probs_ready"), sem("h_done"),
                                                                 sem("h_ready"), sem("h_sq"))
            s_pt_done, s_pt_ready, s_pv_done, s_out_ready, ml_rstd, o_exp = (
                sem("s_pt_done"), sem("s_pt_ready"), sem("s_pv_done"), sem("s_out_ready"), sem("ml_rstd"), sem("o_exp"))
            silu_den, silu_sig, o_den, o_sig = sem("silu_den"), sem("silu_sig"), sem("o_den"), sem("o_sig")
            comb_done, s_att_ready, att_sq, att_ms_done, att_rstd = (sem("comb_done"), sem("s_att_ready"), sem("att_sq"),
                                                                     sem("att_ms_done"), sem("att_rstd"))
            mix_ready, mix_hi, mix_lo, x_reloaded = sem("mix_ready"), sem("mix_hi"), sem("mix_lo"), [sem(f"x_reloaded{t}") for t in range(KT)]
            dve_self, act_self, post_self, post_dve = sem("dve_self"), sem("act_self"), sem("post_self"), sem("post_dve")
            up_relu, up_hi, up_sq, up_lo, down_taken = sem("up_relu"), sem("up_hi"), sem("up_sq"), sem("up_lo"), sem("down_taken")


            def head_steps(eng, prologue, both):
                prologue(Step(0))
                both(Step(1), Step(0))
                with eng.Fori(0, HEADS // 2 - 1) as i:
                    both(Step(2, 2, i), Step(1, 2, i))
                    both(Step(3, 2, i), Step(2, 2, i))

            def ffn_steps(eng, step):
                with eng.Fori(0, NBLK // 2 - 1) as i:
                    step(Step(0, 2, i))
                    step(Step(1, 2, i))
                step(Step(NBLK - 2))


            phase_a.close()
            hid_hi = sb("hid_hi", [P, 2, BLOCK, T], f32r)
            hid_lo = sb("hid_lo", [P, 2, BLOCK, T], f32r)
            block = ctx.enter_context(nc.Block())

            @block.sync
            def _(sp):
                for q in range(4):
                    sp.dma_start(w_raw[:, q, :], wstream[q]).then_inc(raw_loaded[q], 16)
                with sp.Fori(0, QUARTERS // 4 - 1) as i:
                    for q in range(4):
                        sp.wait_ge(lo_ready, i * 4 + (q + 1))
                        sp.dma_start(w_raw[:, q, :],
                                     wstream[bass.ds(i * 4 + (q + 4), 1)].rearrange("a p n -> p (a n)")
                                     ).then_inc(raw_loaded[q], 16)

            @block.gpsimd
            def _(pool):
                n = [0]

                def const(ins):
                    n[0] += 1
                    ins.then_inc(consts_ready, 1)
                    pool.wait_ge(consts_ready, n[0])

                const(nc.gpsimd.memset(ones[:], 1.0))
                const(nc.gpsimd.memset(ident[:], 0.0))
                const(nc.gpsimd.memset(blk[:], 1.0))
                const(nc.gpsimd.memset(comb[:], 0.0))
                const(nc.gpsimd.memset(causal[:], 0.0))
                const(nc.gpsimd.memset(early_q[:], 0.0))
                const(nc.gpsimd.memset(late_row[:], 0.0))
                const(nc.gpsimd.memset(q_pad[:], 0.0))
                const(nc.gpsimd.memset(q_s[:], 0.0))
                const(nc.gpsimd.memset(mk_u[:, 0:PAD], 0.0))
                const(nc.gpsimd.memset(mq_u[:, 0:PAD], 0.0))
                const(nc.gpsimd.memset(v_aug[:, :, DK:DK + 1], 1.0))
                const(nc.gpsimd.memset(acc[:], 0.0))
                const(nc.gpsimd.memset(zero_row, 0.0))
                const(nc.gpsimd.memset(lam_sel[0:32, :], 1.0))
                const(nc.gpsimd.memset(eps_col[:], EPS))
                const(nc.gpsimd.affine_select(out=ident[:], in_=ident[:], compare_op=ALU.not_equal, fill=1.0,
                                              base=0, pattern=[[-1, P]], channel_multiplier=1))
                const(nc.gpsimd.memset(blk[0:64, 64:128], 0.0))
                const(nc.gpsimd.memset(blk[64:128, 0:64], 0.0))
                const(nc.gpsimd.affine_select(out=causal[:], in_=causal[:], compare_op=ALU.is_ge, fill=BIG,
                                              base=0, pattern=[[1, P]], channel_multiplier=-1))
                const(nc.gpsimd.affine_select(out=comb[:], in_=comb[:], compare_op=ALU.not_equal, fill=1.0,
                                              base=0, pattern=[[-1, DEC]], channel_multiplier=1))
                const(nc.gpsimd.memset(early_q[:, 0:64], 1.0))
                const(nc.gpsimd.memset(late_row[:, 64:128], -BIG))
                const(nc.gpsimd.affine_select(out=comb[:], in_=comb[:], compare_op=ALU.not_equal, fill=1.0,
                                              base=-DEC, pattern=[[-1, DEC]], channel_multiplier=1))
                assert n[0] == N_CONSTS, n

                def dma_after_waits(dst, src, done):
                    pool.wait_ge(smalls_loaded, 16)
                    pool.dma_start(dst, src).then_inc(done, 16)

                def load_head(p, first):
                    if not first:
                        pool.wait_ge(s_scores_done, p.v)
                    dma_after_waits(kc_sb[:, 0:PAST], kcT[bass.ds(p.v, 1)].rearrange("a p n -> p (a n)"), cache_loaded)
                    if not first:
                        pool.wait_ge(smalls_loaded, 16)
                        pool.wait_ge(s_pv_done, p.v)
                        pool.wait_ge(h_done, p.v)
                        pool.wait_ge(h_ready, p.v)
                    pool.dma_start(vc_sb[:], vc[bass.ds(p.v, 1)].rearrange("a p t n -> p (a t) n")).then_inc(cache_loaded, 16)
                    pool.dma_start(c0_sb[:], c0[bass.ds(p.v, 1)].rearrange("a p n -> p (a n)")).then_inc(c0_loaded, 16)
                    for r, row in enumerate((decay, wi_row, en_row)):
                        pool.dma_start(row[:], rows_dram[r, bass.ds(p.v, 1), :].to_broadcast([P, T])).then_inc(rows_loaded, 16)

                def store_head(p):
                    pool.wait_ge(qk_ready, (p + 1).v)
                    dma_after_waits(k_out[bass.ds(p.v, 1)].rearrange("a p n -> p (a n)"), k_T[:], kv_stored)
                    pool.dma_start(v_out[bass.ds(p.v, 1)].rearrange("a p n -> p (a n)"), v_T[:]).then_inc(kv_stored, 16)
                    pool.wait_ge(state_ready, (p + 1).v)
                    dma_after_waits(st_out[bass.ds(p.v, 1)].rearrange("a s p n -> p (a s) n"),
                                    state[:, NCH - 1:NCH + 1, :], st_stored)

                def prologue(h):
                    pool.wait_ge(gates_exp, 1)
                    pool.dma_start(rows_dram[0], gates[4][0:HEADS, :]).then_inc(rows_stored, 16)
                    pool.dma_start(rows_dram[1], gates[6][0:HEADS, :]).then_inc(rows_stored, 16)
                    pool.dma_start(rows_dram[2], tmp[0][0:HEADS, :]).then_inc(rows_stored, 16)
                    pool.dma_start(m_out, m_end[:]).then_inc(stored, 16)
                    pool.wait_ge(rows_stored, 48)
                    load_head(Step(0), True)

                def both(h, p):
                    store_head(p)
                    load_head(h, False)

                def reload(n_):
                    pool.wait_ge(mix_lo, n_ + 1)
                    pool.dma_start(res[:, SPLIT[n_], :], xT[:, SPLIT[n_], :]).then_inc(x_reloaded[SPLIT[n_]], 16)

                head_steps(pool, prologue, both)
                for n_ in range(EARLY):
                    reload(n_)
                store_head(Step(HEADS - 1))
                for n_ in range(EARLY, KT):
                    reload(n_)
                for j in range(KT):
                    if j == 0:
                        pool.wait_ge(acc_clear, 1)
                    pool.wait_ge(x_sq, KT + j + 1)
                    nc.gpsimd.tensor_tensor(acc[:], acc[:], tmp[j % 2][:], ALU.add).then_inc(x_acc, 1)
                    pool.wait_ge(x_acc, KT + j + 1)
                pool.dma_start(conv_out, conv_sb[:]).then_inc(stored, 16)

                def square(t, slot):
                    pool.wait_ge(up_relu, (t + 1).v)
                    if not (t.reg is None and t.first < 2):
                        pool.wait_ge(up_lo, (t + (-1)).v)
                    nc.gpsimd.tensor_tensor(tmp[2 + slot][:], tmp[slot][:], tmp[slot][:], ALU.mult).then_inc(up_sq, 1)

                for t in range(BLOCK):
                    square(Step(t), t % 2)

                def step(b):
                    for t in range(BLOCK):
                        square((b + 1) * BLOCK + t, t % 2)

                ffn_steps(pool, step)
                pool.wait_ge(kv_stored, 16 * 2 * HEADS)
                pool.wait_ge(st_stored, 16 * HEADS)
                for m in range(KT):
                    pool.wait_ge(down_taken, (NBLK - 1) * KT + m + 1)
                    pool.dma_start(yT[:, m, :], res[:, m, :]).then_inc(stored, 16)
                pool.wait_ge(stored, 16 * (KT + 2))

            @block.tensor
            def _(pe):
                def passes(out, w_slot, col, m, x_hi_t, x_lo_t, start, stop):
                    for n_, (w, x) in enumerate(((w_hi, x_hi_t), (w_hi, x_lo_t), (w_lo, x_hi_t))):
                        for half in range(2):
                            last = nc.tensor.matmul(out[0:m, half, :], w[:, w_slot, col:col + m],
                                                    x[:, half * HB:(half + 1) * HB],
                                                    start=start and n_ == 0, stop=stop and n_ == 2)
                    return last

                def unit(u, m=P, x_ready=None, pieces=(None, None), taken=True, tiles=range(KT)):
                    out = group(u.mod(2))
                    if taken:
                        pe.wait_ge(out_taken, (u + (-1)).v)
                    for q in range(4):
                        pe.wait_ge(lo_ready, (u * 4 + (q + 1)).v)
                        for k in range(4):
                            kk = 4 * q + k
                            if x_ready is not None:
                                pe.wait_ge(x_ready[0], x_ready[1] + kk + 1)
                            t = tiles[kk]
                            last = passes(out, q, k * P, m, act_hi[:, t, :], act_lo[:, t, :], kk == 0, kk == KT - 1)
                        last.then_inc(quarter_done, 1)
                        if q == 1 and pieces[0]:
                            pieces[0]()
                        if q == 3 and pieces[1]:
                            pieces[1]()

                def sum_rows(w, src, bank):
                    for half in range(2):
                        last = nc.tensor.matmul(pp[:, bank + half, 0:HB], w[:], src[:, half * HB:(half + 1) * HB],
                                                start=True, stop=True)
                    return last

                def post(p):
                    def ms_qk():
                        pe.wait_ge(sq_ready, (p + 1).v)
                        sum_rows(blk, tmp[0], 0)
                        sum_rows(blk, tmp[1], 2).then_inc(qk_ms_done, 1)

                    def to_tokens():
                        pe.wait_ge(silu_ready, (p + 1).v)
                        pe.wait_ge(qk_rstd, (p + 1).v)
                        for n_, (src, at0) in enumerate(((v_T, SEQ), (mk_T, CS), (mv_T, SEQ))):
                            for c in range(NCH):
                                nc.tensor.transpose(pp[:, n_, c * P:(c + 1) * P], src[:, c * P:(c + 1) * P], ident[:])
                            last = nc.tensor.transpose(pp[0:DEC, 3, n_ * P:(n_ + 1) * P], src[:, at0:at0 + DEC], ident[:])
                        last.then_inc(tok_done, 1)

                    def scores(m):
                        def piece():
                            if m == 0:
                                pe.wait_ge(qk_ready, (p + 1).v)
                                pe.wait_ge(tok_act, (p + 1).v)
                                pe.wait_ge(tok_dve, (p + 1).v)
                            else:
                                pe.wait_ge(probs_ready, (p * 2 + 1).v)
                            for i in range(NCH):
                                w = (i + 1) * P
                                nc.tensor.matmul(pp[:, i, 0:w], q_pad[:, m, i * P:(i + 1) * P], k_T[:, 0:w],
                                                 start=True, stop=False, skip_group_check=True)
                                last = nc.tensor.matmul(pp[:, i, w - P:w], early_q[:], late_row[:],
                                                        start=False, stop=True, skip_group_check=True)
                            last.then_inc(scores_done, 1)
                        return piece

                    def transpose_weights():
                        pe.wait_ge(weights_ready, (p + 1).v)
                        pe.wait_ge(probs_ready, (p * 2 + 2).v)
                        for j in range(NCH):
                            for i in range(j, NCH):
                                o = ATO[j] + (i - j) * P
                                nc.tensor.transpose(pp[:, o // 512, o % 512:o % 512 + P],
                                                    prob[0][:, OFF[i] + j * P:OFF[i] + (j + 1) * P], ident[:])
                        for c in range(NCH):
                            nc.tensor.matmul(pp[:, 3, c * P:(c + 1) * P], mk_T[:, c * P:(c + 1) * P],
                                             mq_T[:, c * P:(c + 1) * P], start=True, stop=True)
                        nc.tensor.matmul(pp[0:DEC, 2, 256:256 + DEC], mk_T[:, CS:CS + DEC], mq_T[:, CS:CS + DEC],
                                         start=True, stop=True).then_inc(at_done, 1)

                    def values():
                        pe.wait_ge(at_ready, (p + 1).v)
                        pe.wait_ge(pt_ready, (p + 1).v)
                        for j in range(NCH):
                            nc.tensor.matmul(pp[:, 0, j * P:SEQ], v_tok[:, j, :], at[:, ATO[j]:ATO[j] + SEQ - j * P],
                                             start=(j == 0), stop=(j == NCH - 1))
                        for c in range(NCH):
                            o = c * (DK + 1) if c < 3 else 512
                            nc.tensor.matmul(pp[:, 1 + o // 512, o % 512:o % 512 + DK + 1], kw_tok[:, c, :], v_aug[:, c, :],
                                             start=True, stop=True)
                        nc.tensor.matmul(pp[:, 2, DK + 1:2 * (DK + 1)], kw_tok[0:DEC, NCH, :], v_aug[0:DEC, NCH, :],
                                         start=True, stop=True).then_inc(pv_done, 1)

                    def sample_scores():
                        pe.wait_ge(att_ready, (p + 1).v)
                        pe.wait_ge(state_ready, (p + 1).v)
                        pe.wait_ge(cache_loaded, ((p + 1) * 32).v)
                        for b in range(3):
                            last = nc.tensor.matmul(pp[0:64, b, 0:SB], q_s[:], kc_sb[:, b * SB:(b + 1) * SB],
                                                    start=True, stop=True)
                        last.then_inc(s_scores_done, 1)

                    def mlstm():
                        pe.wait_ge(s_exp_ready, (p + 1).v)
                        for bank, inter, intra in ((0, lambda c: state[:, c, 0:DK], lambda c: v_aug[:, c, 0:DK]),
                                                   (2, lambda c: n_b[:, c, :], lambda c: ones[:])):
                            for c in range(NCH):
                                o = pp[:, bank, c * P:(c + 1) * P]
                                if c:
                                    nc.tensor.matmul(o, inter(c - 1), mq_T[:, c * P:(c + 1) * P], start=True, stop=False)
                                nc.tensor.matmul(o, intra(c), decay[:, c * P:(c + 1) * P], start=(c == 0), stop=True)
                            first = c0_sb[:, 0:DK] if bank == 0 else n_b[:, NCH - 1, :]
                            own = v_aug[0:DEC, NCH, 0:DK] if bank == 0 else ones[0:DEC, :]
                            o = pp[:, bank + 1, 0:DEC]
                            nc.tensor.matmul(o, first, mq_T[:, CS:CS + DEC], start=True, stop=False)
                            last = nc.tensor.matmul(o, own, decay[0:DEC, SEQ:T], start=False, stop=True)
                        last.then_inc(h_done, 1)

                    def sample_transpose():
                        pe.wait_ge(consts_ready, N_CONSTS)
                        pe.wait_ge(s_probs_ready, (p + 1).v)
                        pe.wait_ge(h_ready, (p + 1).v)
                        for j in range(PAST // P):
                            nc.tensor.transpose(pp[:, 0, j * 64:(j + 1) * 64], s_prob[:, j * P:(j + 1) * P], ident[0:64, 0:64])
                        nc.tensor.transpose(pp[0:DEC, 1, 0:64], s_prob[:, PAST:PAST + DEC], ident[0:64, 0:64]).then_inc(s_pt_done, 1)

                    def sample_values():
                        pe.wait_ge(s_pt_ready, (p + 1).v)
                        pe.wait_ge(h_sq, (p + 1).v)
                        for j in range(PAST // P):
                            nc.tensor.matmul(pp[0:64, 2, 0:DK], s_pt[:, j * 64:(j + 1) * 64], vc_sb[:, j, :],
                                             start=(j == 0), stop=False)
                        nc.tensor.matmul(pp[0:64, 2, 0:DK], s_pt[0:DEC, 512:576], v_tok[0:DEC, NCH, :], start=False, stop=True)
                        sum_rows(ones, tmp[0], 0).then_inc(s_pv_done, 1)

                    def sample_combine():
                        pe.wait_ge(s_out_ready, (p + 1).v)
                        nc.tensor.matmul(pp[:, 3, 0:DEC], s_out, comb[:], start=True, stop=True).then_inc(comb_done, 1)

                    def ms_att():
                        pe.wait_ge(att_sq, (p + 1).v)
                        pe.wait_ge(ml_rstd, (p + 1).v)
                        sum_rows(ones, tmp[1], 0).then_inc(att_ms_done, 1)

                    return [None, ms_qk, to_tokens, scores(0), scores(1), transpose_weights, values, sample_scores,
                            mlstm, sample_transpose, sample_values, sample_combine, ms_att, None]

                def norm_sum():
                    pe.wait_ge(consts_ready, N_CONSTS)
                    pe.wait_ge(x_acc, KT)
                    sum_rows(ones, acc, 0).then_inc(norm_done, 1)

                def gate_columns():
                    pe.wait_ge(gates_exp, 1)
                    pe.wait_ge(rstd_ready, 1)
                    for n_, row in enumerate((gates[0], tmp[1])):
                        for c in range(NCH + 1):
                            w = min(P, T - c * P)
                            last = nc.tensor.transpose(pp[0:w, n_, c * 8:c * 8 + 8], row[0:HEADS, c * P:c * P + w],
                                                       ident[0:HEADS, 0:HEADS])
                    last.then_inc(cols_done, 1)

                unit(Step(U_GATES), GR, (x_lo, 0), taken=False)

                def prologue(h):
                    for n_ in range(PER_HEAD):
                        unit(Step(U_HEAD + n_), taken=n_ > 0, pieces=(None, {0: norm_sum, 3: gate_columns}.get(n_)))

                def both(h, p):
                    pieces = post(p)
                    for n_ in range(PER_HEAD):
                        unit(h * PER_HEAD + (U_HEAD + n_), pieces=pieces[2 * n_:2 * n_ + 2])

                head_steps(pe, prologue, both)

                pieces = post(Step(HEADS - 1))
                for idx, (g, kk, first, end) in enumerate(OUT_ORDER):
                    r = idx // 4
                    if idx % 4 == 0:
                        pe.wait_ge(lo_ready, 4 * U_OUT + r + 1)
                    if first:
                        out = group((U_OUT + g) % 2)
                        pe.wait_ge(out_taken, U_OUT + g - 1)
                    if g in (0, KT):
                        pe.wait_ge(mix_lo, kk + 1)
                    t = SPLIT[kk]
                    last = passes(out, r % 4, (idx % 4) * P, P, act_hi[:, t, :], act_lo[:, t, :], first, end)
                    if idx % 4 == 3:
                        last.then_inc(quarter_done, 1)
                        if r % 2 and r // 2 < len(pieces) and pieces[r // 2]:
                            pieces[r // 2]()

                def norm2_sum():
                    pe.wait_ge(x_acc, 2 * KT)
                    sum_rows(ones, acc, 0).then_inc(norm_done, 1)


                def down(b, u, parity, first):
                    for m in range(KT):
                        out = group(2 + m % 2)
                        if not (first and m < 2):
                            pe.wait_ge(down_taken, (b * KT + (m - 1)).v)
                        pe.wait_ge(lo_ready, (u * 4 + (m + 1)).v)
                        if m == 0:
                            pe.wait_ge(up_lo, (b * BLOCK + BLOCK).v)
                        for k in range(BLOCK):
                            last = passes(out, m % 4, k * P, P, hid_hi[:, parity, k, :], hid_lo[:, parity, k, :],
                                          k == 0, k == BLOCK - 1)
                        last.then_inc(quarter_done, 1)

                def step(b, first=False):
                    u = b * (2 * BLOCK) + U_FFN
                    for t in range(BLOCK):
                        unit_up(u + t, (b + 1) * BLOCK + t)
                    down(b, u + BLOCK, b.mod(2), first)

                def unit_up(u, t, x_ready=None, piece=None):
                    out = group((t.mod(2) + UP_SLOT) % 2)
                    if t.reg is None and t.first < 2:
                        pe.wait_ge(out_taken, U_OUT + 2 * KT)
                    else:
                        pe.wait_ge(up_relu, (t + (-1)).v)
                    for q in range(4):
                        pe.wait_ge(lo_ready, (u * 4 + (q + 1)).v)
                        for k in range(4):
                            kk = 4 * q + k
                            if x_ready is not None:
                                pe.wait_ge(x_ready[0], x_ready[1] + kk + 1)
                            tile = SPLIT[kk]
                            last = passes(out, q, k * P, P, act_hi[:, tile, :], act_lo[:, tile, :], kk == 0, kk == KT - 1)
                        last.then_inc(quarter_done, 1)
                    if piece:
                        piece()

                unit_up(Step(U_UP0), Step(0), (x_lo, KT), norm2_sum)
                for t in range(1, BLOCK):
                    unit_up(Step(U_UP0 + t), Step(t))
                pe.wait_ge(rstd_ready, 2)

                step(Step(0), first=True)
                step(Step(1))
                with pe.Fori(1, NBLK // 2 - 1) as i:
                    step(Step(0, 2, i))
                    step(Step(1, 2, i))
                step(Step(NBLK - 2))
                down(Step(NBLK - 1), Step(U_LAST), (NBLK - 1) % 2, False)

            @block.scalar
            def _(act):
                def split(q):
                    if q.reg is None and q.first >= QUARTERS:
                        return
                    slot = q.mod(4)
                    act.wait_ge(raw_loaded[slot], (Step(q.first // 4, q.per // 4, q.reg) * 16 + 16).v)
                    if not (q.reg is None and q.first < 4):
                        act.wait_ge(quarter_done, (q + (-3)).v)
                    nc.scalar.activation(w_hi[:, slot, :], w_raw[:, slot, :], ACT.Copy).then_inc(hi_ready, 1)

                def rsqrt(out, src, n_, wait_sem, wait_value, done):
                    act.wait_ge(wait_sem, wait_value)
                    nc.scalar.activation(two(out[:]), src, ACT.Ln, scale=1.0 / n_, bias=eps_ap).then_inc(act_self, 1)
                    self_n[0] = self_n[0] + 1
                    act.wait_ge(act_self, self_n[0].v)
                    nc.scalar.activation(out[:], out[:], ACT.Exp, scale=-0.5).then_inc(done, 1)

                eps_ap = eps_col[:]
                self_n = [Step(0)]

                def x_tile(k):
                    act.wait_ge(x_loaded[k // 2], 16)
                    nc.scalar.activation(act_hi[:, k, :], res[:, k, :], ACT.Copy, scale=sm[:, S_N1 + k:S_N1 + k + 1]
                                         ).then_inc(x_hi, 1)

                def x_square(k):
                    if k >= 2:
                        act.wait_ge(x_acc, k - 1)
                    nc.scalar.activation(tmp[k % 2][:], res[:, k, :], ACT.Square).then_inc(x_sq, 1)

                act.dma_start(sm[:], smalls).then_inc(smalls_loaded, 16)
                for i in range(8):
                    act.dma_start(res[:, 2 * i:2 * i + 2, :], xT[:, 2 * i:2 * i + 2, :]).then_inc(x_loaded[i], 16)
                nc.scalar.preload_act_table_set("natural_log_exp_and_others")
                act.wait_ge(smalls_loaded, 16)
                for k in range(KT):
                    if k % 4 == 0:
                        split(Step(k // 4))
                    x_tile(k)
                split(Step(4))
                split(Step(5))
                for k in range(KT):
                    x_square(k)
                    if k == 5:
                        split(Step(6))
                act.wait_ge(lam_sum, 1)
                nc.scalar.activation(lam4[:, 2:4], lam4[:, 0:2], ACT.Exp).then_inc(lam_exp, 1)

                def gates_exp_stage():
                    act.wait_ge(gates_raw, 1)
                    nc.scalar.activation(gates[2][0:HEADS, :], gates[1][0:HEADS, :], ACT.Abs).then_inc(act_self, 1)
                    self_n[0] = self_n[0] + 1
                    act.wait_ge(act_self, self_n[0].v)
                    nc.scalar.activation(gates[2][0:HEADS, :], gates[2][0:HEADS, :], ACT.Exp, scale=-1.0).then_inc(act_self, 1)
                    self_n[0] = self_n[0] + 1
                    act.wait_ge(act_self, self_n[0].v)
                    nc.scalar.activation(gates[2][0:HEADS, :], gates[2][0:HEADS, :], ACT.Ln, bias=1.0).then_inc(gates_lf, 1)

                def gates_weights_stage():
                    act.wait_ge(gates_scan, 1)
                    g, M, m, wi = gates[0], gates[4], gates[5], gates[6]
                    for c in range(NCH + 1):
                        lo, hi = c * P, min(T, (c + 1) * P)
                        prev = 0.0 if c == 0 else (m[0:HEADS, lo - 1:lo] if c < NCH else sm[0:HEADS, S_M0:S_M0 + 1])
                        nc.scalar.activation(wi[0:HEADS, lo:hi], M[0:HEADS, lo:hi], ACT.Exp, scale=-1.0, bias=prev)
                        nc.scalar.activation(tmp[1][0:HEADS, lo:hi], g[0:HEADS, lo:hi], ACT.Exp, bias=nm_end[:, c:c + 1])
                    nc.scalar.activation(tmp[0][0:HEADS, :], m[0:HEADS, :], ACT.Exp, scale=-1.0).then_inc(gates_exp, 1)

                def post(p):
                    k_self = [0]

                    def own(ins):
                        k_self[0] += 1
                        ins.then_inc(post_self, 1)
                        act.wait_ge(post_self, (p * ACT_LINKS + k_self[0]).v)

                    def inverse(row, given, value, done):
                        act.wait_ge(given, value)
                        own(nc.scalar.activation(row, row, ACT.Ln))
                        nc.scalar.activation(row, row, ACT.Exp, scale=-1.0).then_inc(done, 1)

                    def s0():
                        if not (p.reg is None and p.first == 0):
                            act.wait_ge(mix_ready, (p * 2).v)
                        nc.scalar.activation(tmp[0][:], k_raw[:], ACT.Square)
                        nc.scalar.activation(tmp[1][:], q_raw[:], ACT.Square).then_inc(sq_ready, 1)
                        act.wait_ge(conv_ready, (p * 2 + 1).v)
                        nc.scalar.activation(tmp[2][:, 0:SEQ], mk_T[:, 0:SEQ], ACT.Exp, scale=-1.0)
                        nc.scalar.activation(tmp[2][:, SEQ:T], mk_T[:, CS:CW], ACT.Exp, scale=-1.0).then_inc(conv_exp, 1)
                        act.wait_ge(conv_ready, (p * 2 + 2).v)
                        nc.scalar.activation(tmp[3][:, 0:SEQ], mq_T[:, 0:SEQ], ACT.Exp, scale=-1.0)
                        nc.scalar.activation(tmp[3][:, SEQ:T], mq_T[:, CS:CW], ACT.Exp, scale=-1.0).then_inc(conv_exp, 1)

                    def s0b():
                        for n_ in range(2):
                            inverse(tmp[2 + n_][:], silu_den, (p * 2 + (n_ + 1)).v, silu_sig)

                    def s1():
                        act.wait_ge(qk_ms_done, (p + 1).v)
                        nc.scalar.activation(two(tmp[0][:]), pp[:, 0:2, 0:HB], ACT.Ln, scale=1.0 / DQK, bias=eps_ap)
                        own(nc.scalar.activation(two(tmp[1][:]), pp[:, 2:4, 0:HB], ACT.Ln, scale=1.0 / DQK, bias=eps_ap))
                        nc.scalar.activation(tmp[0][:], tmp[0][:], ACT.Exp, scale=-0.5)
                        nc.scalar.activation(tmp[1][:], tmp[1][:], ACT.Exp, scale=-0.5).then_inc(qk_rstd, 1)

                    def s2():
                        act.wait_ge(tok_done, (p + 1).v)
                        nc.scalar.activation(flat(v_tok[:, 0:NCH, :]), pp[:, 0, :], ACT.Copy)
                        nc.scalar.activation(v_tok[0:DEC, NCH, :], pp[0:DEC, 3, 0:P], ACT.Copy)
                        nc.scalar.activation(v_aug[0:DEC, NCH, 0:DK], pp[0:DEC, 3, 2 * P:3 * P], ACT.Copy)
                        nc.scalar.activation(kw_tok[0:DEC, NCH, :], pp[0:DEC, 3, P:2 * P], ACT.Copy,
                                             scale=ws_col[0:DEC, NCH, bass.ds(p.v, 1)]).then_inc(tok_act, 1)
                        act.wait_ge(decay_sum, (p + 1).v)
                        for c in range(NCH):
                            nc.scalar.activation(decay[:, c * P:(c + 1) * P], decay[:, c * P:(c + 1) * P], ACT.Exp,
                                                 scale=-1.0, bias=g_col[:, c, bass.ds(p.v, 1)])
                        nc.scalar.activation(decay[0:DEC, SEQ:T], decay[0:DEC, SEQ:T], ACT.Exp, scale=-1.0,
                                             bias=g_col[0:DEC, NCH, bass.ds(p.v, 1)]).then_inc(decay_ready, 1)

                    def soft(m):
                        def stage():
                            act.wait_ge(max_ready, (p * 2 + (m + 1)).v)
                            for i in range(NCH):
                                w = (i + 1) * P
                                last = nc.scalar.activation(prob[m][:, OFF[i]:OFF[i] + w], pp[:, i, 0:w], ACT.Exp,
                                                            bias=neg_max[:, m, i:i + 1], accum_out=sums[:, m, i:i + 1])
                            last.then_inc(probs_ready, 1)
                        return stage

                    def s5():
                        act.wait_ge(at_done, (p + 1).v)
                        nc.scalar.activation(at[:, 0:1024], flat(pp[:, 0:2, :]), ACT.Copy).then_inc(at_ready, 1)

                    def s6():
                        act.wait_ge(pv_done, (p + 1).v)
                        nc.scalar.activation(att_T[:, 0:SEQ], pp[:, 0, :], ACT.Copy).then_inc(att_ready, 1)

                    def s7():
                        act.wait_ge(s_max_ready, (p + 1).v)
                        nc.scalar.activation(s_prob.rearrange("p (b n) -> p b n", b=3), pp[0:64, 0:3, 0:SB], ACT.Exp, bias=s_max[:],
                                             accum_out=s_sum[:]).then_inc(s_exp_ready, 1)

                    def s8():
                        act.wait_ge(h_done, (p + 1).v)
                        nc.scalar.activation(tmp[2][:, 0:SEQ], pp[:, 2, :], ACT.Abs)
                        nc.scalar.activation(tmp[2][:, SEQ:T], pp[:, 3, 0:DEC], ACT.Abs).then_inc(den_abs, 1)
                        act.wait_ge(h_ready, (p + 1).v)
                        nc.scalar.activation(tmp[0][:], tmp[3][:], ACT.Square).then_inc(h_sq, 1)
                        act.wait_ge(out_taken, (p * PER_HEAD + (U_HEAD + PER_HEAD)).v)
                        nc.scalar.activation(mo_T[:], mo_T[:], ACT.Exp, scale=-1.0).then_inc(o_exp, 1)

                    def s9():
                        inverse(mo_T[:], o_den, (p + 1).v, o_sig)
                        act.wait_ge(s_pt_done, (p + 1).v)
                        nc.scalar.activation(s_pt[:, 0:512], pp[:, 0, :], ACT.Copy)
                        nc.scalar.activation(s_pt[0:DEC, 512:576], pp[0:DEC, 1, 0:64], ACT.Copy).then_inc(s_pt_ready, 1)

                    def s10():
                        act.wait_ge(s_pv_done, (p + 1).v)
                        nc.scalar.activation(s_out, pp[0:64, 2, 0:DK], ACT.Copy).then_inc(s_out_ready, 1)
                        own(nc.scalar.activation(two(tmp[0][:]), pp[:, 0:2, 0:HB], ACT.Ln, scale=1.0 / DK, bias=eps_ap))
                        nc.scalar.activation(tmp[0][:], tmp[0][:], ACT.Exp, scale=-0.5).then_inc(ml_rstd, 1)

                    def s11():
                        act.wait_ge(comb_done, (p + 1).v)
                        own(nc.scalar.activation(att_T[:, SEQ:T], pp[:, 3, 0:DEC], ACT.Copy))
                        nc.scalar.activation(tmp[1][:], att_T, ACT.Square).then_inc(att_sq, 1)

                    def s12():
                        act.wait_ge(att_ms_done, (p + 1).v)
                        own(nc.scalar.activation(two(tmp[1][:]), pp[:, 0:2, 0:HB], ACT.Ln, scale=1.0 / DK, bias=eps_ap))
                        nc.scalar.activation(tmp[1][:], tmp[1][:], ACT.Exp, scale=-0.5).then_inc(att_rstd, 1)
                        assert k_self[0] == ACT_LINKS, k_self

                    return [s0, s0b, s1, s2, soft(0), soft(1), s5, s6, s7, s8, s9, s10, s11, s12]

                def unit(u, pieces=(None, None)):
                    q = u * 4
                    split(q + 3)
                    if pieces[0]:
                        pieces[0]()
                    split(q + 4)
                    split(q + 5)
                    if pieces[1]:
                        pieces[1]()
                    split(q + 6)

                def prologue(h):
                    for n_ in range(PER_HEAD):
                        unit(Step(U_HEAD + n_), pieces=((gates_exp_stage, gates_weights_stage) if n_ == 1 else (None, None)))
                        if n_ == 0:
                            act.wait_ge(consts_ready, N_CONSTS)
                            rsqrt(rstd, pp[:, 0:2, 0:HB], D_MODEL, norm_done, 1, rstd_ready)
                        if n_ == 4:
                            act.wait_ge(cols_done, 1)
                            nc.scalar.activation(flat(g_col[:, 0:NCH, :]), pp[:, 0, 0:32], ACT.Copy)
                            nc.scalar.activation(g_col[0:DEC, NCH, :], pp[0:DEC, 0, 32:40], ACT.Copy)
                            nc.scalar.activation(flat(ws_col[:, 0:NCH, :]), pp[:, 1, 0:32], ACT.Copy)
                            nc.scalar.activation(ws_col[0:DEC, NCH, :], pp[0:DEC, 1, 32:40], ACT.Copy).then_inc(cols_ready, 1)
                    act.wait_ge(rows_stored, 48)

                def both(h, p):
                    stages = post(p)
                    for n_ in range(PER_HEAD):
                        if n_ == 0:
                            act.wait_ge(out_taken, (h * PER_HEAD + (U_HEAD - 1)).v)
                        unit(h * PER_HEAD + (U_HEAD + n_), pieces=stages[2 * n_:2 * n_ + 2])

                def mlp_in(j):
                    t = SPLIT[j]
                    if j in (0, EARLY):
                        act.wait_ge(quarter_done, 4 * U_OUT + (56 if j == 0 else 64))
                    nc.scalar.activation(act_hi[:, t, :], res[:, t, :], ACT.Copy, scale=sm[:, S_N2 + t:S_N2 + t + 1]
                                         ).then_inc(x_hi, 1)

                def split_mix(n_):
                    t = SPLIT[n_]
                    if n_ == 0:
                        act.wait_ge(quarter_done, 4 * U_OUT)
                    act.wait_ge(mix_ready, 2 * (t % HEADS) + 1 + (t < HEADS))
                    nc.scalar.activation(act_hi[:, t, :], res[:, t, :], ACT.Copy).then_inc(mix_hi, 1)

                head_steps(act, prologue, both)

                stages = post(Step(HEADS - 1))
                for n_ in range(EARLY):
                    split_mix(n_)
                    if n_ == 3:
                        split(Step(4 * U_OUT + 3))
                act.wait_ge(out_taken, U_OUT - 1)
                for r in range(4 * KT):
                    if r:
                        split(Step(4 * U_OUT + r + 3))
                    if r % 2 == 0 and r // 2 < len(stages) and stages[r // 2]:
                        stages[r // 2]()
                    if r == 2 * len(stages) - 1:
                        for n_ in range(EARLY, KT):
                            split_mix(n_)
                    for g in OUT_ENDS[r]:
                        if g >= KT:
                            j = g - KT
                            act.wait_ge(out_taken, U_OUT + g + 1)
                            if j >= 2:
                                act.wait_ge(x_acc, KT + j - 1)
                            nc.scalar.activation(tmp[j % 2][:], res[:, SPLIT[j], :], ACT.Square).then_inc(x_sq, 1)
                            if j < EARLY:
                                mlp_in(j)
                for j in range(EARLY, KT):
                    mlp_in(j)

                def hidden(t, k, parity):
                    act.wait_ge(up_relu, (t + 1).v)
                    nc.scalar.activation(hid_hi[:, parity, k, :], tmp[k % 2][:], ACT.Square).then_inc(up_hi, 1)

                act.wait_ge(kv_stored, 32 * HEADS)
                act.wait_ge(st_stored, 16 * HEADS)
                act.wait_ge(stored, 32)

                def up_units(u, t, parity, first):
                    for k in range(BLOCK):
                        unit(u + k)
                        if first and k == 0:
                            rsqrt(rstd, pp[:, 0:2, 0:HB], D_MODEL, norm_done, 2, rstd_ready)
                        hidden(t + k, k, parity)

                def down_units(u):
                    for k in range(BLOCK):
                        unit(u + k)

                up_units(Step(U_UP0), Step(0), 0, True)

                def step(b):
                    u = b * (2 * BLOCK) + U_FFN
                    up_units(u, (b + 1) * BLOCK, 1 - b.mod(2), False)
                    down_units(u + BLOCK)

                ffn_steps(act, step)
                down_units(Step(U_LAST))

            @block.vector
            def _(dve):
                links = [0]

                def link(ins):
                    links[0] += 1
                    ins.then_inc(dve_self, 1)
                    dve.wait_ge(dve_self, links[0])

                def split(q):
                    if q.reg is None and q.first >= QUARTERS:
                        return
                    slot = q.mod(4)
                    dve.wait_ge(hi_ready, (q + 1).v)
                    nc.vector.tensor_tensor(w_lo[:, slot, :], w_raw[:, slot, :], w_hi[:, slot, :].bitcast(f32),
                                            ALU.subtract).then_inc(lo_ready, 1)

                def x_tile(k):
                    dve.wait_ge(x_hi, k + 1)
                    nc.vector.scalar_tensor_tensor(out=act_lo[:, k, :], in0=res[:, k, :], scalar=sm[:, S_N1 + k:S_N1 + k + 1],
                                                   in1=act_hi[:, k, :].bitcast(f32), op0=ALU.mult, op1=ALU.subtract
                                                   ).then_inc(x_lo, 1)

                def x_add(k):
                    dve.wait_ge(x_sq, k + 1)
                    nc.vector.tensor_tensor(acc[:], acc[:], tmp[k % 2][:], ALU.add).then_inc(x_acc, 1)
                    dve.wait_ge(x_acc, k + 1)

                for k in range(KT):
                    if k % 4 == 0:
                        split(Step(k // 4))
                    x_tile(k)
                split(Step(4))
                split(Step(5))
                dve.wait_ge(consts_ready, N_CONSTS)
                for k in range(KT):
                    x_add(k)
                    if k == 5:
                        split(Step(6))
                dve.wait_ge(smalls_loaded, 16)
                link(nc.vector.tensor_scalar(qn8[:], sm[:, S_QN:S_QN + 1], DQK ** -0.5, None, ALU.mult))
                link(nc.vector.tensor_scalar(an8[:], sm[:, S_AN:S_AN + 1], 1.0 - LAM_INIT, None, ALU.mult))
                lq = sm[:, S_LQ:S_ALL].rearrange("p (a b d) -> p a b d", a=2, b=2)
                link(nc.vector.tensor_tensor(lam_p, lq[:, :, 0, :], lq[:, :, 1, :], ALU.mult))
                nc.vector.reduce_sum(lam4[:, 0:2], lam_p, axis=AX.X).then_inc(lam_sum, 1)
                dve.wait_ge(lam_exp, 1)
                link(nc.vector.scalar_tensor_tensor(out=neg_lam[:], in0=lam4[:, 3:4], scalar=-LAM_INIT, in1=lam4[:, 2:3],
                                                    op0=ALU.add, op1=ALU.subtract))
                link(nc.vector.tensor_copy(lam_sel[32:64, :], neg_lam[32:64, :]))

                def gates_evac():
                    dve.wait_ge(rstd_ready, 1)
                    nc.vector.tensor_tensor(two(gates[0][0:GR, :]), group(0)[0:GR], two(rstd[0:GR, :]), ALU.mult).then_inc(out_taken, 1)
                    dve.wait_ge(out_taken, 1)
                    nc.vector.tensor_scalar(gates[1][0:HEADS, :], gates[0][32:GR, :], sm[32:GR, S_BG:S_BG + 1], None,
                                            ALU.add).then_inc(gates_raw, 1)
                    link(nc.vector.tensor_scalar(gates[0][0:HEADS, :], gates[0][0:HEADS, :], sm[0:HEADS, S_BG:S_BG + 1], None, ALU.add))

                def gates_scan_stage():
                    z, b, g, M, m = (gates[i][0:HEADS, :] for i in (1, 3, 0, 4, 5))
                    dve.wait_ge(gates_lf, 1)
                    link(nc.vector.scalar_tensor_tensor(out=z, in0=z, scalar=0.0, in1=gates[2][0:HEADS, :],
                                                        op0=ALU.min, op1=ALU.subtract))
                    for c in range(NCH + 1):
                        lo, hi = c * P, min(T, (c + 1) * P)
                        last = nc.vector.tensor_tensor_scan(out=b[:, lo:hi], data0=z[:, lo:hi], data1=zero_row[:, lo:hi],
                                                            initial=0.0, op0=ALU.add, op1=ALU.add)
                    link(last)
                    link(nc.vector.tensor_tensor(g, g, b, ALU.subtract))
                    for c in range(NCH + 1):
                        lo, hi = c * P, min(T, (c + 1) * P)
                        prev = 0.0 if c == 0 else (m[:, lo - 1:lo] if c < NCH else sm[0:HEADS, S_M0:S_M0 + 1])
                        link(nc.vector.tensor_tensor_scan(out=M[:, lo:hi], data0=g[:, lo:hi], data1=g[:, lo:hi],
                                                          initial=prev, op0=ALU.max, op1=ALU.max))
                        link(nc.vector.tensor_tensor(m[:, lo:hi], b[:, lo:hi], M[:, lo:hi], ALU.add))
                        nc.vector.tensor_scalar(nm_end[:, c:c + 1], M[:, hi - 1:hi], -1.0, None, ALU.mult)
                    nc.vector.tensor_copy(m_end[:, 0:1], m[:, SEQ - 1:SEQ])
                    nc.vector.tensor_copy(m_end[:, 1:2], m[:, T - 1:T]).then_inc(gates_scan, 1)

                OUTS = {K_: k_raw, Q_: q_raw, V_: v_T, MV: mv_T, MO: mo_T}

                def evac(h, n_):
                    u = h * PER_HEAD + (U_HEAD + n_)
                    src = group(u.mod(2))
                    if n_ in (MK, MQ) and not (h.reg is None and h.first == 0):
                        dve.wait_ge(conv_ready, (h * 2).v)
                    if n_ == K_ and not (h.reg is None and h.first == 0):
                        dve.wait_ge(qk_ready, h.v)
                    dve.wait_ge(quarter_done, (u * 4 + 4).v)
                    if n_ == V_ and not (h.reg is None and h.first == 0):
                        dve.wait_ge(kv_stored, (h * 32).v)
                    if n_ in OUTS:
                        nc.vector.tensor_tensor(two(OUTS[n_][:]), src, two(rstd[:]), ALU.mult).then_inc(out_taken, 1)
                        return
                    dst, tile = (mk_u, HEADS) if n_ == MK else (mq_u, 0)
                    c = bass.ds((h + tile).v, 1)
                    nc.vector.tensor_copy(dst[:, CS:CS + PAD], sm[:, S_SC:S_LQ].rearrange("p (c j) -> p c j", j=PAD)[:, c, :]
                                          .rearrange("p a j -> p (a j)"))
                    nc.vector.tensor_tensor(dst[:, PAD:PAD + HB], src[:, 0, :], rstd[:, 0:HB], ALU.mult)
                    nc.vector.tensor_tensor(dst[:, PAD + HB:CS], src[:, 1, 0:SEQ - HB], rstd[:, HB:SEQ], ALU.mult)
                    nc.vector.tensor_tensor(dst[:, CS + PAD:UW], src[:, 1, SEQ - HB:HB], rstd[:, SEQ:T], ALU.mult).then_inc(out_taken, 1)

                def post(p):
                    k_links = [0]

                    def own(ins):
                        k_links[0] += 1
                        ins.then_inc(post_dve, 1)
                        dve.wait_ge(post_dve, (p * DVE_LINKS + k_links[0]).v)

                    def conv(u, out, tile):
                        wcol = sm[:, S_CW:S_CB].rearrange("p (c j) -> p c j", j=CONV_W)
                        for j in range(CONV_W):
                            w = wcol[:, bass.ds((p + tile).v, 1), j:j + 1].rearrange("p a j -> p (a j)")
                            if j == 0:
                                own(nc.vector.tensor_scalar(out[:], u[:, 0:CW], w, sm[:, bass.ds((p + (tile + S_CB)).v, 1)],
                                                            ALU.mult, ALU.add))
                            else:
                                i = nc.vector.scalar_tensor_tensor(out=out[:], in0=u[:, j:j + CW], scalar=w, in1=out[:],
                                                                   op0=ALU.mult, op1=ALU.add)
                                if j < CONV_W - 1:
                                    own(i)
                                else:
                                    i.then_inc(conv_ready, 1)
                        c = bass.ds((p + tile).v, 1)
                        nc.vector.tensor_copy(conv_sb[:, c, 0, :].rearrange("p a j -> p (a j)"), u[:, SEQ:CS])
                        nc.vector.tensor_copy(conv_sb[:, c, 1, :].rearrange("p a j -> p (a j)"), u[:, UW - PAD:UW])

                    def s0():
                        dve.wait_ge(out_taken, (p * PER_HEAD + (U_HEAD + PER_HEAD)).v)
                        conv(mk_u, mk_T, HEADS)
                        conv(mq_u, mq_T, 0)

                    def silu_one(e, n_):
                        dve.wait_ge(conv_exp, (p * 2 + n_).v)
                        nc.vector.tensor_scalar(e[:], e[:], 1.0, LN_MAX, ALU.add, ALU.min).then_inc(silu_den, 1)

                    def silu(e, out, scale, n_):
                        dve.wait_ge(silu_sig, (p * 2 + n_).v)
                        nc.vector.scalar_tensor_tensor(out=out[:, 0:SEQ], in0=out[:, 0:SEQ], scalar=scale, in1=e[:, 0:SEQ],
                                                       op0=ALU.mult, op1=ALU.mult)
                        return nc.vector.scalar_tensor_tensor(out=out[:, CS:CW], in0=out[:, CS:CW], scalar=scale,
                                                              in1=e[:, SEQ:T], op0=ALU.mult, op1=ALU.mult)

                    def s0b():
                        silu_one(tmp[2], 1)
                        silu_one(tmp[3], 2)
                        silu(tmp[2], mk_T, DK ** -0.5, 1)
                        silu(tmp[3], mq_T, 1.0, 2).then_inc(silu_ready, 1)

                    def s1():
                        dve.wait_ge(qk_rstd, (p + 1).v)
                        nc.vector.scalar_tensor_tensor(out=k_T[:], in0=k_raw[:], scalar=sm[:, S_KN:S_KN + 1], in1=tmp[0][:],
                                                       op0=ALU.mult, op1=ALU.mult)
                        nc.vector.scalar_tensor_tensor(out=kc_sb[:, PAST:], in0=k_raw[:, SEQ:T], scalar=sm[:, S_KN:S_KN + 1],
                                                       in1=tmp[0][:, SEQ:T], op0=ALU.mult, op1=ALU.mult)
                        for m in range(2):
                            h = slice(64 * m, 64 * m + 64)
                            nc.vector.scalar_tensor_tensor(out=q_pad[h, m, 0:SEQ], in0=q_raw[h, 0:SEQ], scalar=qn8[h, :],
                                                           in1=tmp[1][h, 0:SEQ], op0=ALU.mult, op1=ALU.mult)
                            last = nc.vector.scalar_tensor_tensor(out=q_s[h, m * DEC:(m + 1) * DEC], in0=q_raw[h, SEQ:T],
                                                                  scalar=qn8[h, :], in1=tmp[1][h, SEQ:T],
                                                                  op0=ALU.mult, op1=ALU.mult)
                        last.then_inc(qk_ready, 1)

                    def s2():
                        dve.wait_ge(tok_done, (p + 1).v)
                        nc.vector.tensor_copy(v_aug[:, 0:NCH, 0:DK], pp[:, 2, :].rearrange("p (c d) -> p c d", c=NCH)
                                              )
                        for c in range(NCH):
                            last = nc.vector.tensor_scalar(kw_tok[:, c, :], pp[:, 1, c * P:(c + 1) * P],
                                                           ws_col[:, c, bass.ds(p.v, 1)], None, ALU.mult)
                        last.then_inc(tok_dve, 1)
                        dve.wait_ge(rows_loaded, ((p + 1) * 48).v)
                        for c in range(NCH):
                            nc.vector.tensor_tensor(decay[:, c * P:(c + 1) * P], decay[:, c * P:(c + 1) * P], causal[:], ALU.add)
                        nc.vector.tensor_tensor(decay[:, SEQ:T], decay[:, SEQ:T], causal[:, 0:DEC], ALU.add).then_inc(decay_sum, 1)

                    def maxima(m):
                        dve.wait_ge(scores_done, (p * 2 + (m + 1)).v)
                        for i in range(NCH):
                            last = nc.vector.tensor_reduce(neg_max[:, m, i:i + 1], pp[:, i, 0:(i + 1) * P], axis=AX.X,
                                                           op=ALU.max, negate=True)
                        last.then_inc(max_ready, 1)

                    def s3():
                        maxima(0)

                    def s4():
                        maxima(1)
                        dve.wait_ge(probs_ready, (p * 2 + 2).v)
                        own(nc.vector.reciprocal(flat(inv[:]), flat(sums[:])))
                        own(nc.vector.tensor_scalar(inv[:, 1, :], inv[:, 1, :], neg_lam[:], None, ALU.mult))
                        for i in range(NCH):
                            s = slice(OFF[i], OFF[i] + (i + 1) * P)
                            last = nc.vector.tensor_scalar(prob[1][:, s], prob[1][:, s], inv[:, 1, i:i + 1], None, ALU.mult)
                        own(last)
                        for i in range(NCH):
                            s = slice(OFF[i], OFF[i] + (i + 1) * P)
                            last = nc.vector.scalar_tensor_tensor(out=prob[0][:, s], in0=prob[0][:, s], scalar=inv[:, 0, i:i + 1],
                                                                  in1=prob[1][:, s], op0=ALU.mult, op1=ALU.add)
                        last.then_inc(weights_ready, 1)

                    def s5():
                        dve.wait_ge(at_done, (p + 1).v)
                        dve.wait_ge(decay_ready, (p + 1).v)
                        nc.vector.tensor_copy(at[:, 1024:AW], pp[:, 2, 0:256])
                        nc.vector.tensor_tensor(decay[:, 0:SEQ], pp[:, 3, :], decay[:, 0:SEQ], ALU.mult)
                        nc.vector.tensor_tensor(decay[0:DEC, SEQ:T], pp[0:DEC, 2, 256:256 + DEC], decay[0:DEC, SEQ:T],
                                                ALU.mult).then_inc(pt_ready, 1)

                    def s6():
                        dve.wait_ge(pv_done, (p + 1).v)
                        dve.wait_ge(c0_loaded, ((p + 1) * 16).v)
                        if not (p.reg is None and p.first == 0):
                            dve.wait_ge(st_stored, (p * 16).v)
                        own(nc.vector.tensor_copy(state[:, 0, :], pp[:, 1, 0:DK + 1]))
                        for c in range(1, NCH):
                            src = pp[:, 1, c * (DK + 1):(c + 1) * (DK + 1)] if c < 3 else pp[:, 2, 0:DK + 1]
                            own(nc.vector.scalar_tensor_tensor(out=state[:, c, :], in0=state[:, c - 1, :],
                                                               scalar=wi_row[:, (c + 1) * P - 1:(c + 1) * P], in1=src,
                                                               op0=ALU.mult, op1=ALU.add))
                        nc.vector.scalar_tensor_tensor(out=state[:, NCH, :], in0=c0_sb[:], scalar=wi_row[:, T - 1:T],
                                                       in1=pp[:, 2, DK + 1:2 * (DK + 1)], op0=ALU.mult, op1=ALU.add)
                        for c in range(NCH):
                            n_col = state[:, c, DK:DK + 1] if c < NCH - 1 else c0_sb[:, DK:DK + 1]
                            nc.vector.tensor_scalar(n_b[:, c, :], ones[:], n_col, None, ALU.mult)
                        nc.vector.tensor_tensor(mq_T[:, P:SEQ], mq_T[:, P:SEQ], wi_row[:, P:SEQ], ALU.mult)
                        nc.vector.tensor_tensor(mq_T[:, CS:CW], mq_T[:, CS:CW], wi_row[:, SEQ:T], ALU.mult).then_inc(state_ready, 1)

                    def s7():
                        dve.wait_ge(s_scores_done, (p + 1).v)
                        nc.vector.tensor_reduce(s_max[:], pp[0:64, 0:3, 0:SB], axis=AX.XY, op=ALU.max,
                                                negate=True).then_inc(s_max_ready, 1)
                        dve.wait_ge(s_exp_ready, (p + 1).v)
                        own(nc.vector.reciprocal(s_inv[:], s_sum[:]))
                        own(nc.vector.tensor_tensor(s_inv[:], s_inv[:], lam_sel[:], ALU.mult))
                        nc.vector.tensor_scalar(s_prob, s_prob, s_inv[:], None, ALU.mult).then_inc(s_probs_ready, 1)

                    def s8():
                        dve.wait_ge(den_abs, (p + 1).v)
                        own(nc.vector.tensor_tensor(tmp[2][:], tmp[2][:], en_row[:], ALU.max))
                        own(nc.vector.reciprocal(tmp[2][:], tmp[2][:]))
                        nc.vector.tensor_tensor(tmp[3][:, 0:SEQ], pp[:, 0, :], tmp[2][:, 0:SEQ], ALU.mult)
                        nc.vector.tensor_tensor(tmp[3][:, SEQ:T], pp[:, 1, 0:DEC], tmp[2][:, SEQ:T], ALU.mult).then_inc(h_ready, 1)
                        dve.wait_ge(o_exp, (p + 1).v)
                        nc.vector.tensor_scalar(mo_T[:], mo_T[:], 1.0, LN_MAX, ALU.add, ALU.min).then_inc(o_den, 1)

                    def s10():
                        dve.wait_ge(o_sig, (p + 1).v)
                        dve.wait_ge(ml_rstd, (p + 1).v)
                        own(nc.vector.scalar_tensor_tensor(out=tmp[3][:], in0=tmp[3][:], scalar=sm[:, S_MN:S_MN + 1],
                                                           in1=tmp[0][:], op0=ALU.mult, op1=ALU.mult))
                        nc.vector.tensor_tensor(res[:, bass.ds((p + HEADS).v, 1), :].rearrange("p a b -> p (a b)"),
                                                tmp[3][:], mo_T[:], ALU.mult).then_inc(mix_ready, 1)

                    def s12():
                        dve.wait_ge(att_rstd, (p + 1).v)
                        nc.vector.scalar_tensor_tensor(out=res[:, bass.ds(p.v, 1), :].rearrange("p a b -> p (a b)"),
                                                       in0=att_T, scalar=an8[:], in1=tmp[1][:],
                                                       op0=ALU.mult, op1=ALU.mult).then_inc(mix_ready, 1)
                        assert k_links[0] == DVE_LINKS, k_links

                    return [s0, s0b, s1, s2, s3, s4, s5, s6, s7, s8, None, s10, None, s12]

                def unit(u, pieces=(None, None)):
                    q = u * 4
                    split(q + 3)
                    if pieces[0]:
                        pieces[0]()
                    split(q + 4)
                    split(q + 5)
                    if pieces[1]:
                        pieces[1]()
                    split(q + 6)

                def prologue(h):
                    for n_ in range(PER_HEAD):
                        unit(Step(U_HEAD + n_), pieces=(None, gates_scan_stage if n_ == 1 else None))
                        if n_ == 0:
                            gates_evac()
                        evac(h, n_)

                def both(h, p):
                    stages = post(p)
                    for n_ in range(PER_HEAD):
                        unit(h * PER_HEAD + (U_HEAD + n_), pieces=stages[2 * n_:2 * n_ + 2])
                        evac(h, n_)

                def split_mix(n_):
                    t = SPLIT[n_]
                    dve.wait_ge(mix_hi, n_ + 1)
                    nc.vector.tensor_tensor(act_lo[:, t, :], res[:, t, :], act_hi[:, t, :].bitcast(f32),
                                            ALU.subtract).then_inc(mix_lo, 1)

                def mlp_in(j):
                    t = SPLIT[j]
                    dve.wait_ge(x_hi, KT + j + 1)
                    nc.vector.scalar_tensor_tensor(out=act_lo[:, t, :], in0=res[:, t, :], scalar=sm[:, S_N2 + t:S_N2 + t + 1],
                                                   in1=act_hi[:, t, :].bitcast(f32), op0=ALU.mult, op1=ALU.subtract
                                                   ).then_inc(x_lo, 1)

                head_steps(dve, prologue, both)

                stages = post(Step(HEADS - 1))
                for n_ in range(EARLY):
                    split_mix(n_)
                    if n_ == 3:
                        split(Step(4 * U_OUT + 3))
                for r in range(4 * KT):
                    if r:
                        split(Step(4 * U_OUT + r + 3))
                    if r % 2 == 0 and r // 2 < len(stages) and stages[r // 2]:
                        stages[r // 2]()
                    if r == 2 * len(stages) - 1:
                        for n_ in range(EARLY, KT):
                            split_mix(n_)
                        nc.vector.memset(acc[:], 0.0).then_inc(acc_clear, 1)
                    for g in OUT_ENDS[r]:
                        t = SPLIT[g % KT]
                        dve.wait_ge(quarter_done, 4 * U_OUT + r + 1)
                        if g < KT:
                            dve.wait_ge(x_reloaded[t], 16)
                        else:
                            dve.wait_ge(out_taken, U_OUT + g - KT + 1)
                        nc.vector.tensor_tensor(two(res[:, t, :]), group((U_OUT + g) % 2), two(res[:, t, :]), ALU.add
                                                ).then_inc(out_taken, 1)
                        if KT < g <= KT + EARLY:
                            mlp_in(g - KT - 1)
                for j in range(EARLY, KT):
                    mlp_in(j)

                def hidden_out(u, t, k):
                    dve.wait_ge(quarter_done, (u * 4 + 4).v)
                    if not (t.reg is None and t.first < 2):
                        dve.wait_ge(up_hi, (t + (-1)).v)
                        dve.wait_ge(up_sq, (t + (-1)).v)
                    nc.vector.scalar_tensor_tensor(out=two(tmp[k % 2][:]), in0=group((k + UP_SLOT) % 2), scalar=0.0,
                                                   in1=two(rstd[:]), op0=ALU.max, op1=ALU.mult).then_inc(up_relu, 1)

                def hidden_lo(t, k, parity):
                    dve.wait_ge(up_hi, (t + 1).v)
                    dve.wait_ge(up_sq, (t + 1).v)
                    nc.vector.tensor_tensor(hid_lo[:, parity, k, :], tmp[2 + k % 2][:], hid_hi[:, parity, k, :].bitcast(f32),
                                            ALU.subtract).then_inc(up_lo, 1)

                def up_units(u, t, parity, first):
                    for k in range(BLOCK):
                        if first:
                            unit(u + k)
                        else:
                            split((u + k) * 4 + 3)
                            if k:
                                hidden_lo(t + (k - 1), k - 1, parity)
                            for q in (4, 5, 6):
                                split((u + k) * 4 + q)
                        if first and k == 0:
                            dve.wait_ge(rstd_ready, 2)
                        hidden_out(u + k, t + k, k)
                        if first:
                            hidden_lo(t + k, k, parity)

                def down_units(b, u, before=None):
                    for k in range(BLOCK):
                        for q in range(4):
                            m = 4 * k + q
                            split((u + k) * 4 + (q + 3))
                            if m == 0 and before:
                                before()
                            dve.wait_ge(quarter_done, ((u + k) * 4 + (q + 1)).v)
                            r = two(res[:, m, :])
                            nc.vector.tensor_tensor(r, group(2 + m % 2), r, ALU.add).then_inc(down_taken, 1)

                up_units(Step(U_UP0), Step(0), 0, True)

                def step(b):
                    u = b * (2 * BLOCK) + U_FFN
                    t = (b + 1) * BLOCK
                    up_units(u, t, 1 - b.mod(2), False)
                    down_units(b, u + BLOCK, lambda: hidden_lo(t + (BLOCK - 1), BLOCK - 1, 1 - b.mod(2)))

                ffn_steps(dve, step)
                down_units(Step(NBLK - 1), Step(U_LAST))


def kernel(x_prompt, x_sample, cache_k, cache_v, state_C, state_n, state_m, state_conv,
           norm1_w, w_in, conv_w, conv_b, b_gates, q_norm_w, k_norm_w, lambda_qk,
           att_norm_w, ml_norm_w, w_out, norm2_w, w_up, w_down):
    import numpy as np
    import concourse.bacc as bacc
    from concourse.bass_utils import run_bass_kernel_spmd

    def host(a):
        return np.asarray(a)

    x = np.concatenate([host(x_prompt)[0], host(x_sample)[0]], axis=0)
    xT = x.T.reshape(KT, P, T).transpose(1, 0, 2)

    def quarters(w):
        k, n = w.shape
        return w.reshape(k // QW, 4, P, n // P, P).transpose(3, 0, 2, 1, 4).reshape(n // P, k // QW, P, QW)

    w = host(w_in)[0]
    gate_w = np.zeros((D_MODEL, P), w.dtype)
    gate_w[:, 0:HEADS] = w[:, ROUNDS * P:ROUNDS * P + HEADS]
    gate_w[:, 32:GR] = w[:, ROUNDS * P + HEADS:]
    w_heads = quarters(w[:, 0:ROUNDS * P])
    order = [base * HEADS + h for h in range(HEADS) for base in (4, 3, 1, 0, 2, 5, 6)]
    w_u = host(w_up)[0].reshape(KT, P, D_FF)[SPLIT].reshape(D_MODEL, D_FF)
    up = quarters(w_u).reshape(NBLK, 4 * BLOCK, P, QW)
    down = quarters(host(w_down)[0]).transpose(1, 0, 2, 3)
    w_o = host(w_out)[0].reshape(KT, P, KT, P)[SPLIT][:, :, SPLIT]
    w_o = np.stack([w_o[kk, :, g % KT] for g, kk, _, _ in OUT_ORDER])
    w_o = w_o.reshape(-1, 4, P, P).transpose(0, 2, 1, 3).reshape(-1, P, QW)
    parts = [quarters(gate_w).reshape(-1, P, QW), w_heads[order].reshape(-1, P, QW),
             w_o, up[0]]
    for b in range(NBLK - 1):
        parts += [up[b + 1], down[b]]
    parts.append(down[NBLK - 1])
    wstream = np.concatenate(parts, axis=0)

    smalls = np.zeros((P, S_ALL), x.dtype)
    smalls[:, S_N1:S_N2] = host(norm1_w)[0].reshape(KT, P).T
    smalls[:, S_N2:S_CW] = host(norm2_w)[0].reshape(KT, P).T
    smalls[:, S_CW:S_CB] = host(conv_w)[0].reshape(CONV_W, 2 * HEADS, P).transpose(2, 1, 0).reshape(P, -1)
    smalls[:, S_CB:S_QN] = host(conv_b)[0].reshape(2 * HEADS, P).T
    smalls[:, S_QN] = np.concatenate([host(q_norm_w)[0]] * 2)
    smalls[:, S_KN] = np.concatenate([host(k_norm_w)[0]] * 2)
    smalls[:, S_AN] = host(att_norm_w)[0]
    smalls[:, S_MN] = host(ml_norm_w)[0]
    smalls[0:HEADS, S_BG] = host(b_gates)[0, 0:HEADS]
    smalls[32:GR, S_BG] = host(b_gates)[0, HEADS:]
    smalls[0:HEADS, S_M0] = host(state_m)[0, 0]
    smalls[:, S_SC:S_LQ] = host(state_conv)[0, 0].reshape(PAD, 2 * HEADS, P).transpose(2, 1, 0).reshape(P, -1)
    smalls[:, S_LQ:S_ALL] = host(lambda_qk)[0].reshape(1, -1)

    kcT = host(cache_k)[0, 0].transpose(1, 2, 0)
    vcl = host(cache_v)[0, 0].reshape(PAST // P, P, HEADS, DK).transpose(2, 1, 0, 3)
    c0 = np.concatenate([host(state_C)[0, 0], host(state_n)[0, 0][:, :, None]], axis=2)

    nc = bacc.Bacc("TRN2", target_bir_lowering=False, num_devices=1)
    f32 = mybir.dt.float32
    arrays = {}

    def given(name, a):
        arrays[name] = np.ascontiguousarray(a)
        return nc.dram_tensor(name, a.shape, f32, kind="ExternalInput").ap()

    def wanted(name, shape):
        return nc.dram_tensor(name, shape, f32, kind="ExternalOutput").ap()

    build(nc, given("in_xT", xT), given("in_wstream", wstream), given("in_smalls", smalls), given("in_kcT", kcT),
          given("in_vc", vcl), given("in_c0", c0),
          wanted("out_yT", (P, KT, T)), wanted("out_k", (HEADS, P, T)), wanted("out_v", (HEADS, P, T)),
          wanted("out_st", (HEADS, 2, P, DK + 1)), wanted("out_m", (HEADS, 2)),
          wanted("out_conv", (P, 2 * HEADS, 2, PAD)))
    r = run_bass_kernel_spmd(nc, [arrays], core_ids=[0]).results[0]

    y = r["out_yT"].transpose(2, 1, 0).reshape(T, D_MODEL)
    k = r["out_k"].transpose(2, 0, 1)
    v = r["out_v"].transpose(2, 0, 1)
    st, m = r["out_st"], r["out_m"]
    conv = r["out_conv"].transpose(2, 3, 1, 0).reshape(2, PAD, 2 * HEADS * P)

    def side(s):
        t = slice(0, SEQ) if s == 0 else slice(SEQ, T)
        return (k[None, None, t], v[None, None, t], st[None, None, :, s, :, 0:DK], st[None, None, :, s, :, DK],
                m[None, None, :, s], conv[None, None, s])

    return tuple(np.ascontiguousarray(a) for a in (y[None, 0:SEQ], y[None, SEQ:], *side(0), *side(1)))
```

```python
from contextlib import ExitStack

import concourse.bass as bass
from concourse import mybir

D_MODEL, SEQ, DEC, PAST = 2048, 512, 32, 1024
HEADS, DK, DQK = 8, 128, 64
D_FF = 4 * D_MODEL
CONV_W = 4
EPS = 1e-6
LAM_INIT = 0.2
P = 128
T = SEQ + DEC
HB = T // 2
KT = D_MODEL // P
NCH = SEQ // P
PER_HEAD = 7
MK, MQ, K_, Q_, V_, MV, MO = range(7)
ROUNDS = HEADS * PER_HEAD
BLOCK = 4
NBLK = D_FF // P // BLOCK
EARLY = KT - 2
TWICE = 10
OUT_ORDER = ([(g, kk, kk == 0, kk == EARLY - 1) for g in range(TWICE) for kk in range(EARLY)]
             + [(g, kk, kk == 0, kk == KT - 1) for g in range(TWICE, KT) for kk in range(KT)]
             + [(KT + g, kk, kk == EARLY, kk == KT - 1) for g in range(TWICE) for kk in range(EARLY, KT)])
OUT_MAIN = (len(OUT_ORDER) - TWICE * (KT - EARLY)) // 4
OUT_SHIFT = 4
OUT_ENDS = [[g for i, (g, _, _, end) in enumerate(OUT_ORDER) if end and i // 4 == r] for r in range(4 * KT)]
U_GATES = 0
U_HEAD = 1
U_OUT = U_HEAD + ROUNDS
U_UP0 = U_OUT + KT
U_FFN = U_UP0 + BLOCK
U_LAST = U_FFN + 2 * BLOCK * (NBLK - 1)
UNITS = U_LAST + BLOCK
QW = 4 * P
QUARTERS = 4 * UNITS
PAD = CONV_W - 1
UW = T + 2 * PAD
CW = UW - PAD
CS = SEQ + PAD
SPLIT = [t for h in range(HEADS) for t in (h, HEADS + h)]
MLP_TILES = SPLIT[TWICE:EARLY] + SPLIT[:TWICE] + SPLIT[EARLY:]
OFF = [0, 128, 384, 768]
AW = 1280
SAMPLE_KQ = 256 + P
ATO = {0: 0, 1: 512, 3: 896, 2: 1024}
SB = (PAST + DEC) // 3
BIG = 1e30
LN_MAX = 2.0 ** 63
GR = 40

S_N1 = 0
S_N2 = S_N1 + KT
S_CW = S_N2 + KT
S_CB = S_CW + 2 * HEADS * CONV_W
S_QN = S_CB + 2 * HEADS
S_KN = S_QN + 1
S_AN = S_KN + 1
S_MN = S_AN + 1
S_BG = S_MN + 1
S_M0 = S_BG + 1
S_SC = S_M0 + 1
S_LQ = S_SC + 2 * HEADS * PAD
S_ALL = S_LQ + 4 * DQK

ACT_LINKS = 7
N_CONSTS = 23
BETWEEN = (2, 5, 9, 13)
LAST_BETWEEN = (11, 13)
UP_SLOT = U_UP0 % 2
DVE_LINKS = 21


class Step:

    def __init__(self, first, per=0, reg=None):
        self.first, self.per, self.reg = first, per, reg

    def __add__(self, n):
        return Step(self.first + n, self.per, self.reg)

    def __mul__(self, n):
        return Step(self.first * n, self.per * n, self.reg)

    def mod(self, n):
        assert self.per % n == 0
        return self.first % n

    @property
    def v(self):
        return self.first if self.reg is None else self.reg * self.per + self.first


def build(nc, xT, wstream, smalls, kcT, vc, c0, yT, k_out, v_out, st_out, m_out, conv_out):
    f32, f32r, bf16 = mybir.dt.float32, mybir.dt.float32r, mybir.dt.bfloat16
    ALU, ACT, AX = mybir.AluOpType, mybir.ActivationFunctionType, mybir.AxisListType
    ctx = ExitStack()
    with ctx:
        def sb(name, shape, dt=f32):
            return ctx.enter_context(nc.sbuf_tensor(name, shape, dt))

        def sem(name):
            return ctx.enter_context(nc.semaphore(name))

        res = sb("res", [P, KT, T])
        act_hi = sb("act_hi", [P, KT, T], f32r)
        act_lo = sb("act_lo", [P, KT, T], f32r)
        w_raw = sb("w_raw", [P, 4, QW])
        w_hi = sb("w_hi", [P, 4, QW], f32r)
        w_lo = sb("w_lo", [P, 4, QW], f32r)
        sm = sb("sm", [P, S_ALL])
        ident = sb("ident", [P, P])
        ones_r = sb("ones_r", [P, P], f32r)
        ones = ones_r[:].bitcast(f32)
        rstd = sb("rstd", [P, T])
        with nc.sbuf_tensor("sq_lo", [P, 2, T], f32r) as sq_lo:
            pass
        tmp = [sb(f"tmp{i}", [P, T]) for i in range(4)]
        acc = tmp[3]

        eps_col = sb("eps_col", [P, 1])
        psum = ctx.enter_context(nc.psum_tensor("psum", [P, 8, 512], f32))

        def group(slot):
            return psum[:, 2 * slot:2 * slot + 2, 0:HB]

        def out_slot(g):
            return (U_OUT + g) % 2 if g < KT else (2, 3, 1, 0)[g % 4]

        pp = psum[:, 4:8, :]

        rows_dram = nc.dram_tensor("gate_rows", [3, HEADS, T], f32, kind="Internal").ap()

        raw_loaded = [sem(f"raw_loaded{i}") for i in range(4)]
        hi_ready, lo_ready = sem("hi_ready"), sem("lo_ready")
        quarter_done = sem("quarter_done")
        out_taken = sem("out_taken")
        smalls_loaded, consts_ready = sem("smalls_loaded"), sem("consts_ready")
        x_loaded = [sem(f"x_loaded{i}") for i in range(8)]
        x_hi, x_sq, x_lo, x_acc = sem("x_hi"), sem("x_sq"), sem("x_lo"), sem("x_acc")
        norm_done, rstd_ready, acc_clear = sem("norm_done"), sem("rstd_ready"), sem("acc_clear")
        stored = sem("stored")

        def flat(ap):
            return ap.rearrange("p a b -> p (a b)")

        def two(ap):
            return ap.rearrange("p (a b) -> p a b", a=2)

        phase_a = ExitStack()
        with phase_a:
            def sa(name, shape, dt=f32):
                return phase_a.enter_context(nc.sbuf_tensor(name, shape, dt))

            k_raw, q_raw, v_T = sa("k_raw", [P, T]), sa("q_raw", [P, T]), sa("v_T", [P, T])
            mk_u, mq_u = sa("mk_u", [P, UW]), sa("mq_u", [P, UW])
            mv_T, mo_T = sa("mv_T", [P, T]), sa("mo_T", [P, T])
            k_T = sa("k_T", [P, T])
            k_split = sa("k_split", [P, 2, SEQ], f32r)
            q_s = sa("q_s", [P, 2 * DEC])
            mk_T, mq_T = sa("mk_T", [P, CW]), sa("mq_T", [P, CW])
            v_tok, kw_tok = sa("v_tok", [P, NCH + 1, DK]), sa("kw_tok", [P, NCH + 1, DK])
            v_aug = sa("v_aug", [P, NCH + 1, DK + 1])
            with nc.sbuf_tensor("big_r", [P, 3, AW], f32r) as big_r:
                pass
            big = sa("big", [P, 3, AW])
            prob = [big[:, 0, :], big[:, 1, :]]
            at = big[:, 2, :]
            q_hi = big_r[:, 2, 0:2 * SEQ].rearrange("p (m t) -> p m t", m=2)
            q_lo = big_r[:, 1, 0:SEQ]
            k_sq_hi, q_sq_hi, sq_hi = (big_r[:, i, 0:T] for i in (1, 2, 0))
            s_prob = big[0:64, 1, 0:PAST + DEC]
            s_pt = big[:, 2, 0:9 * 64]
            decay = sa("decay", [P, T])
            wi_row, en_row = sa("wi_row", [P, T]), sa("en_row", [P, T])
            squares = (tmp[0], tmp[1], decay, wi_row)
            state = sa("state", [P, NCH + 1, DK + 1])
            c0_sb = sa("c0_sb", [P, DK + 1])
            den, den_hi, den_lo = big[:, 0, 0:T], big_r[:, 2, 0:T], big_r[:, 0, 0:T]
            kc_sb, vc_sb = sa("kc_sb", [P, PAST + DEC]), sa("vc_sb", [P, PAST // P, DK])
            att_T = mk_T[:, 0:T]
            s_out = big[0:64, 1, PAST + DEC:PAST + DEC + DK]
            neg_max, sums, inv = sa("neg_max", [P, 2, NCH]), sa("sums", [P, 2, NCH]), sa("inv", [P, 2, NCH])
            s_max, s_sum, s_inv = sa("s_max", [64, 1]), sa("s_sum", [64, 1]), sa("s_inv", [64, 1])
            blk_r = sa("blk_r", [P, P], f32r)
            comb = sa("comb", [64, DEC])
            causal = sa("causal", [P, P])
            late_row, early_q = sa("late_row", [1, P], bf16), sa("early_q", [1, P], bf16)
            g_col, ws_col = sa("g_col", [P, NCH + 1, HEADS]), sa("ws_col", [P, NCH + 1, HEADS])
            conv_sb = sa("conv_sb", [P, 2 * HEADS, 2, PAD])
            qn8, an8, lam4, neg_lam, lam_sel = (sa("qn8", [P, 1]), sa("an8", [P, 1]), sa("lam4", [P, 4]),
                                                sa("neg_lam", [P, 1]), sa("lam_sel", [64, 1]))
            lam_p = kw_tok[:, 0, :].rearrange("p (a d) -> p a d", a=2)
            m_end, nm_end = sa("m_end", [HEADS, 2]), sa("nm_end", [HEADS, NCH + 1])
            gates = [flat(big[:, :, :])[0:GR, i * T:(i + 1) * T] for i in range(7)]
            zero_row = tmp[2][0:HEADS, :]

            gate_taken, gates_raw, gates_lf, gates_scan = sem("gate_taken"), sem("gates_raw"), sem("gates_lf"), sem("gates_scan")
            gates_exp, cols_done, cols_ready = sem("gates_exp"), sem("cols_done"), sem("cols_ready")
            rows_stored, rows_loaded, cache_loaded, c0_loaded = (sem("rows_stored"), sem("rows_loaded"),
                                                                 sem("cache_loaded"), sem("c0_loaded"))
            lam_sum, lam_exp = sem("lam_sum"), sem("lam_exp")
            kv_stored, st_stored = sem("kv_stored"), sem("st_stored")
            qk_hi, qk_lo = sem("qk_hi"), sem("qk_lo")
            qk_sq_lo, h_sq_lo, att_sq_lo = sem("qk_sq_lo"), sem("h_sq_lo"), sem("att_sq_lo")
            sq_ready, conv_ready, conv_exp = sem("sq_ready"), sem("conv_ready"), sem("conv_exp")
            qk_ms_done, qk_rstd, qk_ready, silu_ready = sem("qk_ms_done"), sem("qk_rstd"), sem("qk_ready"), sem("silu_ready")
            tok_done, tok_act, decay_sum, decay_ready = (sem("tok_done"), sem("tok_act"),
                                                                  sem("decay_sum"), sem("decay_ready"))
            scores_done, max_ready, probs_ready, weights_ready = (sem("scores_done"), sem("max_ready"),
                                                                  sem("probs_ready"), sem("weights_ready"))
            at_done, at_ready, pt_ready, pv_done = sem("at_done"), sem("at_ready"), sem("pt_ready"), sem("pv_done")
            att_ready, state_ready, s_scores_done, s_max_ready = (sem("att_ready"), sem("state_ready"),
                                                                  sem("s_scores_done"), sem("s_max_ready"))
            den_abs, den_ready = sem("den_abs"), sem("den_ready")
            den_hi_ready, den_lo_ready = sem("den_hi_ready"), sem("den_lo_ready")
            s_exp_ready, s_probs_ready, h_done, h_ready, h_sq = (sem("s_exp_ready"), sem("s_probs_ready"), sem("h_done"),
                                                                 sem("h_ready"), sem("h_sq"))
            s_pt_done, s_pt_ready, s_pv_done, s_out_ready, ml_rstd, o_exp = (
                sem("s_pt_done"), sem("s_pt_ready"), sem("s_pv_done"), sem("s_out_ready"), sem("ml_rstd"), sem("o_exp"))
            silu_den, silu_sig, o_den, o_sig = sem("silu_den"), sem("silu_sig"), sem("o_den"), sem("o_sig")
            comb_done, s_att_ready, att_sq, att_ms_done, att_rstd = (sem("comb_done"), sem("s_att_ready"), sem("att_sq"),
                                                                     sem("att_ms_done"), sem("att_rstd"))
            mix_ready, mix_hi, mix_lo, x_reloaded = sem("mix_ready"), sem("mix_hi"), sem("mix_lo"), [sem(f"x_reloaded{t}") for t in range(KT)]
            dve_self, act_self, post_self, post_dve = sem("dve_self"), sem("act_self"), sem("post_self"), sem("post_dve")
            up_relu, up_hi, up_sq, up_lo, down_taken = sem("up_relu"), sem("up_hi"), sem("up_sq"), sem("up_lo"), sem("down_taken")


            def head_steps(eng, prologue, both):
                prologue(Step(0))
                both(Step(1), Step(0))
                with eng.Fori(0, HEADS // 2 - 1) as i:
                    both(Step(2, 2, i), Step(1, 2, i))
                    both(Step(3, 2, i), Step(2, 2, i))

            def ffn_steps(eng, step):
                with eng.Fori(0, NBLK // 2 - 1) as i:
                    step(Step(0, 2, i))
                    step(Step(1, 2, i))
                step(Step(NBLK - 2))


            phase_a.close()
            hid_hi = sb("hid_hi", [P, 2, BLOCK, T], f32r)
            hid_lo = sb("hid_lo", [P, 2, BLOCK, T], f32r)
            block = ctx.enter_context(nc.Block())

            @block.sync
            def _(sp):
                for q in range(4):
                    sp.dma_start(w_raw[:, q, :], wstream[q]).then_inc(raw_loaded[q], 16)
                    for i in (2, 3, 4, 5, 6, 7)[2 * q:2 * q + 2]:
                        sp.dma_start(res[:, 2 * i:2 * i + 2, :], xT[:, 2 * i:2 * i + 2, :]).then_inc(x_loaded[i], 16)
                with sp.Fori(0, QUARTERS // 4 - 1) as i:
                    for q in range(4):
                        sp.wait_ge(lo_ready, i * 4 + (q + 1))
                        sp.dma_start(w_raw[:, q, :],
                                     wstream[bass.ds(i * 4 + (q + 4), 1)].rearrange("a p n -> p (a n)")
                                     ).then_inc(raw_loaded[q], 16)

            @block.gpsimd
            def _(pool):
                n = [0]

                def const(ins):
                    n[0] += 1
                    ins.then_inc(consts_ready, 1)
                    pool.wait_ge(consts_ready, n[0])

                const(nc.gpsimd.memset(ones, 1.0))
                const(nc.gpsimd.memset(ident[:], 0.0))
                const(nc.gpsimd.memset(blk_r[:].bitcast(f32), 1.0))
                const(nc.gpsimd.memset(comb[:], 0.0))
                const(nc.gpsimd.memset(causal[:], 0.0))
                const(nc.gpsimd.memset(early_q[:], 0.0))
                const(nc.gpsimd.memset(late_row[:], 0.0))
                const(nc.gpsimd.memset(q_s[:], 0.0))
                const(nc.gpsimd.memset(mk_u[:, 0:PAD], 0.0))
                const(nc.gpsimd.memset(mq_u[:, 0:PAD], 0.0))
                const(nc.gpsimd.memset(v_aug[:, :, DK:DK + 1], 1.0))
                const(nc.gpsimd.memset(acc[:], 0.0))
                const(nc.gpsimd.memset(zero_row, 0.0))
                const(nc.gpsimd.memset(lam_sel[0:32, :], 1.0))
                const(nc.gpsimd.memset(eps_col[:], EPS))
                const(nc.gpsimd.affine_select(out=ident[:], in_=ident[:], compare_op=ALU.not_equal, fill=1.0,
                                              base=0, pattern=[[-1, P]], channel_multiplier=1))
                const(nc.gpsimd.memset(blk_r[0:64, 64:128].bitcast(f32), 0.0))
                const(nc.gpsimd.memset(blk_r[64:128, 0:64].bitcast(f32), 0.0))
                const(nc.gpsimd.affine_select(out=causal[:], in_=causal[:], compare_op=ALU.is_ge, fill=BIG,
                                              base=0, pattern=[[1, P]], channel_multiplier=-1))
                const(nc.gpsimd.affine_select(out=comb[:], in_=comb[:], compare_op=ALU.not_equal, fill=1.0,
                                              base=0, pattern=[[-1, DEC]], channel_multiplier=1))
                const(nc.gpsimd.memset(early_q[:, 0:64], 1.0))
                const(nc.gpsimd.memset(late_row[:, 64:128], -BIG))
                const(nc.gpsimd.affine_select(out=comb[:], in_=comb[:], compare_op=ALU.not_equal, fill=1.0,
                                              base=-DEC, pattern=[[-1, DEC]], channel_multiplier=1))
                assert n[0] == N_CONSTS, n

                def dma_after_waits(dst, src, done):
                    pool.wait_ge(smalls_loaded, 16)
                    pool.dma_start(dst, src).then_inc(done, 16)

                def load_head(p, first):
                    if not first:
                        pool.wait_ge(s_scores_done, p.v)
                    dma_after_waits(kc_sb[:, 0:PAST], kcT[bass.ds(p.v, 1)].rearrange("a p n -> p (a n)"), cache_loaded)
                    if not first:
                        pool.wait_ge(smalls_loaded, 16)
                        pool.wait_ge(s_pv_done, p.v)
                        pool.wait_ge(h_done, p.v)
                        pool.wait_ge(h_ready, p.v)
                    pool.dma_start(vc_sb[:], vc[bass.ds(p.v, 1)].rearrange("a p t n -> p (a t) n")).then_inc(cache_loaded, 16)
                    pool.dma_start(c0_sb[:], c0[bass.ds(p.v, 1)].rearrange("a p n -> p (a n)")).then_inc(c0_loaded, 16)
                    for r, row in enumerate((decay, wi_row, en_row)):
                        pool.dma_start(row[:], rows_dram[r, bass.ds(p.v, 1), :].to_broadcast([P, T])).then_inc(rows_loaded, 16)

                def store_head(p):
                    pool.wait_ge(qk_ready, (p + 1).v)
                    dma_after_waits(k_out[bass.ds(p.v, 1)].rearrange("a p n -> p (a n)"), k_T[:], kv_stored)
                    pool.dma_start(v_out[bass.ds(p.v, 1)].rearrange("a p n -> p (a n)"), v_T[:]).then_inc(kv_stored, 16)
                    pool.wait_ge(state_ready, (p + 1).v)
                    dma_after_waits(st_out[bass.ds(p.v, 1)].rearrange("a s p n -> p (a s) n"),
                                    state[:, NCH - 1:NCH + 1, :], st_stored)

                def prologue(h):
                    pool.wait_ge(gates_exp, 1)
                    pool.dma_start(rows_dram[0], gates[4][0:HEADS, :]).then_inc(rows_stored, 16)
                    pool.dma_start(rows_dram[1], gates[6][0:HEADS, :]).then_inc(rows_stored, 16)
                    pool.dma_start(rows_dram[2], tmp[0][0:HEADS, :]).then_inc(rows_stored, 16)
                    pool.dma_start(m_out, m_end[:]).then_inc(stored, 16)
                    pool.wait_ge(rows_stored, 48)
                    load_head(Step(0), True)

                def both(h, p):
                    store_head(p)
                    load_head(h, False)

                def reload(n_):
                    pool.wait_ge(mix_lo, n_ + 1)
                    pool.dma_start(res[:, SPLIT[n_], :], xT[:, SPLIT[n_], :]).then_inc(x_reloaded[SPLIT[n_]], 16)

                head_steps(pool, prologue, both)
                for n_ in range(EARLY):
                    reload(n_)
                store_head(Step(HEADS - 1))
                for n_ in range(EARLY, KT):
                    reload(n_)
                for j in range(KT):
                    if j == 0:
                        pool.wait_ge(acc_clear, 1)
                    pool.wait_ge(x_sq, KT + j + 1)
                    nc.gpsimd.tensor_tensor(acc[:], acc[:], tmp[j % 3][:], ALU.add).then_inc(x_acc, 1)
                    pool.wait_ge(x_acc, KT + j + 1)
                pool.dma_start(conv_out, conv_sb[:]).then_inc(stored, 16)

                def square(t, slot):
                    pool.wait_ge(up_relu, (t + 1).v)
                    if not (t.reg is None and t.first < 2):
                        pool.wait_ge(up_lo, (t + (-1)).v)
                    nc.gpsimd.tensor_tensor(tmp[2 + slot][:], tmp[slot][:], tmp[slot][:], ALU.mult).then_inc(up_sq, 1)

                for t in range(BLOCK):
                    square(Step(t), t % 2)

                def step(b):
                    for t in range(BLOCK):
                        square((b + 1) * BLOCK + t, t % 2)

                ffn_steps(pool, step)
                pool.wait_ge(kv_stored, 16 * 2 * HEADS)
                pool.wait_ge(st_stored, 16 * HEADS)
                for m in range(KT):
                    pool.wait_ge(down_taken, (NBLK - 1) * KT + m + 1)
                    pool.dma_start(yT[:, m, :], res[:, m, :]).then_inc(stored, 16)
                pool.wait_ge(stored, 16 * (KT + 2))

            @block.tensor
            def _(pe):
                def passes(out, w_slot, col, m, x_hi_t, x_lo_t, start, stop):
                    for n_, (w, x) in enumerate(((w_hi, x_hi_t), (w_hi, x_lo_t), (w_lo, x_hi_t))):
                        for half in range(2):
                            last = nc.tensor.matmul(out[0:m, half, :], w[:, w_slot, col:col + m],
                                                    x[:, half * HB:(half + 1) * HB],
                                                    start=start and n_ == 0, stop=stop and n_ == 2)
                    return last

                def unit(u, m=P, x_ready=None, pieces=(None, None), taken=True, slot=None):
                    out = group(u.mod(2) if slot is None else slot)
                    if taken:
                        pe.wait_ge(out_taken, (u + (-1)).v)
                    for q in range(4):
                        pe.wait_ge(lo_ready, (u * 4 + (q + 1)).v)
                        for k in range(4):
                            t = 4 * q + k
                            if x_ready is not None:
                                pe.wait_ge(x_ready, t + 1)
                            last = passes(out, q, k * P, m, act_hi[:, t, :], act_lo[:, t, :], t == 0, t == KT - 1)
                        last.then_inc(quarter_done, 1)
                        if q == 1 and pieces[0]:
                            pieces[0]()
                        if q == 3 and pieces[1]:
                            pieces[1]()

                def sum_rows(w, parts, bank):
                    for half in range(2):
                        for n_, src in enumerate(parts):
                            last = nc.tensor.matmul(pp[:, bank + half, 0:HB], w, src[:, half * HB:(half + 1) * HB],
                                                    start=n_ == 0, stop=n_ == len(parts) - 1)
                    return last

                def post(p):
                    def ms_qk():
                        pe.wait_ge(qk_sq_lo, (p + 1).v)
                        sum_rows(blk_r[:], (k_sq_hi, sq_lo[:, 0, :]), 0)
                        sum_rows(blk_r[:], (q_sq_hi, sq_lo[:, 1, :]), 2).then_inc(qk_ms_done, 1)

                    def to_tokens():
                        pe.wait_ge(silu_ready, (p + 1).v)
                        pe.wait_ge(qk_rstd, (p + 1).v)
                        for n_, (src, at0) in enumerate(((v_T, SEQ), (mk_T, CS), (mv_T, SEQ))):
                            for c in range(NCH):
                                nc.tensor.transpose(pp[:, n_, c * P:(c + 1) * P], src[:, c * P:(c + 1) * P], ident[:])
                            last = nc.tensor.transpose(pp[0:DEC, 3, n_ * P:(n_ + 1) * P], src[:, at0:at0 + DEC], ident[:])
                        last.then_inc(tok_done, 1)

                    def scores(m):
                        def piece():
                            if m == 0:
                                pe.wait_ge(qk_lo, (p + 1).v)
                                pe.wait_ge(tok_act, (p + 1).v)
                            else:
                                pe.wait_ge(probs_ready, (p * 2 + 1).v)
                            for i in range(NCH):
                                w = (i + 1) * P
                                h = slice(64 * m, 64 * m + 64)
                                n = max(w, 2 * P)
                                nc.tensor.matmul(pp[:, i, 0:n], q_hi[:, m, i * P:(i + 1) * P], k_split[:, m, 0:n],
                                                 start=True, stop=False, skip_group_check=True)
                                nc.tensor.matmul(pp[:, i, 0:n], q_lo[h, i * P:(i + 1) * P], k_split[h, m, 0:n],
                                                 start=False, stop=False, skip_group_check=True)
                                last = nc.tensor.matmul(pp[:, i, w - P:w], early_q[:], late_row[:],
                                                        start=False, stop=True, skip_group_check=True)
                            last.then_inc(scores_done, 1)
                        return piece

                    def transpose_weights():
                        pe.wait_ge(probs_ready, (p * 2 + 2).v)
                        for c in range(NCH):
                            nc.tensor.matmul(pp[:, 3, c * P:(c + 1) * P], mk_T[:, c * P:(c + 1) * P],
                                             mq_T[:, c * P:(c + 1) * P], start=True, stop=True)
                        nc.tensor.matmul(pp[0:DEC, 2, SAMPLE_KQ - P:SAMPLE_KQ], mk_T[:, CS:CW], mq_T[:, CW - P:CW],
                                         start=True, stop=True)
                        pe.wait_ge(weights_ready, (p + 1).v)
                        for j in range(NCH):
                            for i in range(j, NCH):
                                o = ATO[j] + (i - j) * P
                                last = nc.tensor.transpose(pp[:, o // 512, o % 512:o % 512 + P],
                                                           prob[0][:, OFF[i] + j * P:OFF[i] + (j + 1) * P], ident[:])
                        last.then_inc(at_done, 1)

                    def values():
                        pe.wait_ge(at_ready, (p + 1).v)
                        pe.wait_ge(pt_ready, (p + 1).v)
                        for j in range(NCH):
                            nc.tensor.matmul(pp[:, 0, j * P:SEQ], v_tok[:, j, :], at[:, ATO[j]:ATO[j] + SEQ - j * P],
                                             start=(j == 0), stop=(j == NCH - 1))
                        for c in range(NCH):
                            o = c * (DK + 1) if c < 3 else 512
                            nc.tensor.matmul(pp[:, 1 + o // 512, o % 512:o % 512 + DK + 1], kw_tok[:, c, :], v_aug[:, c, :],
                                             start=True, stop=True)
                        nc.tensor.matmul(pp[:, 2, DK + 1:2 * (DK + 1)], kw_tok[0:DEC, NCH, :], v_aug[0:DEC, NCH, :],
                                         start=True, stop=True).then_inc(pv_done, 1)

                    def sample_scores():
                        pe.wait_ge(att_ready, (p + 1).v)
                        pe.wait_ge(state_ready, (p + 1).v)
                        pe.wait_ge(cache_loaded, ((p + 1) * 32).v)
                        for b in range(3):
                            last = nc.tensor.matmul(pp[0:64, b, 0:SB], q_s[:], kc_sb[:, b * SB:(b + 1) * SB],
                                                    start=True, stop=True)
                        last.then_inc(s_scores_done, 1)

                    def mlstm():
                        pe.wait_ge(s_exp_ready, (p + 1).v)
                        for c in range(NCH):
                            o = pp[:, 0, c * P:(c + 1) * P]
                            if c:
                                nc.tensor.matmul(o, state[:, c - 1, 0:DK], mq_T[:, c * P:(c + 1) * P], start=True, stop=False)
                            nc.tensor.matmul(o, v_aug[:, c, 0:DK], decay[:, c * P:(c + 1) * P], start=(c == 0), stop=True)
                        o = pp[:, 1, 0:P]
                        nc.tensor.matmul(o, c0_sb[:, 0:DK], mq_T[:, CW - P:CW], start=True, stop=False)
                        nc.tensor.matmul(o, v_aug[0:DEC, NCH, 0:DK], decay[0:DEC, T - P:T], start=False, stop=True)
                        pe.wait_ge(den_lo_ready, (p + 1).v)
                        sum_rows(ones_r[:], (den_hi, den_lo), 2).then_inc(h_done, 1)

                    def sample_transpose():
                        pe.wait_ge(consts_ready, N_CONSTS)
                        pe.wait_ge(s_probs_ready, (p + 1).v)
                        pe.wait_ge(den_abs, (p + 1).v)
                        for j in range(PAST // P):
                            nc.tensor.transpose(pp[:, 2, j * 64:(j + 1) * 64], s_prob[:, j * P:(j + 1) * P], ident[0:64, 0:64])
                        nc.tensor.transpose(pp[0:DEC, 3, 0:64], s_prob[:, PAST:PAST + DEC], ident[0:64, 0:64]).then_inc(s_pt_done, 1)

                    def sample_values():
                        pe.wait_ge(s_pt_ready, (p + 1).v)
                        pe.wait_ge(h_sq_lo, (p + 1).v)
                        for j in range(PAST // P):
                            nc.tensor.matmul(pp[0:64, 2, 0:DK], s_pt[:, j * 64:(j + 1) * 64], vc_sb[:, j, :],
                                             start=(j == 0), stop=False)
                        nc.tensor.matmul(pp[0:64, 2, 0:DK], s_pt[0:DEC, 512:576], v_tok[0:DEC, NCH, :], start=False, stop=True)
                        sum_rows(ones_r[:], (sq_hi, sq_lo[:, 0, :]), 0).then_inc(s_pv_done, 1)

                    def sample_combine():
                        pe.wait_ge(s_out_ready, (p + 1).v)
                        nc.tensor.matmul(pp[:, 3, 0:DEC], s_out, comb[:], start=True, stop=True).then_inc(comb_done, 1)

                    def ms_att():
                        pe.wait_ge(att_sq_lo, (p + 1).v)
                        pe.wait_ge(ml_rstd, (p + 1).v)
                        sum_rows(ones_r[:], (sq_hi, sq_lo[:, 1, :]), 0).then_inc(att_ms_done, 1)

                    return [None, ms_qk, to_tokens, scores(0), scores(1), transpose_weights, values, sample_scores,
                            mlstm, sample_transpose, sample_values, sample_combine, ms_att, None]

                def norm_sum():
                    pe.wait_ge(consts_ready, N_CONSTS)
                    pe.wait_ge(x_acc, KT)
                    sum_rows(ones, (acc,), 0).then_inc(norm_done, 1)

                def gate_columns():
                    pe.wait_ge(gates_exp, 1)
                    pe.wait_ge(rstd_ready, 1)
                    for n_, row in enumerate((gates[0], tmp[1])):
                        for c in range(NCH + 1):
                            w = min(P, T - c * P)
                            last = nc.tensor.transpose(pp[0:w, n_, c * 8:c * 8 + 8], row[0:HEADS, c * P:c * P + w],
                                                       ident[0:HEADS, 0:HEADS])
                    last.then_inc(cols_done, 1)

                unit(Step(U_GATES), GR, x_lo, taken=False, slot=3)

                def prologue(h):
                    for n_ in range(PER_HEAD):
                        unit(Step(U_HEAD + n_), taken=n_ > 1,
                             pieces=(norm_sum if n_ == 1 else None, gate_columns if n_ == 4 else None))

                def both(h, p):
                    pieces = post(p)
                    for n_ in range(PER_HEAD):
                        unit(h * PER_HEAD + (U_HEAD + n_), pieces=pieces[2 * n_:2 * n_ + 2])

                head_steps(pe, prologue, both)

                pieces = post(Step(HEADS - 1))
                for idx, (g, kk, first, end) in enumerate(OUT_ORDER):
                    r = idx // 4
                    if idx % 4 == 0:
                        pe.wait_ge(lo_ready, 4 * U_OUT + r + 1)
                    if first:
                        out = group(out_slot(g))
                        if g in (KT, KT + 1):
                            pe.wait_ge(att_rstd, HEADS)
                        else:
                            pe.wait_ge(out_taken, U_OUT + g - (1 if g < KT else 3))
                    if g == 0 or kk >= EARLY and g in (TWICE, KT):
                        pe.wait_ge(mix_lo, kk + 1)
                    t = SPLIT[kk]
                    last = passes(out, r % 4, (idx % 4) * P, P, act_hi[:, t, :], act_lo[:, t, :], first, end)
                    if idx % 4 == 3:
                        last.then_inc(quarter_done, 1)
                        i, odd = divmod(r - OUT_SHIFT, 2)
                        if odd and 0 <= i < len(pieces) and pieces[i]:
                            pieces[i]()

                def norm2_sum():
                    pe.wait_ge(x_acc, 2 * KT)
                    sum_rows(ones, (acc,), 0).then_inc(norm_done, 1)


                def down(b, u, parity, first):
                    for m in range(KT):
                        out = group(2 + m % 2)
                        if not (first and m < 2):
                            pe.wait_ge(down_taken, (b * KT + (m - 1)).v)
                        pe.wait_ge(lo_ready, (u * 4 + (m + 1)).v)
                        if m == 0:
                            pe.wait_ge(up_lo, (b * BLOCK + BLOCK).v)
                        for k in range(BLOCK):
                            last = passes(out, m % 4, k * P, P, hid_hi[:, parity, k, :], hid_lo[:, parity, k, :],
                                          k == 0, k == BLOCK - 1)
                        last.then_inc(quarter_done, 1)

                def step(b, first=False):
                    u = b * (2 * BLOCK) + U_FFN
                    for t in range(BLOCK):
                        unit_up(u + t, (b + 1) * BLOCK + t)
                    down(b, u + BLOCK, b.mod(2), first)

                def unit_up(u, t, x_ready=False, piece=None):
                    out = group((t.mod(2) + UP_SLOT) % 2)
                    if t.reg is None and t.first < 2:
                        pe.wait_ge(out_taken, U_OUT + KT + TWICE - 3 + t.first)
                    else:
                        pe.wait_ge(up_relu, (t + (-1)).v)
                    for q in range(4):
                        pe.wait_ge(lo_ready, (u * 4 + (q + 1)).v)
                        for k in range(4):
                            kk = 4 * q + k
                            if x_ready:
                                pe.wait_ge(x_lo, KT + kk + 1)
                            tile = MLP_TILES[kk]
                            last = passes(out, q, k * P, P, act_hi[:, tile, :], act_lo[:, tile, :], kk == 0, kk == KT - 1)
                        last.then_inc(quarter_done, 1)
                    if piece:
                        piece()

                unit_up(Step(U_UP0), Step(0), True, norm2_sum)
                for t in range(1, BLOCK):
                    unit_up(Step(U_UP0 + t), Step(t))
                pe.wait_ge(rstd_ready, 2)

                step(Step(0), first=True)
                step(Step(1))
                with pe.Fori(1, NBLK // 2 - 1) as i:
                    step(Step(0, 2, i))
                    step(Step(1, 2, i))
                step(Step(NBLK - 2))
                down(Step(NBLK - 1), Step(U_LAST), (NBLK - 1) % 2, False)

            @block.scalar
            def _(act):
                def split(q):
                    if q.reg is None and q.first >= QUARTERS:
                        return
                    slot = q.mod(4)
                    act.wait_ge(raw_loaded[slot], (Step(q.first // 4, q.per // 4, q.reg) * 16 + 16).v)
                    if not (q.reg is None and q.first < 4):
                        act.wait_ge(quarter_done, (q + (-3)).v)
                    nc.scalar.activation(w_hi[:, slot, :], w_raw[:, slot, :], ACT.Copy).then_inc(hi_ready, 1)

                def rsqrt(out, src, n_, wait_sem, wait_value, done):
                    act.wait_ge(wait_sem, wait_value)
                    nc.scalar.activation(two(out[:]), src, ACT.Ln, scale=1.0 / n_, bias=eps_ap).then_inc(act_self, 1)
                    self_n[0] = self_n[0] + 1
                    act.wait_ge(act_self, self_n[0].v)
                    nc.scalar.activation(out[:], out[:], ACT.Exp, scale=-0.5).then_inc(done, 1)

                eps_ap = eps_col[:]
                self_n = [Step(0)]

                def x_tile(k):
                    act.wait_ge(x_loaded[k // 2], 16)
                    nc.scalar.activation(act_hi[:, k, :], res[:, k, :], ACT.Copy, scale=sm[:, S_N1 + k:S_N1 + k + 1]
                                         ).then_inc(x_hi, 1)

                def x_square(k):
                    if k >= 4:
                        act.wait_ge(x_acc, k - 3)
                    nc.scalar.activation(squares[k % 4][:], res[:, k, :], ACT.Square).then_inc(x_sq, 1)

                act.dma_start(sm[:], smalls).then_inc(smalls_loaded, 16)
                for i in range(2):
                    act.dma_start(res[:, 2 * i:2 * i + 2, :], xT[:, 2 * i:2 * i + 2, :]).then_inc(x_loaded[i], 16)
                nc.scalar.preload_act_table_set("natural_log_exp_and_others")
                act.wait_ge(smalls_loaded, 16)
                for k in range(KT):
                    if k % 4 == 0:
                        split(Step(k // 4))
                    x_tile(k)
                split(Step(4))
                split(Step(5))
                for k in range(KT):
                    x_square(k)
                    if k in BETWEEN:
                        split(Step(6 + BETWEEN.index(k)))
                split(Step(10))
                act.wait_ge(lam_sum, 1)
                nc.scalar.activation(lam4[:, 2:4], lam4[:, 0:2], ACT.Exp).then_inc(lam_exp, 1)

                def first_rstd():
                    act.wait_ge(consts_ready, N_CONSTS)
                    rsqrt(rstd, pp[:, 0:2, 0:HB], D_MODEL, norm_done, 1, rstd_ready)

                def gates_exp_stage():
                    act.wait_ge(gates_raw, 1)
                    nc.scalar.activation(gates[2][0:HEADS, :], gates[1][0:HEADS, :], ACT.Abs).then_inc(act_self, 1)
                    self_n[0] = self_n[0] + 1
                    act.wait_ge(act_self, self_n[0].v)
                    nc.scalar.activation(gates[2][0:HEADS, :], gates[2][0:HEADS, :], ACT.Exp, scale=-1.0).then_inc(act_self, 1)
                    self_n[0] = self_n[0] + 1
                    act.wait_ge(act_self, self_n[0].v)
                    nc.scalar.activation(gates[2][0:HEADS, :], gates[2][0:HEADS, :], ACT.Ln, bias=1.0).then_inc(gates_lf, 1)

                def gates_weights_stage():
                    act.wait_ge(gates_scan, 1)
                    g, M, m, wi = gates[0], gates[4], gates[5], gates[6]
                    for c in range(NCH + 1):
                        lo, hi = c * P, min(T, (c + 1) * P)
                        prev = 0.0 if c == 0 else (m[0:HEADS, lo - 1:lo] if c < NCH else sm[0:HEADS, S_M0:S_M0 + 1])
                        nc.scalar.activation(wi[0:HEADS, lo:hi], M[0:HEADS, lo:hi], ACT.Exp, scale=-1.0, bias=prev)
                        nc.scalar.activation(tmp[1][0:HEADS, lo:hi], g[0:HEADS, lo:hi], ACT.Exp, bias=nm_end[:, c:c + 1])
                    nc.scalar.activation(tmp[0][0:HEADS, :], m[0:HEADS, :], ACT.Exp, scale=-1.0).then_inc(gates_exp, 1)

                def post(p):
                    k_self = [0]

                    def own(ins):
                        k_self[0] += 1
                        ins.then_inc(post_self, 1)
                        act.wait_ge(post_self, (p * ACT_LINKS + k_self[0]).v)

                    def inverse(row, given, value, done):
                        act.wait_ge(given, value)
                        own(nc.scalar.activation(row, row, ACT.Ln))
                        nc.scalar.activation(row, row, ACT.Exp, scale=-1.0).then_inc(done, 1)

                    def s0():
                        if not (p.reg is None and p.first == 0):
                            act.wait_ge(mix_ready, (p * 2).v)
                        for src, whole, high in ((k_raw, tmp[0], k_sq_hi), (q_raw, tmp[1], q_sq_hi)):
                            nc.scalar.activation(whole[:], src[:], ACT.Square)
                            last = nc.scalar.activation(high, src[:], ACT.Square)
                        last.then_inc(sq_ready, 1)
                        act.wait_ge(conv_ready, (p * 2 + 1).v)
                        nc.scalar.activation(tmp[2][:, 0:SEQ], mk_T[:, 0:SEQ], ACT.Exp, scale=-1.0)
                        nc.scalar.activation(tmp[2][:, SEQ:T], mk_T[:, CS:CW], ACT.Exp, scale=-1.0).then_inc(conv_exp, 1)
                        act.wait_ge(conv_ready, (p * 2 + 2).v)
                        nc.scalar.activation(tmp[3][:, 0:SEQ], mq_T[:, 0:SEQ], ACT.Exp, scale=-1.0)
                        nc.scalar.activation(tmp[3][:, SEQ:T], mq_T[:, CS:CW], ACT.Exp, scale=-1.0).then_inc(conv_exp, 1)

                    def s0b():
                        for n_ in range(2):
                            inverse(tmp[2 + n_][:], silu_den, (p * 2 + (n_ + 1)).v, silu_sig)

                    def s1():
                        act.wait_ge(qk_ms_done, (p + 1).v)
                        nc.scalar.activation(two(tmp[0][:]), pp[:, 0:2, 0:HB], ACT.Ln, scale=1.0 / DQK, bias=eps_ap)
                        own(nc.scalar.activation(two(tmp[1][:]), pp[:, 2:4, 0:HB], ACT.Ln, scale=1.0 / DQK, bias=eps_ap))
                        nc.scalar.activation(tmp[0][:], tmp[0][:], ACT.Exp, scale=-0.5)
                        nc.scalar.activation(tmp[1][:], tmp[1][:], ACT.Exp, scale=-0.5).then_inc(qk_rstd, 1)
                        act.wait_ge(qk_ready, (p + 1).v)
                        for m in range(2):
                            h = slice(64 * m, 64 * m + 64)
                            nc.scalar.activation(q_hi[h, m, :], q_raw[h, 0:SEQ], ACT.Copy)
                            last = nc.scalar.activation(k_split[h, m, :], k_T[h, 0:SEQ], ACT.Copy)
                        last.then_inc(qk_hi, 1)

                    def s2():
                        act.wait_ge(tok_done, (p + 1).v)
                        nc.scalar.activation(flat(v_tok[:, 0:NCH, :]), pp[:, 0, :], ACT.Copy)
                        for c in range(NCH):
                            nc.scalar.activation(kw_tok[:, c, :], pp[:, 1, c * P:(c + 1) * P], ACT.Copy,
                                                 scale=ws_col[:, c, bass.ds(p.v, 1)])
                        nc.scalar.activation(v_aug[:, 0:NCH, 0:DK], pp[:, 2, :].rearrange("p (c d) -> p c d", c=NCH), ACT.Copy)
                        nc.scalar.activation(v_tok[0:DEC, NCH, :], pp[0:DEC, 3, 0:P], ACT.Copy)
                        nc.scalar.activation(v_aug[0:DEC, NCH, 0:DK], pp[0:DEC, 3, 2 * P:3 * P], ACT.Copy)
                        nc.scalar.activation(kw_tok[0:DEC, NCH, :], pp[0:DEC, 3, P:2 * P], ACT.Copy,
                                             scale=ws_col[0:DEC, NCH, bass.ds(p.v, 1)]).then_inc(tok_act, 1)

                    def decay_exps():
                        act.wait_ge(decay_sum, (p + 1).v)
                        for c in range(NCH):
                            nc.scalar.activation(decay[:, c * P:(c + 1) * P], decay[:, c * P:(c + 1) * P], ACT.Exp,
                                                 scale=-1.0, bias=g_col[:, c, bass.ds(p.v, 1)])
                        nc.scalar.activation(decay[0:DEC, SEQ:T], decay[0:DEC, SEQ:T], ACT.Exp, scale=-1.0,
                                             bias=g_col[0:DEC, NCH, bass.ds(p.v, 1)]).then_inc(decay_ready, 1)

                    def soft(m):
                        def stage():
                            if m == 0:
                                decay_exps()
                            act.wait_ge(max_ready, (p * 2 + (m + 1)).v)
                            for i in range(NCH):
                                w = (i + 1) * P
                                last = nc.scalar.activation(prob[m][:, OFF[i]:OFF[i] + w], pp[:, i, 0:w], ACT.Exp,
                                                            bias=neg_max[:, m, i:i + 1], accum_out=sums[:, m, i:i + 1])
                            last.then_inc(probs_ready, 1)
                        return stage

                    def s5():
                        act.wait_ge(at_done, (p + 1).v)
                        nc.scalar.activation(at[:, 0:1024], flat(pp[:, 0:2, :]), ACT.Copy).then_inc(at_ready, 1)

                    def s6():
                        act.wait_ge(pv_done, (p + 1).v)
                        nc.scalar.activation(att_T[:, 0:SEQ], pp[:, 0, :], ACT.Copy).then_inc(att_ready, 1)

                    def s7():
                        act.wait_ge(den_ready, (p + 1).v)
                        nc.scalar.activation(den_hi, den, ACT.Copy).then_inc(den_hi_ready, 1)
                        act.wait_ge(s_max_ready, (p + 1).v)
                        nc.scalar.activation(s_prob.rearrange("p (b n) -> p b n", b=3), pp[0:64, 0:3, 0:SB], ACT.Exp, bias=s_max[:],
                                             accum_out=s_sum[:]).then_inc(s_exp_ready, 1)

                    def s8():
                        act.wait_ge(h_done, (p + 1).v)
                        nc.scalar.activation(two(tmp[2][:]), pp[:, 2:4, 0:HB], ACT.Abs).then_inc(den_abs, 1)
                        act.wait_ge(h_ready, (p + 1).v)
                        nc.scalar.activation(tmp[0][:], tmp[3][:], ACT.Square)
                        nc.scalar.activation(sq_hi, tmp[3][:], ACT.Square).then_inc(h_sq, 1)
                        act.wait_ge(out_taken, (p * PER_HEAD + (U_HEAD + PER_HEAD)).v)
                        nc.scalar.activation(mo_T[:], mo_T[:], ACT.Exp, scale=-1.0).then_inc(o_exp, 1)

                    def s9():
                        act.wait_ge(s_pt_done, (p + 1).v)
                        nc.scalar.activation(s_pt[:, 0:512], pp[:, 2, :], ACT.Copy)
                        nc.scalar.activation(s_pt[0:DEC, 512:576], pp[0:DEC, 3, 0:64], ACT.Copy).then_inc(s_pt_ready, 1)
                        inverse(mo_T[:], o_den, (p + 1).v, o_sig)

                    def s10():
                        act.wait_ge(s_pv_done, (p + 1).v)
                        nc.scalar.activation(s_out, pp[0:64, 2, 0:DK], ACT.Copy).then_inc(s_out_ready, 1)
                        own(nc.scalar.activation(two(tmp[0][:]), pp[:, 0:2, 0:HB], ACT.Ln, scale=1.0 / DK, bias=eps_ap))
                        nc.scalar.activation(tmp[0][:], tmp[0][:], ACT.Exp, scale=-0.5).then_inc(ml_rstd, 1)

                    def s11():
                        act.wait_ge(comb_done, (p + 1).v)
                        own(nc.scalar.activation(att_T[:, SEQ:T], pp[:, 3, 0:DEC], ACT.Copy))
                        nc.scalar.activation(tmp[1][:], att_T, ACT.Square)
                        nc.scalar.activation(sq_hi, att_T, ACT.Square).then_inc(att_sq, 1)

                    def s12():
                        act.wait_ge(att_ms_done, (p + 1).v)
                        own(nc.scalar.activation(two(tmp[1][:]), pp[:, 0:2, 0:HB], ACT.Ln, scale=1.0 / DK, bias=eps_ap))
                        nc.scalar.activation(tmp[1][:], tmp[1][:], ACT.Exp, scale=-0.5).then_inc(att_rstd, 1)
                        assert k_self[0] == ACT_LINKS, k_self

                    return [s0, s0b, s1, s2, soft(0), soft(1), s5, s6, s7, s8, s9, s10, s11, s12]

                def unit(u, pieces=(None, None), begun=False):
                    q = u * 4
                    if not begun:
                        split(q + 3)
                        if pieces[0]:
                            pieces[0]()
                        split(q + 4)
                    split(q + 5)
                    if pieces[1]:
                        pieces[1]()
                    split(q + 6)

                def prologue(h):
                    for n_ in range(PER_HEAD):
                        if n_:
                            unit(Step(U_HEAD + n_), {1: (None, first_rstd), 2: (gates_exp_stage, None),
                                                     3: (gates_weights_stage, None)}.get(n_, (None, None)))
                        if n_ == 5:
                            act.wait_ge(cols_done, 1)
                            nc.scalar.activation(flat(g_col[:, 0:NCH, :]), pp[:, 0, 0:32], ACT.Copy)
                            nc.scalar.activation(g_col[0:DEC, NCH, :], pp[0:DEC, 0, 32:40], ACT.Copy)
                            nc.scalar.activation(flat(ws_col[:, 0:NCH, :]), pp[:, 1, 0:32], ACT.Copy)
                            nc.scalar.activation(ws_col[0:DEC, NCH, :], pp[0:DEC, 1, 32:40], ACT.Copy).then_inc(cols_ready, 1)
                    act.wait_ge(rows_stored, 48)

                def both(h, p):
                    stages = post(p)
                    for n_ in range(PER_HEAD):
                        if n_ == 0:
                            act.wait_ge(out_taken, (h * PER_HEAD + (U_HEAD - 1)).v)
                        unit(h * PER_HEAD + (U_HEAD + n_), pieces=stages[2 * n_:2 * n_ + 2])

                def mlp_in(j):
                    t = MLP_TILES[j]
                    if j in (0, EARLY):
                        act.wait_ge(quarter_done, 4 * U_OUT + (OUT_MAIN if j == 0 else 4 * KT))
                    nc.scalar.activation(act_hi[:, t, :], res[:, t, :], ACT.Copy, scale=sm[:, S_N2 + t:S_N2 + t + 1]
                                         ).then_inc(x_hi, 1)

                def split_mix(n_):
                    t = SPLIT[n_]
                    if n_ < EARLY:
                        act.wait_ge(quarter_done, 4 * U_OUT - 3 + t // 4)
                    act.wait_ge(mix_ready, 2 * (t % HEADS) + 1 + (t < HEADS))
                    nc.scalar.activation(act_hi[:, t, :], res[:, t, :], ACT.Copy).then_inc(mix_hi, 1)

                head_steps(act, prologue, both)

                stages = post(Step(HEADS - 1))
                for n_ in range(EARLY):
                    split_mix(n_)
                    if n_ == 3:
                        split(Step(4 * U_OUT + 3))
                act.wait_ge(out_taken, U_OUT - 1)
                for r in range(4 * KT):
                    if 0 < r <= OUT_MAIN:
                        split(Step(4 * U_OUT + r + 3))
                    if OUT_MAIN <= r < 4 * KT - 1:
                        split(Step(4 * U_OUT + r + 4))
                    i, odd = divmod(r - OUT_SHIFT, 2)
                    if not odd and 0 <= i < len(stages) and stages[i]:
                        stages[i]()
                    if r == OUT_SHIFT + 2 * len(stages) - 1:
                        for n_ in range(EARLY, KT):
                            split_mix(n_)
                    for g in OUT_ENDS[r]:
                        if g >= TWICE:
                            j = g - TWICE
                            act.wait_ge(out_taken, U_OUT + g + 1)
                            if j >= 3:
                                act.wait_ge(x_acc, KT + j - 2)
                            nc.scalar.activation(tmp[j % 3][:], res[:, SPLIT[g % KT], :], ACT.Square).then_inc(x_sq, 1)
                            if g >= KT:
                                mlp_in(g - KT)
                for j in range(TWICE, KT):
                    mlp_in(j)
                    if j in LAST_BETWEEN:
                        split(Step(4 * U_UP0 + 3 + LAST_BETWEEN.index(j)))

                def hidden(t, k, parity):
                    act.wait_ge(up_relu, (t + 1).v)
                    nc.scalar.activation(hid_hi[:, parity, k, :], tmp[k % 2][:], ACT.Square).then_inc(up_hi, 1)

                act.wait_ge(kv_stored, 32 * HEADS)
                act.wait_ge(st_stored, 16 * HEADS)
                act.wait_ge(stored, 32)

                def up_units(u, t, parity, first):
                    for k in range(BLOCK):
                        unit(u + k, begun=first and k == 0)
                        if first and k == 0:
                            rsqrt(rstd, pp[:, 0:2, 0:HB], D_MODEL, norm_done, 2, rstd_ready)
                        hidden(t + k, k, parity)

                def down_units(u):
                    for k in range(BLOCK):
                        unit(u + k)

                up_units(Step(U_UP0), Step(0), 0, True)

                def step(b):
                    u = b * (2 * BLOCK) + U_FFN
                    up_units(u, (b + 1) * BLOCK, 1 - b.mod(2), False)
                    down_units(u + BLOCK)

                ffn_steps(act, step)
                down_units(Step(U_LAST))

            @block.vector
            def _(dve):
                links = [0]

                def link(ins):
                    links[0] += 1
                    ins.then_inc(dve_self, 1)
                    dve.wait_ge(dve_self, links[0])

                def split(q):
                    if q.reg is None and q.first >= QUARTERS:
                        return
                    slot = q.mod(4)
                    dve.wait_ge(hi_ready, (q + 1).v)
                    nc.vector.tensor_tensor(w_lo[:, slot, :], w_raw[:, slot, :], w_hi[:, slot, :].bitcast(f32),
                                            ALU.subtract).then_inc(lo_ready, 1)

                def x_tile(k):
                    dve.wait_ge(x_hi, k + 1)
                    nc.vector.scalar_tensor_tensor(out=act_lo[:, k, :], in0=res[:, k, :], scalar=sm[:, S_N1 + k:S_N1 + k + 1],
                                                   in1=act_hi[:, k, :].bitcast(f32), op0=ALU.mult, op1=ALU.subtract
                                                   ).then_inc(x_lo, 1)

                def x_add(k):
                    dve.wait_ge(x_sq, k + 1)
                    nc.vector.tensor_tensor(acc[:], acc[:], squares[k % 4][:], ALU.add).then_inc(x_acc, 1)
                    dve.wait_ge(x_acc, k + 1)

                for k in range(KT):
                    if k % 4 == 0:
                        split(Step(k // 4))
                    x_tile(k)
                split(Step(4))
                split(Step(5))
                dve.wait_ge(consts_ready, N_CONSTS)
                for k in range(KT):
                    x_add(k)
                    if k in BETWEEN:
                        split(Step(6 + BETWEEN.index(k)))
                split(Step(10))
                dve.wait_ge(smalls_loaded, 16)
                link(nc.vector.tensor_scalar(qn8[:], sm[:, S_QN:S_QN + 1], DQK ** -0.5, None, ALU.mult))
                link(nc.vector.tensor_scalar(an8[:], sm[:, S_AN:S_AN + 1], 1.0 - LAM_INIT, None, ALU.mult))
                lq = sm[:, S_LQ:S_ALL].rearrange("p (a b d) -> p a b d", a=2, b=2)
                link(nc.vector.tensor_tensor(lam_p, lq[:, :, 0, :], lq[:, :, 1, :], ALU.mult))
                nc.vector.reduce_sum(lam4[:, 0:2], lam_p, axis=AX.X).then_inc(lam_sum, 1)
                dve.wait_ge(lam_exp, 1)
                link(nc.vector.scalar_tensor_tensor(out=neg_lam[:], in0=lam4[:, 3:4], scalar=-LAM_INIT, in1=lam4[:, 2:3],
                                                    op0=ALU.add, op1=ALU.subtract))
                link(nc.vector.tensor_copy(lam_sel[32:64, :], neg_lam[32:64, :]))

                def gates_evac():
                    dve.wait_ge(rstd_ready, 1)
                    nc.vector.tensor_tensor(two(gates[0][0:GR, :]), group(3)[0:GR], two(rstd[0:GR, :]), ALU.mult).then_inc(out_taken, 1)
                    dve.wait_ge(out_taken, 1)
                    nc.vector.tensor_scalar(gates[1][0:HEADS, :], gates[0][32:GR, :], sm[32:GR, S_BG:S_BG + 1], None,
                                            ALU.add).then_inc(gates_raw, 1)
                    link(nc.vector.tensor_scalar(gates[0][0:HEADS, :], gates[0][0:HEADS, :], sm[0:HEADS, S_BG:S_BG + 1], None, ALU.add))

                def gates_scan_stage():
                    z, b, g, M, m = (gates[i][0:HEADS, :] for i in (1, 3, 0, 4, 5))
                    dve.wait_ge(gates_lf, 1)
                    link(nc.vector.scalar_tensor_tensor(out=z, in0=z, scalar=0.0, in1=gates[2][0:HEADS, :],
                                                        op0=ALU.min, op1=ALU.subtract))
                    for c in range(NCH + 1):
                        lo, hi = c * P, min(T, (c + 1) * P)
                        last = nc.vector.tensor_tensor_scan(out=b[:, lo:hi], data0=z[:, lo:hi], data1=zero_row[:, lo:hi],
                                                            initial=0.0, op0=ALU.add, op1=ALU.add)
                    link(last)

                def gates_max_stage():
                    z, b, g, M, m = (gates[i][0:HEADS, :] for i in (1, 3, 0, 4, 5))
                    link(nc.vector.tensor_tensor(g, g, b, ALU.subtract))
                    for c in range(NCH + 1):
                        lo, hi = c * P, min(T, (c + 1) * P)
                        prev = 0.0 if c == 0 else (m[:, lo - 1:lo] if c < NCH else sm[0:HEADS, S_M0:S_M0 + 1])
                        link(nc.vector.tensor_tensor_scan(out=M[:, lo:hi], data0=g[:, lo:hi], data1=g[:, lo:hi],
                                                          initial=prev, op0=ALU.max, op1=ALU.max))
                        link(nc.vector.tensor_tensor(m[:, lo:hi], b[:, lo:hi], M[:, lo:hi], ALU.add))
                        nc.vector.tensor_scalar(nm_end[:, c:c + 1], M[:, hi - 1:hi], -1.0, None, ALU.mult)
                    nc.vector.tensor_copy(m_end[:, 0:1], m[:, SEQ - 1:SEQ])
                    nc.vector.tensor_copy(m_end[:, 1:2], m[:, T - 1:T]).then_inc(gates_scan, 1)

                OUTS = {K_: k_raw, Q_: q_raw, V_: v_T, MV: mv_T, MO: mo_T}

                def evac(h, n_):
                    u = h * PER_HEAD + (U_HEAD + n_)
                    src = group(u.mod(2))
                    if n_ in (MK, MQ) and not (h.reg is None and h.first == 0):
                        dve.wait_ge(conv_ready, (h * 2).v)
                    if n_ == K_ and not (h.reg is None and h.first == 0):
                        dve.wait_ge(qk_lo, h.v)
                    dve.wait_ge(quarter_done, (u * 4 + 4).v)
                    if n_ == V_ and not (h.reg is None and h.first == 0):
                        dve.wait_ge(kv_stored, (h * 32).v)
                    if n_ in OUTS:
                        nc.vector.tensor_tensor(two(OUTS[n_][:]), src, two(rstd[:]), ALU.mult).then_inc(out_taken, 1)
                        return
                    dst, tile = (mk_u, HEADS) if n_ == MK else (mq_u, 0)
                    c = bass.ds((h + tile).v, 1)
                    nc.vector.tensor_copy(dst[:, CS:CS + PAD], sm[:, S_SC:S_LQ].rearrange("p (c j) -> p c j", j=PAD)[:, c, :]
                                          .rearrange("p a j -> p (a j)"))
                    nc.vector.tensor_tensor(dst[:, PAD:PAD + HB], src[:, 0, :], rstd[:, 0:HB], ALU.mult)
                    nc.vector.tensor_tensor(dst[:, PAD + HB:CS], src[:, 1, 0:SEQ - HB], rstd[:, HB:SEQ], ALU.mult)
                    nc.vector.tensor_tensor(dst[:, CS + PAD:UW], src[:, 1, SEQ - HB:HB], rstd[:, SEQ:T], ALU.mult).then_inc(out_taken, 1)

                def post(p):
                    k_links = [0]

                    def own(ins):
                        k_links[0] += 1
                        ins.then_inc(post_dve, 1)
                        dve.wait_ge(post_dve, (p * DVE_LINKS + k_links[0]).v)

                    def conv(u, out, tile):
                        wcol = sm[:, S_CW:S_CB].rearrange("p (c j) -> p c j", j=CONV_W)
                        for j in range(CONV_W):
                            w = wcol[:, bass.ds((p + tile).v, 1), j:j + 1].rearrange("p a j -> p (a j)")
                            if j == 0:
                                own(nc.vector.tensor_scalar(out[:], u[:, 0:CW], w, sm[:, bass.ds((p + (tile + S_CB)).v, 1)],
                                                            ALU.mult, ALU.add))
                            else:
                                i = nc.vector.scalar_tensor_tensor(out=out[:], in0=u[:, j:j + CW], scalar=w, in1=out[:],
                                                                   op0=ALU.mult, op1=ALU.add)
                                if j < CONV_W - 1:
                                    own(i)
                                else:
                                    i.then_inc(conv_ready, 1)
                        c = bass.ds((p + tile).v, 1)
                        nc.vector.tensor_copy(conv_sb[:, c, 0, :].rearrange("p a j -> p (a j)"), u[:, SEQ:CS])
                        nc.vector.tensor_copy(conv_sb[:, c, 1, :].rearrange("p a j -> p (a j)"), u[:, UW - PAD:UW])

                    def s0():
                        dve.wait_ge(out_taken, (p * PER_HEAD + (U_HEAD + PER_HEAD)).v)
                        conv(mk_u, mk_T, HEADS)
                        conv(mq_u, mq_T, 0)
                        dve.wait_ge(sq_ready, (p + 1).v)
                        square_lo(0, k_sq_hi)
                        square_lo(1, q_sq_hi).then_inc(qk_sq_lo, 1)

                    def square_lo(i, high):
                        return nc.vector.tensor_tensor(sq_lo[:, i, :], tmp[i][:], high.bitcast(f32), ALU.subtract)

                    def silu_one(e, n_):
                        dve.wait_ge(conv_exp, (p * 2 + n_).v)
                        nc.vector.tensor_scalar(e[:], e[:], 1.0, LN_MAX, ALU.add, ALU.min).then_inc(silu_den, 1)

                    def silu(e, out, scale, n_):
                        dve.wait_ge(silu_sig, (p * 2 + n_).v)
                        nc.vector.scalar_tensor_tensor(out=out[:, 0:SEQ], in0=out[:, 0:SEQ], scalar=scale, in1=e[:, 0:SEQ],
                                                       op0=ALU.mult, op1=ALU.mult)
                        return nc.vector.scalar_tensor_tensor(out=out[:, CS:CW], in0=out[:, CS:CW], scalar=scale,
                                                              in1=e[:, SEQ:T], op0=ALU.mult, op1=ALU.mult)

                    def s0b():
                        silu_one(tmp[2], 1)
                        silu_one(tmp[3], 2)
                        silu(tmp[2], mk_T, DK ** -0.5, 1)
                        silu(tmp[3], mq_T, 1.0, 2).then_inc(silu_ready, 1)

                    def s1():
                        dve.wait_ge(qk_rstd, (p + 1).v)
                        nc.vector.scalar_tensor_tensor(out=k_T[:], in0=k_raw[:], scalar=sm[:, S_KN:S_KN + 1], in1=tmp[0][:],
                                                       op0=ALU.mult, op1=ALU.mult)
                        nc.vector.scalar_tensor_tensor(out=kc_sb[:, PAST:], in0=k_raw[:, SEQ:T], scalar=sm[:, S_KN:S_KN + 1],
                                                       in1=tmp[0][:, SEQ:T], op0=ALU.mult, op1=ALU.mult)
                        nc.vector.scalar_tensor_tensor(out=q_raw[:], in0=q_raw[:], scalar=qn8[:], in1=tmp[1][:],
                                                       op0=ALU.mult, op1=ALU.mult).then_inc(qk_ready, 1)
                        dve.wait_ge(qk_ready, (p + 1).v)
                        nc.vector.tensor_copy(q_s[0:64, 0:DEC], q_raw[0:64, SEQ:T])
                        own(nc.vector.tensor_copy(q_s[64:128, DEC:2 * DEC], q_raw[64:128, SEQ:T]))
                        decay_exponents()
                        dve.wait_ge(qk_hi, (p + 1).v)
                        for m in range(2):
                            h, other = slice(64 * m, 64 * m + 64), slice(64 - 64 * m, 128 - 64 * m)
                            nc.vector.tensor_copy(q_hi[other, m, :], q_hi[h, m, :].bitcast(f32))
                            nc.vector.tensor_tensor(q_lo[h, :], q_raw[h, 0:SEQ], q_hi[h, m, :].bitcast(f32), ALU.subtract)
                            last = nc.vector.tensor_tensor(k_split[other, m, :], k_T[h, 0:SEQ], k_split[h, m, :].bitcast(f32),
                                                           ALU.subtract)
                        last.then_inc(qk_lo, 1)

                    def decay_exponents():
                        dve.wait_ge(rows_loaded, ((p + 1) * 48).v)
                        for c in range(NCH):
                            nc.vector.tensor_tensor(decay[:, c * P:(c + 1) * P], decay[:, c * P:(c + 1) * P], causal[:], ALU.add)
                        nc.vector.tensor_tensor(decay[:, SEQ:T], decay[:, SEQ:T], causal[:, 0:DEC], ALU.add).then_inc(decay_sum, 1)

                    def maxima(m):
                        dve.wait_ge(scores_done, (p * 2 + (m + 1)).v)
                        for i in range(NCH):
                            last = nc.vector.tensor_reduce(neg_max[:, m, i:i + 1], pp[:, i, 0:(i + 1) * P], axis=AX.X,
                                                           op=ALU.max, negate=True)
                        last.then_inc(max_ready, 1)

                    def s3():
                        maxima(0)

                    def s4():
                        maxima(1)
                        dve.wait_ge(probs_ready, (p * 2 + 1).v)
                        own(nc.vector.reciprocal(inv[:, 0, :], sums[:, 0, :]))
                        for i in range(NCH):
                            s = slice(OFF[i], OFF[i] + (i + 1) * P)
                            last = nc.vector.tensor_scalar(prob[0][:, s], prob[0][:, s], inv[:, 0, i:i + 1], None, ALU.mult)
                        own(last)
                        dve.wait_ge(probs_ready, (p * 2 + 2).v)
                        own(nc.vector.reciprocal(inv[:, 1, :], sums[:, 1, :]))
                        own(nc.vector.tensor_scalar(inv[:, 1, :], inv[:, 1, :], neg_lam[:], None, ALU.mult))
                        for i in range(NCH):
                            s = slice(OFF[i], OFF[i] + (i + 1) * P)
                            last = nc.vector.scalar_tensor_tensor(out=prob[0][:, s], in0=prob[1][:, s], scalar=inv[:, 1, i:i + 1],
                                                                  in1=prob[0][:, s], op0=ALU.mult, op1=ALU.add)
                        last.then_inc(weights_ready, 1)

                    def s5():
                        dve.wait_ge(at_done, (p + 1).v)
                        dve.wait_ge(decay_ready, (p + 1).v)
                        nc.vector.tensor_copy(at[:, 1024:AW], pp[:, 2, 0:256])
                        nc.vector.tensor_tensor(decay[:, 0:SEQ], pp[:, 3, :], decay[:, 0:SEQ], ALU.mult)
                        nc.vector.tensor_tensor(decay[0:DEC, SEQ:T], pp[0:DEC, 2, SAMPLE_KQ - DEC:SAMPLE_KQ], decay[0:DEC, SEQ:T],
                                                ALU.mult).then_inc(pt_ready, 1)

                    def s6():
                        dve.wait_ge(pv_done, (p + 1).v)
                        dve.wait_ge(c0_loaded, ((p + 1) * 16).v)
                        if not (p.reg is None and p.first == 0):
                            dve.wait_ge(st_stored, (p * 16).v)
                        own(nc.vector.tensor_copy(state[:, 0, :], pp[:, 1, 0:DK + 1]))
                        for c in range(1, NCH):
                            src = pp[:, 1, c * (DK + 1):(c + 1) * (DK + 1)] if c < 3 else pp[:, 2, 0:DK + 1]
                            own(nc.vector.scalar_tensor_tensor(out=state[:, c, :], in0=state[:, c - 1, :],
                                                               scalar=wi_row[:, (c + 1) * P - 1:(c + 1) * P], in1=src,
                                                               op0=ALU.mult, op1=ALU.add))
                        nc.vector.scalar_tensor_tensor(out=state[:, NCH, :], in0=c0_sb[:], scalar=wi_row[:, T - 1:T],
                                                       in1=pp[:, 2, DK + 1:2 * (DK + 1)], op0=ALU.mult, op1=ALU.add)
                        nc.vector.tensor_tensor(mq_T[:, P:SEQ], mq_T[:, P:SEQ], wi_row[:, P:SEQ], ALU.mult)
                        nc.vector.tensor_tensor(mq_T[:, CS:CW], mq_T[:, CS:CW], wi_row[:, SEQ:T], ALU.mult).then_inc(state_ready, 1)
                        dve.wait_ge(state_ready, (p + 1).v)
                        own(nc.vector.tensor_scalar(den[:, SEQ:T], mq_T[:, CS:CW], c0_sb[:, DK:DK + 1], None, ALU.mult))
                        nc.vector.tensor_tensor(den[0:DEC, SEQ:T], den[0:DEC, SEQ:T], decay[0:DEC, SEQ:T], ALU.add)
                        nc.vector.tensor_copy(den[:, 0:P], decay[:, 0:P])
                        for c in range(1, NCH):
                            s = slice(c * P, (c + 1) * P)
                            last = nc.vector.scalar_tensor_tensor(out=den[:, s], in0=mq_T[:, s], scalar=state[:, c - 1, DK:DK + 1],
                                                                  in1=decay[:, s], op0=ALU.mult, op1=ALU.add)
                        last.then_inc(den_ready, 1)

                    def s7():
                        dve.wait_ge(den_hi_ready, (p + 1).v)
                        nc.vector.tensor_tensor(den_lo, den, den_hi.bitcast(f32), ALU.subtract).then_inc(den_lo_ready, 1)
                        dve.wait_ge(s_scores_done, (p + 1).v)
                        nc.vector.tensor_reduce(s_max[:], pp[0:64, 0:3, 0:SB], axis=AX.XY, op=ALU.max,
                                                negate=True).then_inc(s_max_ready, 1)
                        dve.wait_ge(s_exp_ready, (p + 1).v)
                        own(nc.vector.reciprocal(s_inv[:], s_sum[:]))
                        own(nc.vector.tensor_tensor(s_inv[:], s_inv[:], lam_sel[:], ALU.mult))
                        nc.vector.tensor_scalar(s_prob, s_prob, s_inv[:], None, ALU.mult).then_inc(s_probs_ready, 1)

                    def s8():
                        dve.wait_ge(den_abs, (p + 1).v)
                        own(nc.vector.tensor_tensor(tmp[2][:], tmp[2][:], en_row[:], ALU.max))
                        own(nc.vector.reciprocal(tmp[2][:], tmp[2][:]))
                        nc.vector.tensor_tensor(tmp[3][:, 0:SEQ], pp[:, 0, :], tmp[2][:, 0:SEQ], ALU.mult)
                        nc.vector.tensor_tensor(tmp[3][:, SEQ:T], pp[:, 1, P - DEC:P], tmp[2][:, SEQ:T], ALU.mult).then_inc(h_ready, 1)
                        dve.wait_ge(o_exp, (p + 1).v)
                        nc.vector.tensor_scalar(mo_T[:], mo_T[:], 1.0, LN_MAX, ALU.add, ALU.min).then_inc(o_den, 1)
                        dve.wait_ge(h_sq, (p + 1).v)
                        square_lo(0, sq_hi).then_inc(h_sq_lo, 1)

                    def s10():
                        dve.wait_ge(o_sig, (p + 1).v)
                        dve.wait_ge(ml_rstd, (p + 1).v)
                        own(nc.vector.scalar_tensor_tensor(out=tmp[3][:], in0=tmp[3][:], scalar=sm[:, S_MN:S_MN + 1],
                                                           in1=tmp[0][:], op0=ALU.mult, op1=ALU.mult))
                        nc.vector.tensor_tensor(res[:, bass.ds((p + HEADS).v, 1), :].rearrange("p a b -> p (a b)"),
                                                tmp[3][:], mo_T[:], ALU.mult).then_inc(mix_ready, 1)

                    def s11():
                        dve.wait_ge(att_sq, (p + 1).v)
                        square_lo(1, sq_hi).then_inc(att_sq_lo, 1)

                    def s12():
                        dve.wait_ge(att_rstd, (p + 1).v)
                        nc.vector.scalar_tensor_tensor(out=res[:, bass.ds(p.v, 1), :].rearrange("p a b -> p (a b)"),
                                                       in0=att_T, scalar=an8[:], in1=tmp[1][:],
                                                       op0=ALU.mult, op1=ALU.mult).then_inc(mix_ready, 1)
                        assert k_links[0] == DVE_LINKS, k_links

                    return [s0, s0b, s1, None, s3, s4, s5, s6, s7, s8, None, s10, s11, s12]

                def unit(u, pieces=(None, None), begun=False):
                    q = u * 4
                    if not begun:
                        split(q + 3)
                        if pieces[0]:
                            pieces[0]()
                        split(q + 4)
                    split(q + 5)
                    if pieces[1]:
                        pieces[1]()
                    split(q + 6)

                def first_evacs():
                    gates_evac()
                    evac(Step(0), 0)

                def prologue(h):
                    for n_ in range(PER_HEAD):
                        if n_:
                            unit(Step(U_HEAD + n_), {1: (None, first_evacs), 2: (None, gates_scan_stage),
                                                     3: (gates_max_stage, None)}.get(n_, (None, None)))
                            evac(h, n_)

                def both(h, p):
                    stages = post(p)
                    for n_ in range(PER_HEAD):
                        unit(h * PER_HEAD + (U_HEAD + n_), pieces=stages[2 * n_:2 * n_ + 2])
                        evac(h, n_)

                def split_mix(n_):
                    t = SPLIT[n_]
                    dve.wait_ge(mix_hi, n_ + 1)
                    nc.vector.tensor_tensor(act_lo[:, t, :], res[:, t, :], act_hi[:, t, :].bitcast(f32),
                                            ALU.subtract).then_inc(mix_lo, 1)

                def mlp_in(j):
                    t = MLP_TILES[j]
                    dve.wait_ge(x_hi, KT + j + 1)
                    nc.vector.scalar_tensor_tensor(out=act_lo[:, t, :], in0=res[:, t, :], scalar=sm[:, S_N2 + t:S_N2 + t + 1],
                                                   in1=act_hi[:, t, :].bitcast(f32), op0=ALU.mult, op1=ALU.subtract
                                                   ).then_inc(x_lo, 1)

                head_steps(dve, prologue, both)

                stages = post(Step(HEADS - 1))
                for n_ in range(EARLY):
                    split_mix(n_)
                    if n_ == 3:
                        split(Step(4 * U_OUT + 3))
                for r in range(4 * KT):
                    if 0 < r <= OUT_MAIN:
                        split(Step(4 * U_OUT + r + 3))
                    i, odd = divmod(r - OUT_SHIFT, 2)
                    if not odd and 0 <= i < len(stages) and stages[i]:
                        stages[i]()
                    if r == OUT_SHIFT + 2 * len(stages) - 1:
                        for n_ in range(EARLY, KT):
                            split_mix(n_)
                        nc.vector.memset(acc[:], 0.0).then_inc(acc_clear, 1)
                    for g in OUT_ENDS[r]:
                        t = SPLIT[g % KT]
                        dve.wait_ge(quarter_done, 4 * U_OUT + r + 1)
                        if g < KT:
                            dve.wait_ge(x_reloaded[t], 16)
                        else:
                            dve.wait_ge(out_taken, U_OUT + g - KT + 1)
                        nc.vector.tensor_tensor(two(res[:, t, :]), group(out_slot(g)), two(res[:, t, :]), ALU.add
                                                ).then_inc(out_taken, 1)
                    if r >= OUT_MAIN:
                        if r < 4 * KT - 1:
                            split(Step(4 * U_OUT + r + 4))
                        for g in OUT_ENDS[r]:
                            mlp_in(g - KT)
                for j in range(TWICE, KT):
                    mlp_in(j)
                    if j in LAST_BETWEEN:
                        split(Step(4 * U_UP0 + 3 + LAST_BETWEEN.index(j)))

                def hidden_out(u, t, k):
                    dve.wait_ge(quarter_done, (u * 4 + 4).v)
                    if not (t.reg is None and t.first < 2):
                        dve.wait_ge(up_hi, (t + (-1)).v)
                        dve.wait_ge(up_sq, (t + (-1)).v)
                    nc.vector.scalar_tensor_tensor(out=two(tmp[k % 2][:]), in0=group((k + UP_SLOT) % 2), scalar=0.0,
                                                   in1=two(rstd[:]), op0=ALU.max, op1=ALU.mult).then_inc(up_relu, 1)

                def hidden_lo(t, k, parity):
                    dve.wait_ge(up_hi, (t + 1).v)
                    dve.wait_ge(up_sq, (t + 1).v)
                    nc.vector.tensor_tensor(hid_lo[:, parity, k, :], tmp[2 + k % 2][:], hid_hi[:, parity, k, :].bitcast(f32),
                                            ALU.subtract).then_inc(up_lo, 1)

                def up_units(u, t, parity, first):
                    for k in range(BLOCK):
                        if first:
                            unit(u + k, begun=k == 0)
                        else:
                            split((u + k) * 4 + 3)
                            if k:
                                hidden_lo(t + (k - 1), k - 1, parity)
                            for q in (4, 5, 6):
                                split((u + k) * 4 + q)
                        if first and k == 0:
                            dve.wait_ge(rstd_ready, 2)
                        hidden_out(u + k, t + k, k)
                        if first:
                            hidden_lo(t + k, k, parity)

                def down_units(b, u, before=None):
                    for k in range(BLOCK):
                        for q in range(4):
                            m = 4 * k + q
                            split((u + k) * 4 + (q + 3))
                            if m == 0 and before:
                                before()
                            dve.wait_ge(quarter_done, ((u + k) * 4 + (q + 1)).v)
                            r = two(res[:, m, :])
                            nc.vector.tensor_tensor(r, group(2 + m % 2), r, ALU.add).then_inc(down_taken, 1)

                up_units(Step(U_UP0), Step(0), 0, True)

                def step(b):
                    u = b * (2 * BLOCK) + U_FFN
                    t = (b + 1) * BLOCK
                    up_units(u, t, 1 - b.mod(2), False)
                    down_units(b, u + BLOCK, lambda: hidden_lo(t + (BLOCK - 1), BLOCK - 1, 1 - b.mod(2)))

                ffn_steps(dve, step)
                down_units(Step(NBLK - 1), Step(U_LAST))


def kernel(x_prompt, x_sample, cache_k, cache_v, state_C, state_n, state_m, state_conv,
           norm1_w, w_in, conv_w, conv_b, b_gates, q_norm_w, k_norm_w, lambda_qk,
           att_norm_w, ml_norm_w, w_out, norm2_w, w_up, w_down):
    import numpy as np
    import concourse.bacc as bacc
    from concourse.bass_utils import run_bass_kernel_spmd

    def host(a):
        return np.asarray(a)

    x = np.concatenate([host(x_prompt)[0], host(x_sample)[0]], axis=0)
    xT = x.T.reshape(KT, P, T).transpose(1, 0, 2)

    def quarters(w):
        k, n = w.shape
        return w.reshape(k // QW, 4, P, n // P, P).transpose(3, 0, 2, 1, 4).reshape(n // P, k // QW, P, QW)

    w = host(w_in)[0]
    gate_w = np.zeros((D_MODEL, P), w.dtype)
    gate_w[:, 0:HEADS] = w[:, ROUNDS * P:ROUNDS * P + HEADS]
    gate_w[:, 32:GR] = w[:, ROUNDS * P + HEADS:]
    w_heads = quarters(w[:, 0:ROUNDS * P])
    order = [base * HEADS + h for h in range(HEADS) for base in (4, 3, 1, 0, 2, 5, 6)]
    w_u = host(w_up)[0].reshape(KT, P, D_FF)[MLP_TILES].reshape(D_MODEL, D_FF)
    up = quarters(w_u).reshape(NBLK, 4 * BLOCK, P, QW)
    down = quarters(host(w_down)[0]).transpose(1, 0, 2, 3)
    w_o = host(w_out)[0].reshape(KT, P, KT, P)[SPLIT][:, :, SPLIT]
    w_o = np.stack([w_o[kk, :, g % KT] for g, kk, _, _ in OUT_ORDER])
    w_o = w_o.reshape(-1, 4, P, P).transpose(0, 2, 1, 3).reshape(-1, P, QW)
    parts = [quarters(gate_w).reshape(-1, P, QW), w_heads[order].reshape(-1, P, QW),
             w_o, up[0]]
    for b in range(NBLK - 1):
        parts += [up[b + 1], down[b]]
    parts.append(down[NBLK - 1])
    wstream = np.concatenate(parts, axis=0)

    smalls = np.zeros((P, S_ALL), x.dtype)
    smalls[:, S_N1:S_N2] = host(norm1_w)[0].reshape(KT, P).T
    smalls[:, S_N2:S_CW] = host(norm2_w)[0].reshape(KT, P).T
    smalls[:, S_CW:S_CB] = host(conv_w)[0].reshape(CONV_W, 2 * HEADS, P).transpose(2, 1, 0).reshape(P, -1)
    smalls[:, S_CB:S_QN] = host(conv_b)[0].reshape(2 * HEADS, P).T
    smalls[:, S_QN] = np.concatenate([host(q_norm_w)[0]] * 2)
    smalls[:, S_KN] = np.concatenate([host(k_norm_w)[0]] * 2)
    smalls[:, S_AN] = host(att_norm_w)[0]
    smalls[:, S_MN] = host(ml_norm_w)[0]
    smalls[0:HEADS, S_BG] = host(b_gates)[0, 0:HEADS]
    smalls[32:GR, S_BG] = host(b_gates)[0, HEADS:]
    smalls[0:HEADS, S_M0] = host(state_m)[0, 0]
    smalls[:, S_SC:S_LQ] = host(state_conv)[0, 0].reshape(PAD, 2 * HEADS, P).transpose(2, 1, 0).reshape(P, -1)
    smalls[:, S_LQ:S_ALL] = host(lambda_qk)[0].reshape(1, -1)

    kcT = host(cache_k)[0, 0].transpose(1, 2, 0)
    vcl = host(cache_v)[0, 0].reshape(PAST // P, P, HEADS, DK).transpose(2, 1, 0, 3)
    c0 = np.concatenate([host(state_C)[0, 0], host(state_n)[0, 0][:, :, None]], axis=2)

    nc = bacc.Bacc("TRN2", target_bir_lowering=False, num_devices=1)
    f32 = mybir.dt.float32
    arrays = {}

    def given(name, a):
        arrays[name] = np.ascontiguousarray(a)
        return nc.dram_tensor(name, a.shape, f32, kind="ExternalInput").ap()

    def wanted(name, shape):
        return nc.dram_tensor(name, shape, f32, kind="ExternalOutput").ap()

    build(nc, given("in_xT", xT), given("in_wstream", wstream), given("in_smalls", smalls), given("in_kcT", kcT),
          given("in_vc", vcl), given("in_c0", c0),
          wanted("out_yT", (P, KT, T)), wanted("out_k", (HEADS, P, T)), wanted("out_v", (HEADS, P, T)),
          wanted("out_st", (HEADS, 2, P, DK + 1)), wanted("out_m", (HEADS, 2)),
          wanted("out_conv", (P, 2 * HEADS, 2, PAD)))
    r = run_bass_kernel_spmd(nc, [arrays], core_ids=[0]).results[0]

    y = r["out_yT"].transpose(2, 1, 0).reshape(T, D_MODEL)
    k = r["out_k"].transpose(2, 0, 1)
    v = r["out_v"].transpose(2, 0, 1)
    st, m = r["out_st"], r["out_m"]
    conv = r["out_conv"].transpose(2, 3, 1, 0).reshape(2, PAD, 2 * HEADS * P)

    def side(s):
        t = slice(0, SEQ) if s == 0 else slice(SEQ, T)
        return (k[None, None, t], v[None, None, t], st[None, None, :, s, :, 0:DK], st[None, None, :, s, :, DK],
                m[None, None, :, s], conv[None, None, s])

    return tuple(np.ascontiguousarray(a) for a in (y[None, 0:SEQ], y[None, SEQ:], *side(0), *side(1)))
```
